# Optimizing a Trainium2 kernel written in Bass

```python
import jax, jax.numpy as jnp
from jax import lax
import numpy as np

D_MODEL = 1024
BATCH = 1
SEQ = 512
DEPTH = 1

EPS = 1e-6
D_MIX = D_MODEL
HG_HEADS = 4
HG_DK = 128
HG_DV = 128
HG_WIDTH = HG_HEADS * HG_DV
HG_CHUNK = 64
NSA_HEADS = 8
NSA_KV_GROUPS = 2
NSA_HD = 64
NSA_WIDTH = NSA_HEADS * NSA_HD
NSA_KV = NSA_KV_GROUPS * NSA_HD
CMP_BLOCK = 32
CMP_STRIDE = 16
CMP_HIDDEN = 256
SEL_BLOCK = 64
N_SEL = 16
WINDOW = 512
Q_BLOCK = 128
ROPE_THETA = 10000.0
N_EXPERTS = 64
TOP_K = 8
N_GROUPS = 8
TOPK_GROUPS = 4
EXPERT_HIDDEN = 256
SHARED_HIDDEN = 256
ROUTED_SCALE = 2.5
EXPERT_BLOCK = 128
IN_SPLITS = (HG_WIDTH,) * 4 + (NSA_WIDTH,) + (NSA_KV,) * 6 + (3 * NSA_HEADS,)
IN_COLS = 4 * HG_WIDTH + NSA_WIDTH + 6 * NSA_KV + 3 * NSA_HEADS


def rmsnorm(x, g):
    xf = x.astype(jnp.float32)
    y = xf * lax.rsqrt(jnp.mean(xf * xf, axis=-1, keepdims=True) + EPS)
    return (y * g.astype(jnp.float32)).astype(x.dtype)

def rope(t, pos):
    half = t.shape[-1] // 2
    inv = ROPE_THETA ** (-jnp.arange(half, dtype=jnp.float32) / half)
    ang = pos.astype(jnp.float32)[:, None] * inv[None, :]
    cos, sin = jnp.cos(ang), jnp.sin(ang)
    t1 = t[..., :half].astype(jnp.float32)
    t2 = t[..., half:].astype(jnp.float32)
    return jnp.concatenate([t1 * cos - t2 * sin, t2 * cos + t1 * sin], axis=-1).astype(t.dtype)

def swiglu(t, w_gu, w_dn):
    g, u = jnp.split(t @ w_gu, 2, axis=-1)
    return (jax.nn.silu(g) * u) @ w_dn

def hgrn2_mixer(q, f_logit, i, gate, lb, norm_g):
    B, S, _ = q.shape
    f32 = jnp.float32
    f = lb + (1.0 - lb) * jax.nn.sigmoid(f_logit.astype(f32))
    log_f = jnp.log(f)
    k = 1.0 - f
    n_ch = S // HG_CHUNK

    def to_chunks(t, d):
        return t.reshape(B, n_ch, HG_CHUNK, HG_HEADS, d).transpose(1, 0, 3, 2, 4)

    qc = to_chunks(q.astype(f32) * HG_DK ** -0.5, HG_DK)
    kc = to_chunks(k, HG_DK)
    vc = to_chunks(i.astype(f32), HG_DV)
    bc = jnp.cumsum(to_chunks(log_f, HG_DK), axis=3)
    causal = jnp.tril(jnp.ones((HG_CHUNK, HG_CHUNK), bool))

    def step(state, inp):
        q_, k_, v_, b_ = inp
        diff = jnp.where(causal[:, :, None], b_[:, :, :, None, :] - b_[:, :, None, :, :], -jnp.inf)
        a = jnp.einsum('bhtd,bhtsd,bhsd->bhts', q_, jnp.exp(diff), k_)
        o = a @ v_ + jnp.einsum('bhtd,bhde->bhte', q_ * jnp.exp(b_), state)
        b_last = b_[:, :, -1]
        state = jnp.exp(b_last)[..., None] * state + jnp.einsum(
            'bhsd,bhse->bhde', k_ * jnp.exp(b_last[:, :, None, :] - b_), v_)
        return state, o

    s0 = jnp.zeros((B, HG_HEADS, HG_DK, HG_DV), f32)
    _, o = lax.scan(step, s0, (qc, kc, vc, bc))
    o = o.transpose(1, 0, 3, 2, 4).reshape(B, S, HG_HEADS, HG_DV)
    o = o * lax.rsqrt(jnp.mean(o * o, axis=-1, keepdims=True) + EPS) * norm_g.astype(f32).reshape(HG_HEADS, HG_DV)
    o = o.reshape(B, S, HG_WIDTH) * jax.nn.silu(gate.astype(f32))
    return o.astype(q.dtype)

def nsa_mixer(q, kc, vc, ks, vs, kw, vw, gate_logit,
              pos_k, w1_k, b1_k, w2_k, pos_v, w1_v, b1_v, w2_v):
    B, S, _ = q.shape
    G, HG, HD = NSA_KV_GROUPS, NSA_HEADS // NSA_KV_GROUPS, NSA_HD
    f32 = jnp.float32
    pos = jnp.arange(S)
    scale = HD ** -0.5
    qh = q.reshape(B, S, G, HG, HD).transpose(0, 2, 3, 1, 4)
    q_rot = rope(qh, pos)

    def kv_heads(t):
        return t.reshape(B, S, G, HD).transpose(0, 2, 1, 3)

    n_cmp = (S - CMP_BLOCK) // CMP_STRIDE + 1
    tok_idx = jnp.arange(n_cmp)[:, None] * CMP_STRIDE + jnp.arange(CMP_BLOCK)[None, :]

    def compress(t, pe, w1, b1, w2):
        blocks = kv_heads(t)[:, :, tok_idx] + pe
        hdn = jax.nn.gelu(blocks.reshape(B, G, n_cmp, CMP_BLOCK * HD) @ w1 + b1)
        return hdn @ w2

    k_cmp = compress(kc, pos_k, w1_k, b1_k, w2_k)
    v_cmp = compress(vc, pos_v, w1_v, b1_v, w2_v)
    s_cmp = jnp.einsum('bghsd,bgcd->bghsc', qh, k_cmp).astype(f32) * scale
    c_start = jnp.arange(n_cmp) * CMP_STRIDE
    cmp_mask = (c_start + CMP_BLOCK - 1)[None, :] <= pos[:, None]
    p_cmp = jax.nn.softmax(jnp.where(cmp_mask, s_cmp, -1e30), axis=-1) * cmp_mask
    o_cmp = jnp.einsum('bghsc,bgcd->bghsd', p_cmp, v_cmp.astype(f32))

    n_sb = S // SEL_BLOCK
    n_sel = min(N_SEL, n_sb)
    s_start = jnp.arange(n_sb) * SEL_BLOCK
    overlap = jnp.clip(jnp.minimum(c_start[:, None] + CMP_BLOCK, s_start[None, :] + SEL_BLOCK)
                       - jnp.maximum(c_start[:, None], s_start[None, :]), 0, None).astype(f32) / CMP_BLOCK
    p_slc = jnp.einsum('bghsc,cj->bgsj', p_cmp, overlap)
    cur = pos // SEL_BLOCK
    blk = jnp.arange(n_sb)
    available = blk[None, :] <= cur[:, None]
    forced = (blk[None, :] == 0) | (blk[None, :] == cur[:, None]) | (blk[None, :] == cur[:, None] - 1)
    sel_score = jnp.where(forced, 1e30, jnp.where(available, p_slc, -1e30))
    top_val, top_idx = lax.top_k(sel_score, n_sel)
    top_valid = top_val > -1e29

    n_qb = S // Q_BLOCK
    k_blocks = rope(kv_heads(ks), pos).reshape(B, G, n_sb, SEL_BLOCK * HD)
    v_blocks = kv_heads(vs).reshape(B, G, n_sb, SEL_BLOCK * HD)
    bi = jnp.arange(B)[:, None, None]
    gi = jnp.arange(G)[None, :, None]

    def by_qblock(t, axis):
        shape = t.shape[:axis] + (n_qb, Q_BLOCK) + t.shape[axis + 1:]
        return jnp.moveaxis(t.reshape(shape), axis, 0)

    def slc_block(args):
        qb, idx, valid, qpos = args
        flat = idx.reshape(B, G, Q_BLOCK * n_sel)
        kg = k_blocks[bi, gi, flat].reshape(B, G, Q_BLOCK, n_sel, SEL_BLOCK, HD)
        vg = v_blocks[bi, gi, flat].reshape(B, G, Q_BLOCK, n_sel, SEL_BLOCK, HD)
        s = jnp.einsum('bghqd,bgqnld->bghqnl', qb, kg).astype(f32) * scale
        kpos = idx[..., None] * SEL_BLOCK + jnp.arange(SEL_BLOCK)
        ok = valid[..., None] & (kpos <= qpos[:, None, None])
        s = jnp.where(ok[:, :, None], s, -1e30).reshape(B, G, HG, Q_BLOCK, n_sel * SEL_BLOCK)
        p = jax.nn.softmax(s, axis=-1).reshape(B, G, HG, Q_BLOCK, n_sel, SEL_BLOCK)
        return jnp.einsum('bghqnl,bgqnld->bghqd', p, vg.astype(f32))

    o_slc = lax.map(slc_block, (by_qblock(q_rot, 3), by_qblock(top_idx, 2),
                                by_qblock(top_valid, 2), pos.reshape(n_qb, Q_BLOCK)))
    o_slc = jnp.moveaxis(o_slc, 0, 3).reshape(B, G, HG, S, HD)

    n_back = WINDOW // Q_BLOCK

    def banded(t):
        tp = jnp.pad(t, ((0, 0), (0, 0), (WINDOW, 0), (0, 0))).reshape(B, G, n_qb + n_back, Q_BLOCK, HD)
        return jnp.concatenate([tp[:, :, o:o + n_qb] for o in range(n_back + 1)], axis=3)

    kwb = banded(rope(kv_heads(kw), pos))
    vwb = banded(kv_heads(vw))
    qw = q_rot.reshape(B, G, HG, n_qb, Q_BLOCK, HD)
    s_w = jnp.einsum('bghnqd,bgnkd->bghnqk', qw, kwb).astype(f32) * scale
    qpos = pos.reshape(n_qb, Q_BLOCK)
    kpos = (jnp.arange(n_qb)[:, None] - n_back) * Q_BLOCK + jnp.arange((n_back + 1) * Q_BLOCK)[None, :]
    d = qpos[:, :, None] - kpos[:, None, :]
    ok_w = (d >= 0) & (d < WINDOW) & (kpos[:, None, :] >= 0)
    p_w = jax.nn.softmax(jnp.where(ok_w, s_w, -1e30), axis=-1)
    o_win = jnp.einsum('bghnqk,bgnkd->bghnqd', p_w, vwb.astype(f32)).reshape(B, G, HG, S, HD)

    gates = jax.nn.sigmoid(gate_logit.astype(f32)).reshape(B, S, G, HG, 3).transpose(0, 2, 3, 1, 4)
    o = gates[..., 0:1] * o_cmp + gates[..., 1:2] * o_slc + gates[..., 2:3] * o_win
    return o.transpose(0, 3, 1, 2, 4).reshape(B, S, NSA_WIDTH).astype(q.dtype)

def routed_experts(t, top_i, top_w, w_gu, w_dn):
    T, D = t.shape
    A = T * TOP_K
    e_flat = top_i.reshape(A).astype(jnp.int32)
    w_flat = top_w.reshape(A).astype(jnp.float32)
    order = jnp.argsort(e_flat)
    e_sorted = e_flat[order]
    tok_sorted = (order // TOP_K).astype(jnp.int32)
    counts = jnp.bincount(e_flat, length=N_EXPERTS)
    start = jnp.cumsum(counts) - counts
    padded = (counts + EXPERT_BLOCK - 1) // EXPERT_BLOCK * EXPERT_BLOCK
    pad_end = jnp.cumsum(padded)
    pad_start = pad_end - padded
    dest = pad_start[e_sorted] + jnp.arange(A) - start[e_sorted]
    n_blk = -(-A // EXPERT_BLOCK) + N_EXPERTS
    P = n_blk * EXPERT_BLOCK
    rows = jnp.full((P,), T, jnp.int32).at[dest].set(tok_sorted)
    wts = jnp.zeros((P,), jnp.float32).at[dest].set(w_flat[order])
    blk_expert = jnp.minimum(jnp.searchsorted(pad_end, jnp.arange(n_blk) * EXPERT_BLOCK, side='right'),
                             N_EXPERTS - 1)
    t_pad = jnp.concatenate([t, jnp.zeros((1, D), t.dtype)], axis=0)

    def one_block(args):
        rb, e = args
        return swiglu(t_pad[rb], w_gu[e], w_dn[e]).astype(jnp.float32)

    ys = lax.map(one_block, (rows.reshape(n_blk, EXPERT_BLOCK), blk_expert)).reshape(P, D)
    out = jnp.zeros((T + 1, D), jnp.float32).at[rows].add(ys * wts[:, None])
    return out[:T]

def moe_ffn(h, router_w, router_bias, w_gu, w_dn, w_sh_gu, w_sh_dn):
    B, S, D = h.shape
    t = h.reshape(B * S, D)
    scores = jax.nn.sigmoid((t @ router_w).astype(jnp.float32))
    choice = scores + router_bias.astype(jnp.float32)
    grp = choice.reshape(B * S, N_GROUPS, N_EXPERTS // N_GROUPS)
    grp_score = lax.top_k(grp, 2)[0].sum(-1)
    top_g = lax.top_k(grp_score, TOPK_GROUPS)[1]
    gmask = jnp.any(top_g[..., None] == jnp.arange(N_GROUPS), axis=-2)
    emask = jnp.repeat(gmask, N_EXPERTS // N_GROUPS, axis=-1)
    top_i = lax.top_k(jnp.where(emask, choice, -jnp.inf), TOP_K)[1]
    top_w = jnp.take_along_axis(scores, top_i, axis=-1)
    top_w = top_w / jnp.sum(top_w, axis=-1, keepdims=True) * ROUTED_SCALE
    routed = routed_experts(t, top_i, top_w, w_gu, w_dn)
    shared = swiglu(t, w_sh_gu, w_sh_dn).astype(jnp.float32)
    return (routed + shared).reshape(B, S, D).astype(h.dtype)

def first_inputs(seed: int = 0) -> dict:
    key = jax.random.key(seed)
    ks = jax.random.split(key, 26)
    L = DEPTH

    def nrm(k, shape, s):
        return jax.random.normal(k, shape, jnp.float32) * s

    return {
        "x": nrm(ks[0], (BATCH, SEQ, D_MODEL), 1.0),
        "c": nrm(ks[1], (BATCH, D_MODEL), 1.0),
        "w_ada": nrm(ks[2], (L, D_MODEL, 6 * D_MODEL), 0.5 * D_MODEL ** -0.5),
        "b_ada": nrm(ks[3], (L, 6 * D_MODEL), 0.02),
        "norm1_g": 1.0 + nrm(ks[4], (L, D_MODEL), 0.02),
        "w_in": nrm(ks[5], (L, D_MODEL, IN_COLS), D_MODEL ** -0.5),
        "hg_lb_logits": nrm(ks[6], (L + 1, HG_WIDTH), 0.5),
        "hg_norm_g": 1.0 + nrm(ks[7], (L, HG_WIDTH), 0.02),
        "cmp_pos_k": nrm(ks[8], (L, CMP_BLOCK, NSA_HD), 0.1),
        "cmp_w1_k": nrm(ks[9], (L, CMP_BLOCK * NSA_HD, CMP_HIDDEN), (CMP_BLOCK * NSA_HD) ** -0.5),
        "cmp_b1_k": nrm(ks[10], (L, CMP_HIDDEN), 0.02),
        "cmp_w2_k": nrm(ks[11], (L, CMP_HIDDEN, NSA_HD), CMP_HIDDEN ** -0.5),
        "cmp_pos_v": nrm(ks[12], (L, CMP_BLOCK, NSA_HD), 0.1),
        "cmp_w1_v": nrm(ks[13], (L, CMP_BLOCK * NSA_HD, CMP_HIDDEN), (CMP_BLOCK * NSA_HD) ** -0.5),
        "cmp_b1_v": nrm(ks[14], (L, CMP_HIDDEN), 0.02),
        "cmp_w2_v": nrm(ks[15], (L, CMP_HIDDEN, NSA_HD), CMP_HIDDEN ** -0.5),
        "w_out": nrm(ks[16], (L, D_MIX, D_MODEL), D_MIX ** -0.5),
        "norm2_g": 1.0 + nrm(ks[17], (L, D_MODEL), 0.02),
        "router_w": nrm(ks[18], (L, D_MODEL, N_EXPERTS), D_MODEL ** -0.5),
        "router_bias": nrm(ks[19], (L, N_EXPERTS), 0.01),
        "w_exp_gu": nrm(ks[20], (L, N_EXPERTS, D_MODEL, 2 * EXPERT_HIDDEN), D_MODEL ** -0.5),
        "w_exp_dn": nrm(ks[21], (L, N_EXPERTS, EXPERT_HIDDEN, D_MODEL), EXPERT_HIDDEN ** -0.5),
        "w_sh_gu": nrm(ks[22], (L, D_MODEL, 2 * SHARED_HIDDEN), D_MODEL ** -0.5),
        "w_sh_dn": nrm(ks[23], (L, SHARED_HIDDEN, D_MODEL), SHARED_HIDDEN ** -0.5),
        "final_g": 1.0 + nrm(ks[24], (D_MODEL,), 0.02),
    }

def first_block(x, c, w_ada, b_ada, norm1_g, w_in, hg_lb_logits, hg_norm_g,
              cmp_pos_k, cmp_w1_k, cmp_b1_k, cmp_w2_k, cmp_pos_v, cmp_w1_v, cmp_b1_v, cmp_w2_v,
              w_out, norm2_g, router_w, router_bias, w_exp_gu, w_exp_dn, w_sh_gu, w_sh_dn, final_g):
    offsets = np.cumsum(IN_SPLITS)[:-1].tolist()
    lb_all = jnp.cumsum(jax.nn.softmax(hg_lb_logits.astype(jnp.float32), axis=0), axis=0)
    c_act = jax.nn.silu(c)
    for l in range(DEPTH):
        mod = (c_act @ w_ada[l] + b_ada[l])[:, None, :]
        sh1, sc1, g1, sh2, sc2, g2 = jnp.split(mod, 6, axis=-1)
        h = rmsnorm(x, norm1_g[l]) * (1.0 + sc1) + sh1
        hq, hf, hi, hgt, nq, kc, vc, ksl, vsl, kwn, vwn, ngate = jnp.split(h @ w_in[l], offsets, axis=-1)
        o_hg = hgrn2_mixer(hq, hf, hi, hgt, lb_all[l], hg_norm_g[l])
        o_nsa = nsa_mixer(nq, kc, vc, ksl, vsl, kwn, vwn, ngate,
                          cmp_pos_k[l], cmp_w1_k[l], cmp_b1_k[l], cmp_w2_k[l],
                          cmp_pos_v[l], cmp_w1_v[l], cmp_b1_v[l], cmp_w2_v[l])
        x = x + g1 * (jnp.concatenate([o_hg, o_nsa], axis=-1) @ w_out[l])
        h = rmsnorm(x, norm2_g[l]) * (1.0 + sc2) + sh2
        x = x + g2 * moe_ffn(h, router_w[l], router_bias[l], w_exp_gu[l], w_exp_dn[l], w_sh_gu[l], w_sh_dn[l])
    return rmsnorm(x, final_g)


DEPTH_2 = 2

HEAD_DIM = 64
N_Q_HEADS = 8
N_KV_HEADS = 2
ATTN_WIDTH = N_Q_HEADS * HEAD_DIM
KV_WIDTH = N_KV_HEADS * HEAD_DIM
LRU_HEADS = 4
LRU_WIDTH = LRU_HEADS * HEAD_DIM
CONV_GROUPS = 4
CONV_WIDTH = CONV_GROUPS * HEAD_DIM
MIX_WIDTH = ATTN_WIDTH + LRU_WIDTH + CONV_WIDTH
IN_SPLITS_2 = (ATTN_WIDTH, KV_WIDTH, KV_WIDTH, LRU_WIDTH, LRU_WIDTH, CONV_WIDTH, CONV_WIDTH, CONV_WIDTH)
IN_PROJ_WIDTH = sum(IN_SPLITS_2)
WINDOW_2 = 128
BLOCK = 128
LRU_CONV_K = 4
SHORT_CONV_K = 3
LRU_C = 8.0
D_FF = ((8 * D_MODEL // 3 + 127) // 128) * 128
N_SUBLAYERS = 3
N_MOD = 3 * N_SUBLAYERS
NEG_INF = -1e30


def rmsnorm_2(x, g):
    xf = x.astype(jnp.float32)
    y = xf * lax.rsqrt(jnp.mean(xf * xf, axis=-1, keepdims=True) + EPS)
    return (y * g.astype(jnp.float32)).astype(x.dtype)

def modulate(x, g, shift, scale):
    return rmsnorm_2(x, g) * (1.0 + scale[:, None, :]) + shift[:, None, :]

def swiglu_2(h, w_gu, w_down):
    gu = h @ w_gu
    g, u = jnp.split(gu, 2, axis=-1)
    return (jax.nn.silu(g) * u) @ w_down

def causal_depthwise_conv(x, w, b=None):
    K = w.shape[0]
    S = x.shape[1]
    xp = jnp.pad(x, ((0, 0), (K - 1, 0), (0, 0)))
    y = xp[:, 0:S] * w[0]
    for k in range(1, K):
        y = y + xp[:, k:k + S] * w[k]
    if b is not None:
        y = y + b
    return y

def alibi_slopes(n_heads):
    return jnp.asarray(2.0 ** (-8.0 * np.arange(1, n_heads + 1) / n_heads), dtype=jnp.float32)

def sliding_window_attention(q, k, v, sinks):
    b, s = q.shape[:2]
    nb = s // BLOCK
    G = N_Q_HEADS // N_KV_HEADS
    qb = q.reshape(b, nb, BLOCK, N_KV_HEADS, G, HEAD_DIM)

    def band(t):
        tb = t.reshape(b, nb, BLOCK, N_KV_HEADS, HEAD_DIM)
        prev = jnp.pad(tb[:, :-1], ((0, 0), (1, 0), (0, 0), (0, 0), (0, 0)))
        return jnp.concatenate([prev, tb], axis=2)

    kb, vb = band(k), band(v)
    scores = jnp.einsum('bnqkgd,bnskd->bnkgqs', qb, kb).astype(jnp.float32) * (HEAD_DIM ** -0.5)
    qi = jnp.arange(BLOCK)[:, None]
    kj = jnp.arange(2 * BLOCK)[None, :]
    dist = qi + BLOCK - kj
    in_window = (dist >= 0) & (dist < WINDOW_2)
    blk = jnp.arange(nb)[:, None, None]
    valid = in_window[None] & ((blk > 0) | (kj[None] >= BLOCK))
    slopes = alibi_slopes(N_Q_HEADS).reshape(N_KV_HEADS, G)
    bias = -slopes[:, :, None, None] * dist.astype(jnp.float32)
    scores = jnp.where(valid[None, :, None, None], scores + bias[None, None], NEG_INF)
    sink = sinks.astype(jnp.float32).reshape(N_KV_HEADS, G)[None, None, :, :, None, None]
    m = jnp.maximum(jnp.max(scores, axis=-1, keepdims=True), sink)
    p = jnp.exp(scores - m)
    denom = jnp.sum(p, axis=-1, keepdims=True) + jnp.exp(sink - m)
    out = jnp.einsum('bnkgqs,bnskd->bnqkgd', (p / denom).astype(v.dtype), vb)
    return out.reshape(b, s, ATTN_WIDTH)

def rg_lru(x, gate_a_w, gate_a_b, gate_x_w, gate_x_b, lam):
    b, s, _ = x.shape
    xh = x.reshape(b, s, LRU_HEADS, HEAD_DIM)
    r = jax.nn.sigmoid(jnp.einsum('bshd,hde->bshe', xh, gate_a_w).reshape(b, s, LRU_WIDTH) + gate_a_b)
    i = jax.nn.sigmoid(jnp.einsum('bshd,hde->bshe', xh, gate_x_w).reshape(b, s, LRU_WIDTH) + gate_x_b)
    log_a = -LRU_C * r.astype(jnp.float32) * jax.nn.softplus(-lam.astype(jnp.float32))
    a = jnp.exp(log_a)
    mult = jnp.sqrt(-jnp.expm1(2.0 * log_a))
    first = (jnp.arange(s) == 0)[None, :, None]
    mult = jnp.where(first, 1.0, mult)
    u = mult * (i * x).astype(jnp.float32)

    def combine(left, right):
        a1, b1 = left
        a2, b2 = right
        return a1 * a2, a2 * b1 + b2

    _, h = lax.associative_scan(combine, (a, u), axis=1)
    return h.astype(x.dtype)

def hybrid_mixer(h, w_in, w_out, sinks, lru_conv_w, lru_conv_b, lru_gate_a_w, lru_gate_a_b,
                 lru_gate_x_w, lru_gate_x_b, lru_lambda, sc_conv_w):
    proj = h @ w_in
    offs = np.cumsum(IN_SPLITS_2)[:-1].tolist()
    q, k, v, lx, lg, sb, sc, sx = jnp.split(proj, offs, axis=-1)
    y_attn = sliding_window_attention(q, k, v, sinks)
    lx = causal_depthwise_conv(lx, lru_conv_w, lru_conv_b)
    y_lru = jax.nn.gelu(lg) * rg_lru(lx, lru_gate_a_w, lru_gate_a_b, lru_gate_x_w, lru_gate_x_b, lru_lambda)
    y_sc = sb * causal_depthwise_conv(sc * sx, sc_conv_w)
    y = jnp.concatenate([y_attn, y_lru, y_sc], axis=-1)
    return y @ w_out

def second_inputs(seed: int = 0) -> dict:
    key = jax.random.key(seed)
    ks = jax.random.split(key, 24)
    f32 = jnp.float32

    def nrm(k, shape, scale):
        return jax.random.normal(k, shape, f32) * scale

    u = jax.random.uniform(ks[17], (DEPTH_2, LRU_WIDTH), f32, 0.9, 0.999)
    a0 = u ** (1.0 / LRU_C)
    lru_lambda = jnp.log(a0) - jnp.log1p(-a0)
    return {
        "x": nrm(ks[0], (BATCH, SEQ, D_MODEL), 1.0),
        "c": nrm(ks[1], (BATCH, D_MODEL), 1.0),
        "w_mod": nrm(ks[2], (DEPTH_2, D_MODEL, N_MOD * D_MODEL), D_MODEL ** -0.5),
        "b_mod": nrm(ks[3], (DEPTH_2, N_MOD * D_MODEL), 0.02),
        "g_norm": 1.0 + nrm(ks[4], (DEPTH_2, N_SUBLAYERS, D_MODEL), 0.02),
        "w_ffn1_gu": nrm(ks[5], (DEPTH_2, D_MODEL, 2 * D_FF), D_MODEL ** -0.5),
        "w_ffn1_down": nrm(ks[6], (DEPTH_2, D_FF, D_MODEL), D_FF ** -0.5),
        "w_ffn2_gu": nrm(ks[7], (DEPTH_2, D_MODEL, 2 * D_FF), D_MODEL ** -0.5),
        "w_ffn2_down": nrm(ks[8], (DEPTH_2, D_FF, D_MODEL), D_FF ** -0.5),
        "w_in": nrm(ks[9], (DEPTH_2, D_MODEL, IN_PROJ_WIDTH), D_MODEL ** -0.5),
        "w_out": nrm(ks[10], (DEPTH_2, MIX_WIDTH, D_MODEL), MIX_WIDTH ** -0.5),
        "attn_sinks": nrm(ks[11], (DEPTH_2, N_Q_HEADS), 0.5),
        "lru_conv_w": nrm(ks[12], (DEPTH_2, LRU_CONV_K, LRU_WIDTH), LRU_CONV_K ** -0.5),
        "lru_conv_b": nrm(ks[13], (DEPTH_2, LRU_WIDTH), 0.02),
        "lru_gate_a_w": nrm(ks[14], (DEPTH_2, LRU_HEADS, HEAD_DIM, HEAD_DIM), HEAD_DIM ** -0.5),
        "lru_gate_a_b": nrm(ks[15], (DEPTH_2, LRU_WIDTH), 0.02),
        "lru_gate_x_w": nrm(ks[16], (DEPTH_2, LRU_HEADS, HEAD_DIM, HEAD_DIM), HEAD_DIM ** -0.5),
        "lru_gate_x_b": nrm(ks[18], (DEPTH_2, LRU_WIDTH), 0.02),
        "lru_lambda": lru_lambda,
        "sc_conv_w": nrm(ks[19], (DEPTH_2, SHORT_CONV_K, CONV_WIDTH), SHORT_CONV_K ** -0.5),
        "g_final": 1.0 + nrm(ks[20], (D_MODEL,), 0.02),
    }

def second_block(x, c, w_mod, b_mod, g_norm, w_ffn1_gu, w_ffn1_down, w_ffn2_gu, w_ffn2_down,
              w_in, w_out, attn_sinks, lru_conv_w, lru_conv_b, lru_gate_a_w, lru_gate_a_b,
              lru_gate_x_w, lru_gate_x_b, lru_lambda, sc_conv_w, g_final):
    c_act = jax.nn.silu(c)
    for l in range(DEPTH_2):
        mod = (c_act @ w_mod[l] + b_mod[l]).reshape(c.shape[0], N_MOD, D_MODEL)
        h = modulate(x, g_norm[l, 0], mod[:, 0], mod[:, 1])
        x = x + 0.5 * mod[:, 2][:, None, :] * swiglu_2(h, w_ffn1_gu[l], w_ffn1_down[l])
        h = modulate(x, g_norm[l, 1], mod[:, 3], mod[:, 4])
        x = x + mod[:, 5][:, None, :] * hybrid_mixer(
            h, w_in[l], w_out[l], attn_sinks[l], lru_conv_w[l], lru_conv_b[l],
            lru_gate_a_w[l], lru_gate_a_b[l], lru_gate_x_w[l], lru_gate_x_b[l],
            lru_lambda[l], sc_conv_w[l])
        h = modulate(x, g_norm[l, 2], mod[:, 6], mod[:, 7])
        x = x + 0.5 * mod[:, 8][:, None, :] * swiglu_2(h, w_ffn2_gu[l], w_ffn2_down[l])
    return rmsnorm_2(x, g_final)


def setup_inputs(seed=0):
    out = dict(first_inputs(seed))
    for name, value in second_inputs(seed + 1).items():
        if name != "x":
            out[name + "_2"] = value
    return out


def reference(
    x, c, w_ada, b_ada, norm1_g, w_in, hg_lb_logits, hg_norm_g, cmp_pos_k, cmp_w1_k, cmp_b1_k,
    cmp_w2_k, cmp_pos_v, cmp_w1_v, cmp_b1_v, cmp_w2_v, w_out, norm2_g, router_w, router_bias,
    w_exp_gu, w_exp_dn, w_sh_gu, w_sh_dn, final_g, c_2, w_mod_2, b_mod_2, g_norm_2, w_ffn1_gu_2,
    w_ffn1_down_2, w_ffn2_gu_2, w_ffn2_down_2, w_in_2, w_out_2, attn_sinks_2, lru_conv_w_2,
    lru_conv_b_2, lru_gate_a_w_2, lru_gate_a_b_2, lru_gate_x_w_2, lru_gate_x_b_2, lru_lambda_2,
    sc_conv_w_2, g_final_2,
):
    x = first_block(
        x, c, w_ada, b_ada, norm1_g, w_in, hg_lb_logits, hg_norm_g, cmp_pos_k, cmp_w1_k,
        cmp_b1_k, cmp_w2_k, cmp_pos_v, cmp_w1_v, cmp_b1_v, cmp_w2_v, w_out, norm2_g, router_w,
        router_bias, w_exp_gu, w_exp_dn, w_sh_gu, w_sh_dn, final_g,
    )
    return second_block(
        x, c_2, w_mod_2, b_mod_2, g_norm_2, w_ffn1_gu_2, w_ffn1_down_2, w_ffn2_gu_2,
        w_ffn2_down_2, w_in_2, w_out_2, attn_sinks_2, lru_conv_w_2, lru_conv_b_2,
        lru_gate_a_w_2, lru_gate_a_b_2, lru_gate_x_w_2, lru_gate_x_b_2, lru_lambda_2,
        sc_conv_w_2, g_final_2,
    )


_drawn_inputs = setup_inputs


def setup_inputs(seed=0):
    import zlib

    import numpy as np

    out = dict(_drawn_inputs(seed))
    spreads = {}
    factors = {'norm1_g': 2.745,
     'hg_norm_g': 5.719,
     'cmp_pos_k': 8.0,
     'cmp_b1_k': 44.363,
     'cmp_b1_v': 43.662,
     'attn_sinks_2': 3.595,
     'lru_gate_a_b_2': 25.472,
     'lru_gate_x_b_2': 8.0,
     'g_final_2': 8.108,
     'cmp_pos_v': 6.705,
     'norm2_g': 3.924}
    for name, (base, spread) in spreads.items():
        noise = np.random.default_rng([zlib.crc32(name.encode()), seed]).standard_normal(out[name].shape)
        drawn = base * np.exp(spread * noise) if base else spread * noise
        out[name] = __import__('jax').numpy.asarray(drawn.astype(out[name].dtype))
    for name, factor in factors.items():
        out[name] = (out[name] * factor).astype(out[name].dtype)
    return out
```

```python
from contextlib import ExitStack, contextmanager

import numpy as np

import concourse.bass as bass
from concourse import mybir

F32 = mybir.dt.float32
I32 = mybir.dt.int32
U32 = mybir.dt.uint32
ACT = mybir.ActivationFunctionType
ALU = mybir.AluOpType
AX = mybir.AxisListType

P = 128
S = 512
D = 1024
KD = D // P
TT = S // P
EPS = 1e-6
HEADS = 4
NSA_PAIRS = 4
N_CMP, CMP_STRIDE, CMP_BLOCK = 31, 16, 32
E, TOPK, GROUPS, TOPG = 64, 8, 8, 4
EH = 256
BLK = 128
NBLK = S * TOPK // BLK + E
ROUTED_SCALE = 2.5
FT = 22
NEG = -1e30
LN_FLOOR = 2.0 ** -63

Q0, F0, G0, NQ0, KC, VC, KS, KW, HI0, VS, VW = 0, 4, 8, 12, 16, 17, 18, 19, 20, 24, 25
IN_TILES = 26
AQ0, AK, AV, LX0, LG0, SB0, SC0, SX0 = 0, 4, 5, 6, 8, 10, 12, 14
IN_TILES_2 = 16

VEC_COLS = [
    ("c", 8), ("b_ada", 48), ("norm1_g", 8), ("lb0", 4), ("lb1", 4), ("hg_norm_g", 4), ("b1_k", 2), ("b1_v", 2),
    ("norm2_g", 8), ("final_g", 8), ("c_2", 8), ("b_mod0", 72), ("b_mod1", 72), ("g_norm", 48), ("conv_w", 16),
    ("conv_b", 4), ("gate_a_b", 4), ("gate_x_b", 4), ("lam", 4), ("sc_conv_w", 12), ("g_final", 8),
    ("router_bias", 64), ("sinks", 16),
]
CONST_COLS = [
    ("ident", 128), ("before", 128), ("rot", 128), ("cos", 512), ("sin", 512), ("levels", 8 * 128), ("causal", 128),
    ("cmp_add", 4 * 31), ("cmp_keep", 31), ("lower8", 64), ("iota", 1), ("tokens", 4),
]


def offsets(cols):
    out, at = {}, 0
    for name, n in cols:
        out[name] = (at, at + n)
        at += n
    return out, at


VEC, NVEC = offsets(VEC_COLS)
CON, NCON = offsets(CONST_COLS)


class Chain:

    def __init__(self, eng, sem, base=0):
        self.eng, self.sem, self.base, self.n = eng, sem, base, 0

    def __call__(self, ins):
        self.n += 1
        ins.then_inc(self.sem, 1)
        self.eng.wait_ge(self.sem, self.base + self.n)


def in_pairs(eng, n, body, first=0):
    if n // 2 > first:
        with eng.Fori(first, n // 2) as r:
            body(r, 0)
            body(r, 1)
    if n % 2:
        body(n // 2, 0)


class Kernel:
    def __init__(self, nc, t):
        self.nc, self.t = nc, t
        sb = nc.alloc_sbuf_tensor
        self.xT = sb("xT", [P, KD, S], F32)
        self.hT = sb("hT", [P, KD, S], F32)
        self.vec = sb("vec", [P, NVEC], F32)
        self.con = sb("con", [P, NCON], F32)
        self.ones = sb("ones", [P, P], F32)
        self.eps = sb("eps", [P, 1], F32)
        self.mod = sb("mod", [P, 72], F32)
        self.pre = sb("pre", [P, KD], F32)

        self.stages = 0

    @contextmanager
    def stage(self, name):
        self.stages += 1
        self.tag = f"{name}{self.stages}_"
        with self.nc.cleanup_on_exit():
            yield

    def sem(self, name):
        return self.nc.alloc_semaphore(self.tag + name)

    def sems(self, names):
        return [self.sem(n) for n in names.split()]

    def sb(self, name, shape, dt=F32):
        return self.nc.alloc_sbuf_tensor(self.tag + name, shape, dt)

    def psum(self, name, banks):
        return self.nc.alloc_psum_tensor(self.tag + name + "_psum", [P, banks, S], F32)

    def v(self, name, a=0, b=None):
        lo, hi = VEC[name]
        return self.vec[:, lo + a:(hi if b is None else lo + b)]

    def c(self, name):
        lo, hi = CON[name]
        return self.con[:, lo:hi]

    def setup(self):
        nc, t = self.nc, self.t
        with self.stage("load"):
            loaded = self.sem("loaded")
            with nc.Block() as block:
                @block.sync
                def _(sp):
                    sp.dma_start(self.vec[:], t["vecs"]).then_inc(loaded, 16)
                    sp.dma_start(self.con[:], t["consts"]).then_inc(loaded, 16)
                    sp.dma_start(self.xT[:], t["xT"].rearrange("(n p) t -> p n t", p=P)).then_inc(loaded, 16)
                    sp.wait_ge(loaded, 48)

                @block.gpsimd
                def _(pool):
                    nc.gpsimd.memset(self.ones[:], 1.0)
                    nc.gpsimd.memset(self.eps[:], EPS)

    def modulation(self, w, c, b, tiles):
        nc = self.nc
        n = tiles * P
        with self.stage("mod"):
            wk = self.sb("wk", [P, 2, n])
            acc = self.sb("acc", [P, n])
            ca = self.sb("ca", [P, KD])
            ps = self.psum("ps", 1)[:, 0, :]
            loaded = [self.sem(f"loaded{s}") for s in range(2)]
            act_done, summed, turned = self.sems("c_ready rows_summed turned")
            with nc.Block() as block:
                @block.sync
                def _(sp):
                    for k in range(KD):
                        if k >= 2:
                            sp.wait_ge(summed, k - 1)
                        sp.dma_start(wk[:, k % 2, :], w[k * P:(k + 1) * P, :]).then_inc(loaded[k % 2], 16)

                @block.scalar
                def _(act):
                    nc.scalar.activation(ca[:], c, ACT.Silu).then_inc(act_done, 1)

                @block.vector
                def _(dve):
                    dve.wait_ge(act_done, 1)
                    for k in range(KD):
                        dve.wait_ge(loaded[k % 2], 16 * (k // 2 + 1))
                        if k == 0:
                            nc.vector.tensor_scalar(acc[:], wk[:, 0, :], ca[:, 0:1], None, ALU.mult).then_inc(summed, 1)
                        else:
                            dve.wait_ge(summed, k)
                            nc.vector.scalar_tensor_tensor(out=acc[:], in0=wk[:, k % 2, :], scalar=ca[:, k:k + 1],
                                                           in1=acc[:], op0=ALU.mult, op1=ALU.add).then_inc(summed, 1)
                    dve.wait_ge(turned, 1)
                    nc.vector.tensor_tensor(self.mod[:, 0:tiles], ps[:, 0:tiles], b, ALU.add)

                @block.tensor
                def _(pe):
                    pe.wait_ge(summed, KD)
                    for i in range(tiles):
                        last = nc.tensor.matmul(ps[:, i:i + 1], acc[:, i * P:(i + 1) * P], self.ones[:, 0:1],
                                                start=True, stop=True)
                    last.then_inc(turned, 1)

    def norm(self, dst, g, scale=None, shift=None):
        nc, xT = self.nc, self.xT
        with self.stage("norm"):
            sq = self.sb("sq", [P, 2, S])
            rstd = self.sb("rstd", [P, S])
            xn = self.sb("xn", [P, 2, S])
            ps = self.psum("ps", 1)[:, 0, :]
            squared, sq_used, summed, rooted, inverted, pre_done, xn_ready, xn_used = (
                self.sem(x) for x in ("squared", "sq_used", "summed", "rooted", "inverted", "pre_done", "xn_ready",
                                                "xn_used"))
            with nc.Block() as block:
                @block.scalar
                def _(act):
                    for k in range(KD):
                        if k >= 2:
                            act.wait_ge(sq_used, k - 1)
                        nc.scalar.activation(sq[:, k % 2, :], xT[:, k, :], ACT.Square).then_inc(squared, 1)
                    act.wait_ge(summed, 1)
                    nc.scalar.activation(rstd[:], ps, ACT.Sqrt, bias=self.eps[:, 0:1], scale=1.0 / D).then_inc(rooted, 1)
                    act.wait_ge(pre_done, 1)
                    for k in range(KD):
                        act.wait_ge(xn_ready, k + 1)
                        if shift is None:
                            nc.scalar.activation(dst[:, k, :], xn[:, k % 2, :], ACT.Copy, scale=self.pre[:, k:k + 1])\
                                .then_inc(xn_used, 1)
                        else:
                            nc.scalar.activation(dst[:, k, :], xn[:, k % 2, :], ACT.Identity, bias=shift[:, k:k + 1],
                                                 scale=self.pre[:, k:k + 1]).then_inc(xn_used, 1)

                @block.tensor
                def _(pe):
                    for k in range(KD):
                        pe.wait_ge(squared, k + 1)
                        mm = nc.tensor.matmul(ps, self.ones[:], sq[:, k % 2, :], start=k == 0, stop=k == KD - 1)
                        mm.then_inc(sq_used, 1)
                    pe.wait_ge(sq_used, KD)
                    pe.sem_inc(summed, 1)

                @block.vector
                def _(dve):
                    if scale is None:
                        nc.vector.tensor_copy(self.pre[:], g).then_inc(pre_done, 1)
                    else:
                        nc.vector.scalar_tensor_tensor(out=self.pre[:], in0=scale, scalar=1.0, in1=g, op0=ALU.add,
                                                       op1=ALU.mult).then_inc(pre_done, 1)
                    dve.wait_ge(rooted, 1)
                    nc.vector.reciprocal(rstd[:], rstd[:]).then_inc(inverted, 1)
                    dve.wait_ge(inverted, 1)
                    for k in range(KD):
                        if k >= 2:
                            dve.wait_ge(xn_used, k - 1)
                        nc.vector.tensor_tensor(xn[:, k % 2, :], xT[:, k, :], rstd[:], ALU.mult).then_inc(xn_ready, 1)

    def project(self, w, pairs, out):
        nc, src = self.nc, self.hT
        with self.stage("proj"):
            wt = self.sb("wt", [P, 2, KD, 2 * P])
            ps = self.psum("ps", 4)
            loaded = [self.sem(f"loaded{s}") for s in range(2)]
            tile_done, bank_free = self.sem("tile_done"), self.sem("bank_free")
            with nc.Block() as block:
                @block.sync
                def _(sp):
                    def load(r, s):
                        sp.dma_start(wt[:, s], w[bass.ds(2 * r + s, 1)].rearrange("a p k n -> (a p) k n"))\
                            .then_inc(loaded[s], 16)

                    def load_again(r, s):
                        sp.wait_ge(tile_done, 4 * r + 2 * s - 2)
                        load(r, s)
                    load(0, 0)
                    load(0, 1)
                    in_pairs(sp, pairs, load_again, first=1)

                @block.tensor
                def _(pe):
                    def tiles(r, s):
                        pe.wait_ge(loaded[s], 16 * (r + 1))
                        for u in range(2):
                            pe.wait_ge(bank_free, 4 * r + 2 * s + u + 1)
                            for k in range(KD):
                                mm = nc.tensor.matmul(ps[:, 2 * s + u, :], wt[:, s, k, u * P:(u + 1) * P], src[:, k, :],
                                                      start=k == 0, stop=k == KD - 1)
                            mm.then_inc(tile_done, 1)
                    in_pairs(pe, pairs, tiles)

                @block.scalar
                def _(act):
                    act.sem_inc(bank_free, 4)

                    def evacuate(r, s):
                        for u in range(2):
                            act.wait_ge(tile_done, 4 * r + 2 * s + u + 1)
                            nc.scalar.activation(out[:, bass.ds(4 * r + 2 * s + u, 1), :].rearrange("p a t -> p (a t)"),
                                                 ps[:, 2 * s + u, :], ACT.Copy).then_inc(bank_free, 1)
                    in_pairs(act, pairs, evacuate)

    def turn_tiles(self, proj, tiles, out):
        nc = self.nc
        with self.stage("turn"):
            ps = self.psum("ps", 4)
            turned, bank_free = self.sems("turned bank_free")
            with nc.Block() as block:
                @block.tensor
                def _(pe):
                    for n, tile in enumerate(tiles):
                        if n >= 4:
                            pe.wait_ge(bank_free, n - 3)
                        for c in range(TT):
                            mm = nc.tensor.transpose(ps[:, n % 4, c * P:(c + 1) * P], proj[:, tile, c * P:(c + 1) * P],
                                                     self.c("ident"))
                        mm.then_inc(turned, 1)

                @block.scalar
                def _(act):
                    for n in range(len(tiles)):
                        act.wait_ge(turned, n + 1)
                        nc.scalar.activation(out[:, :, n * P:(n + 1) * P],
                                             ps[:, n % 4, :].rearrange("p (c f) -> p c f", c=TT), ACT.Copy)\
                            .then_inc(bank_free, 1)

    def attention_gates(self, gates):
        nc = self.nc
        with self.stage("gates"):
            wg = self.sb("wg", [P, KD, 24])
            ps = self.psum("ps", 1)[:, 0, :]
            loaded, done = self.sems("loaded done")
            with nc.Block() as block:
                @block.sync
                def _(sp):
                    sp.dma_start(wg[:], self.t["w_gates"]).then_inc(loaded, 16)

                @block.tensor
                def _(pe):
                    pe.wait_ge(loaded, 16)
                    for c in range(TT):
                        for k in range(KD):
                            mm = nc.tensor.matmul(ps[:, c * 24:(c + 1) * 24], self.hT[:, k, c * P:(c + 1) * P], wg[:, k, :],
                                                  start=k == 0, stop=k == KD - 1)
                    mm.then_inc(done, 1)

                @block.scalar
                def _(act):
                    act.wait_ge(done, 1)
                    nc.scalar.activation(gates[:].rearrange("p c n -> p (c n)"), ps[:, 0:TT * 24], ACT.Sigmoid)

    def hgrn(self, proj, vals):
        nc = self.nc
        W = HEADS * S
        with self.stage("hgrn"):
            f, b, ed, kk, qs, ql, kl = (self.sb(x, [P, HEADS, S]) for x in "f b ed kk qs ql kl".split())
            prod, at = self.sb("prod", [P, W]), self.sb("at", [P, W])
            qe, kend = f, ed
            kend_t = self.sb("kend_t", [P, HEADS, 3, P])
            state = self.sb("state", [P, 3, HEADS, P])
            dec = self.sb("dec", [P, HEADS, TT])
            lb, oml = self.sb("lb", [P, HEADS]), self.sb("oml", [P, HEADS])
            ps = self.psum("ps", 8)
            (lb_sub, lb_done, sig, f_done, log_done, scanned, k_done, q_done, shifted, decayed, ql_done, kl_done, mm_done,
             masked, added, s_chain, qe_done, kend_done, dec_done, k_turned, k_copied, sv_done, st_done) = self.sems(
                "lb_sub lb_done sig f_done log_done scanned k_done q_done shifted decayed ql_done kl_done mm_done masked "
                "added chain qe_done kend_done dec_done k_turned k_copied sv_done st_done")
            flat = lambda x: x[:].rearrange("p h t -> p (h t)")
            halves = lambda x, m: x[:].rearrange("p h (g m) -> p (h g) m", m=2 * m)
            LEVELS = [64 >> i for i in range(7)] + [0]

            with nc.Block() as block:
                def mask(dve, i):
                    dve.wait_ge(mm_done, i + 1)
                    lev = self.c("levels")[:, i * P:(i + 1) * P].rearrange("p (a t) -> p a t", a=1)
                    src = ps[:, 4 * (i % 2):4 * (i % 2) + 4, :].rearrange("p b (c t) -> p (b c) t", t=P)
                    if i:
                        dve.wait_ge(added, i + 1)
                    nc.vector.tensor_tensor(prod[:].rearrange("p (c t) -> p c t", t=P), src,
                                            lev.broadcast_to([P, HEADS * TT, P]), ALU.mult).then_inc(masked, 1)

                def add(pool, i):
                    pool.wait_ge(masked, i + 1)
                    pool.wait_ge(added, i + 1)
                    nc.gpsimd.tensor_tensor(at[:], at[:], prod[:], ALU.add).then_inc(added, 1)

                @block.scalar
                def _(act):
                    act.wait_ge(lb_sub, 1)
                    nc.scalar.activation(lb[:], lb[:], ACT.Sigmoid).then_inc(lb_done, 1)
                    nc.scalar.activation(flat(f), proj[:, F0:F0 + HEADS, :].rearrange("p h t -> p (h t)"), ACT.Sigmoid)\
                        .then_inc(sig, 1)
                    act.wait_ge(f_done, HEADS + 1)
                    nc.scalar.activation(flat(ql), flat(f), ACT.Ln).then_inc(log_done, 1)
                    for i, m in enumerate(LEVELS[:-1]):
                        act.wait_ge(shifted, 2 * i + 2)
                        nc.scalar.activation(flat(ed), flat(ed), ACT.Exp).then_inc(decayed, 1)
                    act.wait_ge(f_done, HEADS + 1)
                    act.wait_ge(k_done, 1)
                    nc.scalar.activation(flat(qe), flat(b), ACT.Exp).then_inc(qe_done, 1)
                    act.wait_ge(shifted, 15)
                    nc.scalar.activation(flat(kend), flat(kend), ACT.Exp).then_inc(kend_done, 1)
                    nc.scalar.activation(dec[:], b[:].rearrange("p h (c t) -> p h c t", t=P)[:, :, :, P - 1], ACT.Exp)\
                        .then_inc(dec_done, 1)
                    for h in range(HEADS):
                        act.wait_ge(k_turned, h + 1)
                        nc.scalar.activation(kend_t[:, h].rearrange("p c d -> p (c d)"), ps[:, h, 0:3 * P], ACT.Copy)\
                            .then_inc(k_copied, 1)

                @block.vector
                def _(dve):
                    chain = Chain(dve, s_chain)
                    nc.vector.tensor_tensor(lb[:], self.v("lb0"), self.v("lb1"), ALU.subtract).then_inc(lb_sub, 1)
                    dve.wait_ge(lb_done, 1)
                    chain(nc.vector.tensor_scalar(oml[:], lb[:], -1.0, 1.0, ALU.mult, ALU.add))
                    dve.wait_ge(sig, 1)
                    for h in range(HEADS):
                        nc.vector.tensor_scalar(f[:, h, :], f[:, h, :], oml[:, h:h + 1], lb[:, h:h + 1], ALU.mult, ALU.add)\
                            .then_inc(f_done, 1)
                    dve.wait_ge(f_done, HEADS)
                    nc.vector.tensor_scalar(flat(kk), flat(f), -1.0, 1.0, ALU.mult, ALU.add).then_inc(k_done, 1)
                    dve.wait_ge(k_done, 1)
                    nc.vector.tensor_scalar(flat(f), flat(f), LN_FLOOR, None, ALU.max).then_inc(f_done, 1)
                    nc.vector.tensor_scalar(flat(qs), proj[:, Q0:Q0 + HEADS, :].rearrange("p h t -> p (h t)"), P ** -0.5,
                                            None, ALU.mult).then_inc(q_done, 1)
                    dve.wait_ge(log_done, 1)
                    for h in range(HEADS):
                        for c in range(TT):
                            nc.vector.tensor_tensor_scan(b[:, h, c * P:(c + 1) * P], self.ones[:], ql[:, h, c * P:(c + 1) * P],
                                                         0.0, ALU.mult, ALU.add).then_inc(scanned, 1)
                    dve.wait_ge(scanned, HEADS * TT)
                    dve.wait_ge(q_done, 1)
                    for i, m in enumerate(LEVELS):
                        if m:
                            bh, eh = halves(b, m), halves(ed, m)
                            ref = bh[:, :, m - 1:m].broadcast_to([P, W // (2 * m), m])
                            if i:
                                dve.wait_ge(kl_done, i)
                                dve.wait_ge(ql_done, i)
                            nc.vector.tensor_tensor(eh[:, :, 0:m], ref, bh[:, :, 0:m], ALU.subtract).then_inc(shifted, 1)
                            nc.vector.tensor_tensor(eh[:, :, m:2 * m], bh[:, :, m:2 * m], ref, ALU.subtract)\
                                .then_inc(shifted, 1)
                            if i:
                                dve.wait_ge(mm_done, i)
                            dve.wait_ge(decayed, i + 1)
                            nc.vector.tensor_tensor(flat(ql), flat(qs), flat(ed), ALU.mult).then_inc(ql_done, 1)
                        if i:
                            mask(dve, i - 1)
                    bc = b[:].rearrange("p h (c t) -> p (h c) t", t=P)
                    dve.wait_ge(ql_done, 7)
                    dve.wait_ge(kl_done, 7)
                    nc.vector.tensor_tensor(kend[:].rearrange("p h (c t) -> p (h c) t", t=P),
                                            bc[:, :, P - 1:P].broadcast_to([P, HEADS * TT, P]), bc, ALU.subtract)\
                        .then_inc(shifted, 1)
                    mask(dve, 7)
                    dve.wait_ge(qe_done, 1)
                    nc.vector.tensor_tensor(flat(qe), flat(qe), flat(qs), ALU.mult).then_inc(qe_done, 1)
                    dve.wait_ge(kend_done, 1)
                    nc.vector.tensor_tensor(flat(kend), flat(kend), flat(kk), ALU.mult).then_inc(kend_done, 1)
                    dve.wait_ge(dec_done, 1)
                    for c in range(3):
                        dve.wait_ge(sv_done, c + 1)
                        pc = ps[:, 4 + c, :]
                        if c == 0:
                            nc.vector.tensor_copy(state[:, 0].rearrange("p h e -> p (h e)"), pc).then_inc(st_done, HEADS)
                        else:
                            dve.wait_ge(st_done, HEADS * c)
                            for h in range(HEADS):
                                nc.vector.scalar_tensor_tensor(out=state[:, c, h, :], in0=state[:, c - 1, h, :],
                                                               scalar=dec[:, h, c:c + 1], in1=pc[:, h * P:(h + 1) * P],
                                                               op0=ALU.mult, op1=ALU.add).then_inc(st_done, 1)

                @block.gpsimd
                def _(pool):
                    pool.wait_ge(k_done, 1)
                    nc.gpsimd.memset(at[:], 0.0).then_inc(added, 1)
                    for i in range(len(LEVELS)):
                        if LEVELS[i]:
                            pool.wait_ge(decayed, i + 1)
                            if i:
                                pool.wait_ge(mm_done, i)
                            nc.gpsimd.tensor_tensor(flat(kl), flat(kk), flat(ed), ALU.mult).then_inc(kl_done, 1)
                        if i:
                            add(pool, i - 1)
                    add(pool, 7)

                @block.tensor
                def _(pe):
                    for i, m in enumerate(LEVELS):
                        if m:
                            pe.wait_ge(ql_done, i + 1)
                            pe.wait_ge(kl_done, i + 1)
                        if i >= 2:
                            pe.wait_ge(masked, i - 1)
                        q, k = (ql, kl) if m else (qs, kk)
                        for h in range(HEADS):
                            for c in range(TT):
                                r = slice(c * P, (c + 1) * P)
                                mm = nc.tensor.matmul(ps[:, 4 * (i % 2) + h, r], k[:, h, r], q[:, h, r], start=True, stop=True)
                        mm.then_inc(mm_done, 1)
                    pe.wait_ge(kend_done, 2)
                    pe.wait_ge(masked, 7)
                    for h in range(HEADS):
                        for c in range(3):
                            mm = nc.tensor.transpose(ps[:, h, c * P:(c + 1) * P], kend[:, h, c * P:(c + 1) * P],
                                                     self.c("ident"))
                        mm.then_inc(k_turned, 1)
                    pe.wait_ge(k_copied, HEADS)
                    pe.wait_ge(masked, 8)
                    for c in range(3):
                        for h in range(HEADS):
                            mm = nc.tensor.matmul(ps[:, 4 + c, h * P:(h + 1) * P], kend_t[:, h, c, :],
                                                  vals[:, c, h * P:(h + 1) * P], start=True, stop=True)
                        mm.then_inc(sv_done, 1)
                    pe.wait_ge(added, 9)
                    pe.wait_ge(qe_done, 2)
                    for h in range(HEADS):
                        for c in range(TT):
                            r = slice(c * P, (c + 1) * P)
                            if c:
                                pe.wait_ge(st_done, HEADS * c)
                            nc.tensor.matmul(ps[:, h, r], vals[:, c, h * P:(h + 1) * P], at[:, h * S + c * P:h * S + (c + 1) * P],
                                             start=True, stop=c == 0)
                            if c:
                                nc.tensor.matmul(ps[:, h, r], state[:, c - 1, h, :], qe[:, h, r], start=False, stop=True)
            self.hgrn_out(proj, ps, ed, ql, prod[:, 0:S], prod[:, S:2 * S])

    def hgrn_out(self, proj, ps, o, gate, sq, rstd):
        nc = self.nc
        copied, gated, squared, summed, rooted, inverted, scaled, done = self.sems(
            "o_copied gated squared summed rooted inverted scaled out_done")
        with nc.Block() as block:
            @block.scalar
            def _(act):
                nc.scalar.activation(gate[:].rearrange("p h t -> p (h t)"),
                                     proj[:, G0:G0 + HEADS, :].rearrange("p h t -> p (h t)"), ACT.Silu).then_inc(gated, 1)
                for h in range(HEADS):
                    if h:
                        act.wait_ge(summed, h)
                    nc.scalar.activation(sq[:], ps[:, h, :], ACT.Square).then_inc(squared, 1)
                    act.wait_ge(summed, h + 1)
                    if h:
                        act.wait_ge(scaled, h)
                    nc.scalar.activation(rstd[:], ps[:, 4 + h % 2, :], ACT.Sqrt, bias=self.eps[:, 0:1], scale=1.0 / P)\
                        .then_inc(rooted, 1)

            @block.tensor
            def _(pe):
                for h in range(HEADS):
                    pe.wait_ge(squared, h + 1)
                    if h >= 2:
                        pe.wait_ge(rooted, h - 1)
                    nc.tensor.matmul(ps[:, 4 + h % 2, :], self.ones[:], sq[:], start=True, stop=True).then_inc(summed, 1)

            @block.vector
            def _(dve):
                for h in range(HEADS):
                    dve.wait_ge(rooted, h + 1)
                    nc.vector.reciprocal(rstd[:], rstd[:]).then_inc(inverted, 1)
                    dve.wait_ge(inverted, h + 1)
                    nc.vector.tensor_tensor(o[:, h, :], ps[:, h, :], rstd[:], ALU.mult).then_inc(scaled, 1)
                    dve.wait_ge(scaled, h + 1)
                    dve.wait_ge(gated, 1)
                    nc.vector.scalar_tensor_tensor(out=self.hT[:, h, :], in0=o[:, h, :], scalar=self.v("hg_norm_g")[:, h:h + 1],
                                                   in1=gate[:, h, :], op0=ALU.mult, op1=ALU.mult).then_inc(done, 1)

    def rope(self, proj, rot):
        nc = self.nc
        tiles = [NQ0, NQ0 + 1, NQ0 + 2, NQ0 + 3, KS, KW]
        with self.stage("rope"):
            ps = self.psum("ps", 6)
            crossed = self.sb("crossed", [P, 2, S])
            scaled, turned, straight, cross, done = self.sems("q_scaled turned straight crossed done")
            with nc.Block() as block:
                @block.scalar
                def _(act):
                    q = proj[:, NQ0:NQ0 + 4, :]
                    nc.scalar.mul(q, q, 0.125).then_inc(scaled, 1)

                @block.tensor
                def _(pe):
                    pe.wait_ge(scaled, 1)
                    for n, tile in enumerate(tiles):
                        nc.tensor.matmul(ps[:, n, :], self.c("rot"), proj[:, tile, :], start=True, stop=True)\
                            .then_inc(turned, 1)

                @block.gpsimd
                def _(pool):
                    pool.wait_ge(scaled, 1)
                    for n, tile in enumerate(tiles):
                        nc.gpsimd.tensor_tensor(rot[:, n, :], proj[:, tile, :], self.c("cos"), ALU.mult).then_inc(straight, 1)

                @block.vector
                def _(dve):
                    for n in range(len(tiles)):
                        dve.wait_ge(turned, n + 1)
                        if n >= 2:
                            dve.wait_ge(done, n - 1)
                        nc.vector.tensor_tensor(crossed[:, n % 2, :], ps[:, n, :], self.c("sin"), ALU.mult).then_inc(cross, 1)
                        dve.wait_ge(cross, n + 1)
                        dve.wait_ge(straight, n + 1)
                        nc.vector.tensor_tensor(rot[:, n, :], rot[:, n, :], crossed[:, n % 2, :], ALU.add).then_inc(done, 1)

    def compress(self, proj, k_cmp, v_cmp):
        nc, t = self.nc, self.t
        N = S - 16
        B = 3 * N_CMP
        with self.stage("compress"):
            x = self.sb("x", [P, 2, 3, N])
            w1, w2 = self.sb("w1", [P, 2, 16, 256]), self.sb("w2", [P, 2, 2, 64])
            bias, hid = self.sb("bias", [P, 4]), self.sb("hid", [P, 2, 2, 2 * N_CMP])
            ps = self.psum("ps", 6)
            zeroed, loaded, hid_ps, bias_done, hid_done, out_ps = self.sems("zeroed loaded hidden_products bias_done hid_done out_products")
            with nc.Block() as block:
                @block.gpsimd
                def _(pool):
                    nc.gpsimd.memset(x[:, :, 2, :], 0.0).then_inc(zeroed, 1)
                    nc.gpsimd.memset(v_cmp[:], 0.0).then_inc(zeroed, 1)

                @block.sync
                def _(sp):
                    sp.wait_ge(zeroed, 1)
                    for n, (tile, name) in enumerate(((KC, "k"), (VC, "v"))):
                        for g in range(2):
                            rows = slice(64 * g, 64 * g + 64)
                            sp.dma_start(x[0:64, n, g, :], proj[rows, tile, 0:N]).then_inc(loaded, 16)
                            sp.dma_start(x[64:128, n, g, :], proj[rows, tile, 16:S]).then_inc(loaded, 16)
                        sp.dma_start(x[:, n, 2, 0:16], t[f"pos_{name}"]).then_inc(loaded, 16)
                        sp.dma_start(w1[:, n], t[f"w1_{name}"]).then_inc(loaded, 16)
                        sp.dma_start(w2[:, n], t[f"w2_{name}"]).then_inc(loaded, 16)

                @block.tensor
                def _(pe):
                    pe.wait_ge(loaded, 14 * 16)
                    for n in range(2):
                        for m in range(2):
                            for l in range(16):
                                mm = nc.tensor.matmul(ps[:, 2 * n + m, 0:B].rearrange("p (g c) -> p g c", g=3),
                                                      w1[:, n, l, m * P:(m + 1) * P],
                                                      x[:, n, :, l:l + CMP_STRIDE * (N_CMP - 1) + 1:CMP_STRIDE],
                                                      start=l == 0, stop=l == 15)
                            mm.then_inc(hid_ps, 1)
                    pe.wait_ge(hid_done, 4)
                    for g in range(2):
                        for m in range(2):
                            mm = nc.tensor.matmul(ps[64 * g:64 * g + 64, 4, 0:N_CMP], w2[:, 0, m, :],
                                                  hid[:, 0, m, g * N_CMP:(g + 1) * N_CMP], start=m == 0, stop=m == 1)
                    for g in range(2):
                        for m in range(2):
                            mm = nc.tensor.matmul(ps[0:N_CMP, 5, 64 * g:64 * g + 64], hid[:, 1, m, g * N_CMP:(g + 1) * N_CMP],
                                                  w2[:, 1, m, :], start=m == 0, stop=m == 1)
                    mm.then_inc(out_ps, 1)

                @block.vector
                def _(dve):
                    for i in range(4):
                        dve.wait_ge(hid_ps, i + 1)
                        b1 = self.v("b1_k" if i < 2 else "b1_v")
                        nc.vector.tensor_tensor(bias[:, i:i + 1], ps[:, i, 2 * N_CMP:2 * N_CMP + 1], b1[:, i % 2:i % 2 + 1],
                                                ALU.add).then_inc(bias_done, 1)
                    dve.wait_ge(out_ps, 1)
                    dve.wait_ge(zeroed, 2)
                    nc.vector.tensor_copy(k_cmp[:], ps[:, 4, 0:N_CMP])
                    nc.vector.tensor_copy(v_cmp[0:N_CMP, :], ps[0:N_CMP, 5, 0:P])

                @block.scalar
                def _(act):
                    for i in range(4):
                        act.wait_ge(bias_done, i + 1)
                        nc.scalar.activation(hid[:, i // 2, i % 2, :], ps[:, i, 0:2 * N_CMP], ACT.Gelu_apprx_tanh,
                                             bias=bias[:, i:i + 1]).then_inc(hid_done, 1)

    def attend(self, items, out_tile, sink=None):
        nc = self.nc
        n_items = len(items)
        with self.stage("attend"):
            p = self.sb("p", [P, 3, S])
            pt = self.sb("pt", [P, 2, S])
            top, den, fac = (self.sb(x, [P, n_items]) for x in "top den fac".split())
            es = self.sb("es", [P, n_items])
            psS, psT, psO = self.psum("scores", 3), self.psum("turned", 2), self.psum("outs", 2)
            (zeroed, scores, masked, topped, expd, facd, scaled, turned, copied, products, moved, kept, raw_top, sunk) = self.sems(
                "zeroed scores masked topped expd fac_ready scaled turned copied products moved kept raw_top sunk")
            keys = [it["k"].shape[-1] for it in items]
            wide = [-(-n // P) * P for n in keys]
            pairs_before = [sum(x["last"] for x in items[:i]) for i in range(n_items + 1)]

            with nc.Block() as block:
                @block.gpsimd
                def _(pool):
                    nc.gpsimd.memset(p[:], 0.0).then_inc(zeroed, 1)
                    for i, it in enumerate(items):
                        pool.wait_ge(facd, i + 1)
                        s = p[:, i % 3, 0:wide[i]]
                        if it["keep"] is not None:
                            seen = p[:, i % 3, 0:keys[i]]
                            nc.gpsimd.tensor_tensor(seen, seen, it["keep"], ALU.mult).then_inc(kept, 1)
                            pool.wait_ge(kept, sum(x["keep"] is not None for x in items[:i + 1]))
                        if it["gate"] is None:
                            nc.gpsimd.tensor_scalar(s, s, fac[:, i:i + 1], None, ALU.mult).then_inc(scaled, 1)
                        else:
                            nc.gpsimd.tensor_scalar(s, s, fac[:, i:i + 1], it["gate"], ALU.mult, ALU.mult)\
                                .then_inc(scaled, 1)

                @block.tensor
                def _(pe):
                    def score(i):
                        it = items[i]
                        if i >= 3:
                            pe.wait_ge(expd, i - 2)
                        nc.tensor.matmul(psS[:, i % 3, 0:keys[i]], it["q"], it["k"], start=True, stop=True).then_inc(scores, 1)

                    def turn(i):
                        pe.wait_ge(scaled, i + 1)
                        if i >= 2:
                            pe.wait_ge(copied, i - 1)
                        for b in range(wide[i] // P):
                            mm = nc.tensor.transpose(psT[:, i % 2, b * P:(b + 1) * P], p[:, i % 3, b * P:(b + 1) * P],
                                                     self.c("ident"))
                        mm.then_inc(turned, 1)

                    def multiply(i):
                        it = items[i]
                        pe.wait_ge(copied, i + 1)
                        pair = pairs_before[i]
                        if pair >= 2:
                            pe.wait_ge(moved, pair - 1)
                        lo = it["out"][0]
                        for b, v in enumerate(it["v"]):
                            mm = nc.tensor.matmul(psO[lo:lo + 64, pair % 2, 0:P], v, pt[:, i % 2, b * P:(b + 1) * P],
                                                  start=it["first"] and b == 0, stop=it["ends"] and b == len(it["v"]) - 1)
                        mm.then_inc(products, 1)

                    for i in range(n_items + 2):
                        if i < n_items:
                            score(i)
                        if 1 <= i <= n_items:
                            turn(i - 1)
                        if i >= 2:
                            multiply(i - 2)

                @block.vector
                def _(dve):
                    def find_top(i):
                        it = items[i]
                        dve.wait_ge(scores, i + 1)
                        s = psS[:, i % 3, 0:keys[i]]
                        if it["mask"] is not None:
                            at, mask = it["mask"]
                            n = mask.shape[-1]
                            nc.vector.tensor_tensor(s[:, at:at + n], s[:, at:at + n], mask, ALU.add).then_inc(masked, 1)
                            dve.wait_ge(masked, i + 1)
                        else:
                            dve.sem_inc(masked, 1)
                        if sink is None:
                            nc.vector.tensor_reduce(top[:, i:i + 1], s, AX.X, ALU.max, negate=True).then_inc(topped, 1)
                        else:
                            nc.vector.tensor_reduce(top[:, i:i + 1], s, AX.X, ALU.max).then_inc(raw_top, 1)
                            dve.wait_ge(raw_top, i + 1)
                            nc.vector.tensor_scalar(top[:, i:i + 1], top[:, i:i + 1], sink(i), -1.0, ALU.max, ALU.mult)\
                                .then_inc(topped, 1)

                    def factor(i):
                        dve.wait_ge(expd, i + 1)
                        d = den[:, i:i + 1]
                        if sink is not None:
                            nc.vector.tensor_tensor(d, d, es[:, i:i + 1], ALU.add).then_inc(sunk, 1)
                            dve.wait_ge(sunk, i + 1)
                        nc.vector.reciprocal(fac[:, i:i + 1], d).then_inc(facd, 1)

                    def move(i):
                        if 0 <= i < n_items and items[i]["last"]:
                            _, j, qt = items[i]["out"]
                            dve.wait_ge(products, i + 1)
                            nc.vector.tensor_copy(self.hT[:, out_tile + j, qt * P:(qt + 1) * P],
                                                  psO[:, pairs_before[i] % 2, 0:P]).then_inc(moved, 1)

                    for i in range(n_items + 3):
                        if i < n_items:
                            find_top(i)
                        if 1 <= i <= n_items:
                            factor(i - 1)
                        move(i - 3)

                @block.scalar
                def _(act):
                    act.wait_ge(zeroed, 1)

                    def exponents(i):
                        act.wait_ge(topped, i + 1)
                        if i >= 3:
                            act.wait_ge(turned, i - 2)
                        if sink is not None:
                            nc.scalar.activation(es[:, i:i + 1], sink(i), ACT.Exp, bias=top[:, i:i + 1])
                        nc.scalar.activation(p[:, i % 3, 0:keys[i]], psS[:, i % 3, 0:keys[i]], ACT.Exp, bias=top[:, i:i + 1],
                                             accum_out=den[:, i:i + 1]).then_inc(expd, 1)

                    def copy(i):
                        act.wait_ge(turned, i + 1)
                        if i >= 2:
                            act.wait_ge(products, i - 1)
                        nc.scalar.activation(pt[:, i % 2, 0:wide[i]], psT[:, i % 2, 0:wide[i]], ACT.Copy).then_inc(copied, 1)

                    for i in range(n_items + 1):
                        if i < n_items:
                            exponents(i)
                        if i >= 1:
                            copy(i - 1)

    def nsa_items(self, proj, rot, k_cmp, v_cmp, vals, gates):
        items = []
        for qt in range(TT):
            cols = slice(qt * P, (qt + 1) * P)
            for j in range(NSA_PAIRS):
                for g in range(2):
                    rows = slice(64 * g, 64 * g + 64)
                    h = 3 * (4 * g + j)
                    gate = [gates[:, qt, h + b:h + b + 1] for b in range(3)]
                    base = {"out": (64 * g, j, qt), "keep": None, "last": False, "first": False, "ends": False}
                    add = self.c("cmp_add")[:, qt * N_CMP:(qt + 1) * N_CMP]
                    items.append(base | {"q": proj[rows, NQ0 + j, cols], "k": k_cmp[rows, :], "v": [v_cmp[:, rows]],
                                         "mask": (0, add), "gate": gate[0], "keep": self.c("cmp_keep") if qt == 0 else None,
                                         "first": True})
                    for n, branch in enumerate((4, 5)):
                        v0 = 512 + 128 * n + 64 * g
                        items.append(base | {"q": rot[rows, j, cols], "k": rot[rows, branch, 0:(qt + 1) * P],
                                             "v": [vals[:, b, v0:v0 + 64] for b in range(qt + 1)],
                                             "mask": (qt * P, self.c("causal")), "gate": gate[1 + n],
                                             "ends": n == 1, "last": n == 1 and g == 1})
        return items

    def feed_forward(self, layer, sub, w_gu, w_dn):
        nc, t, xT, hT = self.nc, self.t, self.xT, self.hT
        m = 24 * sub
        gn = 24 * layer + 8 * sub
        self.norm(hT, self.v("g_norm", gn, gn + 8), scale=self.mod[:, m + 8:m + 16], shift=self.mod[:, m:m + 8])
        with self.stage("ffn"):
            wu, wd = self.sb("wu", [P, 2, KD, 2 * P]), self.sb("wd", [P, 2, D])
            hid, sg = self.sb("hid", [P, FT, S]), self.sb("sg", [P, 2, S])
            half = self.sb("half", [P, KD])
            ps = self.psum("ps", 8)
            wu_in, wd_in = [[self.sem(f"{n}_loaded{s}") for s in range(2)] for n in ("wu", "wd")]
            gate_ps, up_ps, gate_used, hid_done, down_done, half_done, out_done = self.sems(
                "gate_products up_products gate_used hidden_done down_done half_done out_done")
            with nc.Block() as block:
                @block.sync
                def _(sp):
                    def load_up(r, s):
                        sp.dma_start(wu[:, s], w_gu[bass.ds(2 * r + s, 1)].rearrange("a p k n -> (a p) k n"))\
                            .then_inc(wu_in[s], 16)

                    def load_up_again(r, s):
                        sp.wait_ge(up_ps, 2 * r + s - 1)
                        load_up(r, s)

                    def load_down(r, s):
                        sp.dma_start(wd[:, s], w_dn[bass.ds(2 * r + s, 1)].rearrange("a p n -> (a p) n"))\
                            .then_inc(wd_in[s], 16)

                    def load_down_again(r, s):
                        sp.wait_ge(down_done, 2 * r + s - 1)
                        load_down(r, s)
                    load_up(0, 0)
                    load_up(0, 1)
                    load_down(0, 0)
                    load_down(0, 1)
                    in_pairs(sp, FT, load_up_again, first=1)
                    in_pairs(sp, FT, load_down_again, first=1)

                @block.tensor
                def _(pe):
                    def up(r, s):
                        pe.wait_ge(wu_in[s], 16 * (r + 1))
                        pe.wait_ge(hid_done, 2 * r + s + 1)
                        for half_, sem in ((0, gate_ps), (1, up_ps)):
                            for k in range(KD):
                                mm = nc.tensor.matmul(ps[:, 2 * s + half_, :], wu[:, s, k, half_ * P:(half_ + 1) * P], hT[:, k, :],
                                                      start=k == 0, stop=k == KD - 1)
                            mm.then_inc(sem, 1)
                    in_pairs(pe, FT, up)

                    def down(r, s, first=False, last=False):
                        pe.wait_ge(wd_in[s], 16 * (r + 1))
                        for n in range(KD):
                            rhs = hid[:, bass.ds(2 * r + s, 1), :].rearrange("p a t -> p (a t)")
                            mm = nc.tensor.matmul(ps[:, n, :], wd[:, s, n * P:(n + 1) * P], rhs, start=first, stop=last)
                        mm.then_inc(down_done, 1)
                    pe.wait_ge(hid_done, FT + 2)
                    down(0, 0, first=True)
                    down(0, 1)
                    with pe.Fori(1, FT // 2 - 1) as r:
                        down(r, 0)
                        down(r, 1)
                    down(FT // 2 - 1, 0)
                    down(FT // 2 - 1, 1, last=True)

                @block.scalar
                def _(act):
                    def silu(r, s):
                        act.wait_ge(gate_ps, 2 * r + s + 1)
                        act.wait_ge(hid_done, 2 * r + s + 1)
                        nc.scalar.activation(sg[:, s, :], ps[:, 2 * s, :], ACT.Silu).then_inc(gate_used, 1)
                    in_pairs(act, FT, silu)

                @block.vector
                def _(dve):
                    dve.sem_inc(hid_done, 2)
                    nc.vector.tensor_scalar(half[:], self.mod[:, m + 16:m + 24], 0.5, None, ALU.mult).then_inc(half_done, 1)

                    def hidden(r, s):
                        dve.wait_ge(up_ps, 2 * r + s + 1)
                        dve.wait_ge(gate_used, 2 * r + s + 1)
                        nc.vector.tensor_tensor(hid[:, bass.ds(2 * r + s, 1), :].rearrange("p a t -> p (a t)"), sg[:, s, :],
                                                ps[:, 2 * s + 1, :], ALU.mult).then_inc(hid_done, 1)
                    in_pairs(dve, FT, hidden)
                    dve.wait_ge(down_done, FT)
                    dve.wait_ge(half_done, 1)
                    for n in range(KD):
                        nc.vector.scalar_tensor_tensor(out=xT[:, n, :], in0=ps[:, n, :], scalar=half[:, n:n + 1],
                                                       in1=xT[:, n, :], op0=ALU.mult, op1=ALU.add).then_inc(out_done, 1)

    def project_out(self, w, gate):
        nc, xT, hT = self.nc, self.xT, self.hT
        with self.stage("out"):
            wt = self.sb("wt", [P, 2, KD, 2 * P])
            ps = self.psum("ps", 8)
            loaded = [self.sem(f"loaded{s}") for s in range(2)]
            tile_done, added = self.sems("tile_done added")
            with nc.Block() as block:
                @block.sync
                def _(sp):
                    for g in range(KD // 2):
                        if g >= 2:
                            sp.wait_ge(tile_done, 2 * g - 2)
                        sp.dma_start(wt[:, g % 2], w[g]).then_inc(loaded[g % 2], 16)

                @block.tensor
                def _(pe):
                    for g in range(KD // 2):
                        pe.wait_ge(loaded[g % 2], 16 * (g // 2 + 1))
                        for u in range(2):
                            for k in range(KD):
                                mm = nc.tensor.matmul(ps[:, 2 * g + u, :], wt[:, g % 2, k, u * P:(u + 1) * P], hT[:, k, :],
                                                      start=k == 0, stop=k == KD - 1)
                            mm.then_inc(tile_done, 1)

                @block.vector
                def _(dve):
                    for n in range(KD):
                        dve.wait_ge(tile_done, n + 1)
                        nc.vector.scalar_tensor_tensor(out=xT[:, n, :], in0=ps[:, n, :], scalar=gate[:, n:n + 1],
                                                       in1=xT[:, n, :], op0=ALU.mult, op1=ALU.add).then_inc(added, 1)

    def first_mixer(self):
        nc, t = self.nc, self.t
        self.norm(self.hT, self.v("norm1_g"), scale=self.mod[:, 8:16], shift=self.mod[:, 0:8])
        with ExitStack() as ctx:
            tile = lambda name, shape: ctx.enter_context(nc.sbuf_tensor(name, shape, F32))
            proj, vals = tile("proj", [P, IN_TILES, S]), tile("vals", [P, TT, 768])
            gates, rot = tile("gates", [P, TT, 24]), tile("rot", [P, 6, S])
            k_cmp, v_cmp = tile("k_cmp", [P, N_CMP]), tile("v_cmp", [P, P])
            self.project(t["w_in"], IN_TILES // 2, proj)
            self.attention_gates(gates)
            self.turn_tiles(proj, [HI0, HI0 + 1, HI0 + 2, HI0 + 3, VS, VW], vals)
            self.rope(proj, rot)
            self.compress(proj, k_cmp, v_cmp)
            self.hgrn(proj, vals)
            self.attend(self.nsa_items(proj, rot, k_cmp, v_cmp, vals, gates), 4)
        self.project_out(t["w_out"], self.mod[:, 16:24])

    def second_mixer(self, layer):
        nc, t = self.nc, self.t
        self.norm(self.hT, self.v("g_norm", 24 * layer + 8, 24 * layer + 16), scale=self.mod[:, 32:40],
                  shift=self.mod[:, 24:32])
        with ExitStack() as ctx:
            tile = lambda name, shape: ctx.enter_context(nc.sbuf_tensor(f"{name}_{layer}", shape, F32))
            proj, vals, bias = tile("proj2", [P, IN_TILES_2, S]), tile("vals2", [P, TT, P]), tile("alibi", [P, 8, 2 * P])
            self.project(t["w_in_2"][layer], IN_TILES_2 // 2, proj)
            self.scale_queries(proj, bias)
            self.turn_tiles(proj, [AV], vals)
            self.attend(self.window_items(proj, vals, bias), 0,
                        sink=lambda i: self.v("sinks")[:, 8 * layer + i % 8:8 * layer + i % 8 + 1])
            self.recurrence(layer, proj)
        self.project_out(t["w_out_2"][layer], self.mod[:, 40:48])

    def scale_queries(self, proj, bias):
        nc = self.nc
        with self.stage("scale"):
            loaded = self.sem("loaded")
            with nc.Block() as block:
                @block.sync
                def _(sp):
                    sp.dma_start(bias[:], self.t["alibi"]).then_inc(loaded, 16)
                    sp.wait_ge(loaded, 16)

                @block.scalar
                def _(act):
                    nc.scalar.mul(proj[:, AQ0:AQ0 + 4, :], proj[:, AQ0:AQ0 + 4, :], 0.125)

    def window_items(self, proj, vals, bias):
        items = []
        for qt in range(TT):
            for j in range(4):
                for g in range(2):
                    rows = slice(64 * g, 64 * g + 64)
                    lo = max(qt - 1, 0)
                    skip = P if qt == 0 else 0
                    items.append({"q": proj[rows, AQ0 + j, qt * P:(qt + 1) * P], "k": proj[rows, AK, lo * P:(qt + 1) * P],
                                  "v": [vals[:, b, rows] for b in range(lo, qt + 1)],
                                  "mask": (0, bias[:, 2 * j + g, skip:]), "gate": None, "keep": None,
                                  "out": (64 * g, j, qt), "first": True, "ends": True, "last": g == 1})
        return items

    def recurrence(self, layer, proj):
        nc = self.nc
        with self.stage("lru"):
            wa, wx = self.sb("wa", [P, 2, P]), self.sb("wx", [P, 2, P])
            xc, r, i_, a, mult, u, th, pr, cv = (self.sb(x, [P, 2, S]) for x in "xc r i a mult u th pr cv".split())
            e, s2, z, pos = (self.sb(x, [P, 2]) for x in "e s2 z pos".split())
            poly = self.sb("poly", [P, 2])
            ps = self.psum("ps", 4)
            flat = lambda x: x[:].rearrange("p n t -> p (n t)")
            loaded, conv_done, gates_ps, chain_s, act_s, pool_s, abs_done, loga, tanh_done, mult_in, rooted, hid, gelu = self.sems(
                "loaded conv_done gate_products chain act_steps pool_steps abs_done log_a tanh_done mult_in rooted hidden gelu")
            w4 = lambda k, n: self.v("conv_w")[:, 8 * layer + 2 * k + n:8 * layer + 2 * k + n + 1]
            w3 = lambda k, n: self.v("sc_conv_w")[:, 6 * layer + 2 * k + n:6 * layer + 2 * k + n + 1]
            two = lambda name: self.v(name)[:, 2 * layer:2 * layer + 2]
            with nc.Block() as block:
                @block.sync
                def _(sp):
                    sp.dma_start(wa[:], self.t["gate_a"][layer]).then_inc(loaded, 16)
                    sp.dma_start(wx[:], self.t["gate_x"][layer]).then_inc(loaded, 16)

                @block.vector
                def _(dve):
                    chain = Chain(dve, chain_s)
                    for n in range(2):
                        x = proj[:, LX0 + n, :]
                        chain(nc.vector.tensor_scalar(xc[:, n, :], x, w4(3, n), two("conv_b")[:, n:n + 1], ALU.mult, ALU.add))
                        for k in range(3):
                            d = 3 - k
                            chain(nc.vector.scalar_tensor_tensor(out=xc[:, n, d:], in0=x[:, 0:S - d], scalar=w4(k, n),
                                                                 in1=xc[:, n, d:], op0=ALU.mult, op1=ALU.add))
                    dve.sem_inc(conv_done, 1)
                    lam = two("lam")
                    dve.wait_ge(abs_done, 1)
                    chain(nc.vector.tensor_scalar(z[:], e[:], 2.0, None, ALU.add))
                    chain(nc.vector.reciprocal(z[:], z[:]))
                    chain(nc.vector.tensor_tensor(z[:], z[:], e[:], ALU.mult))
                    chain(nc.vector.tensor_tensor(s2[:], z[:], z[:], ALU.mult))
                    chain(nc.vector.tensor_scalar(poly[:], s2[:], 2.0 / 17, 2.0 / 15, ALU.mult, ALU.add))
                    for k in (13, 11, 9, 7, 5, 3, 1):
                        chain(nc.vector.tensor_tensor(poly[:], poly[:], s2[:], ALU.mult))
                        chain(nc.vector.tensor_scalar(poly[:], poly[:], 2.0 / k, None, ALU.add))
                    chain(nc.vector.tensor_tensor(poly[:], poly[:], z[:], ALU.mult))
                    chain(nc.vector.tensor_scalar(pos[:], lam, -1.0, 0.0, ALU.mult, ALU.max))
                    chain(nc.vector.tensor_tensor(poly[:], poly[:], pos[:], ALU.add))
                    chain(nc.vector.tensor_scalar(poly[:], poly[:], -8.0, None, ALU.mult))
                    dve.wait_ge(act_s, 4)
                    for n in range(2):
                        nc.vector.tensor_scalar(r[:, n, :], r[:, n, :], poly[:, n:n + 1], None, ALU.mult).then_inc(loga, 1)
                    chain(nc.vector.tensor_tensor(flat(u), flat(i_), flat(xc), ALU.mult))
                    dve.wait_ge(tanh_done, 1)
                    chain(nc.vector.tensor_scalar(flat(mult), flat(th), -1.0, 1.0, ALU.mult, ALU.add))
                    chain(nc.vector.reciprocal(flat(mult), flat(mult)))
                    chain(nc.vector.scalar_tensor_tensor(out=flat(mult), in0=flat(th), scalar=-2.0, in1=flat(mult),
                                                         op0=ALU.mult, op1=ALU.mult))
                    nc.vector.tensor_scalar(flat(mult), flat(mult), 1e-30, None, ALU.max).then_inc(mult_in, 1)
                    dve.wait_ge(rooted, 1)
                    chain(nc.vector.memset(mult[:, :, 0:1], 1.0))
                    chain(nc.vector.tensor_tensor(flat(u), flat(u), flat(mult), ALU.mult))
                    for n in range(2):
                        nc.vector.tensor_tensor_scan(mult[:, n, :], a[:, n, :], u[:, n, :], 0.0, ALU.mult, ALU.add)\
                            .then_inc(hid, 1)
                    dve.wait_ge(hid, 2)
                    dve.wait_ge(gelu, 1)
                    nc.vector.tensor_tensor(self.hT[:, 4:6, :], mult[:], th[:], ALU.mult).then_inc(hid, 1)
                    dve.wait_ge(pool_s, 1)
                    for n in range(2):
                        chain(nc.vector.tensor_scalar(cv[:, n, :], pr[:, n, :], w3(2, n), None, ALU.mult))
                        for k in range(2):
                            d = 2 - k
                            chain(nc.vector.scalar_tensor_tensor(out=cv[:, n, d:], in0=pr[:, n, 0:S - d], scalar=w3(k, n),
                                                                 in1=cv[:, n, d:], op0=ALU.mult, op1=ALU.add))
                    nc.vector.tensor_tensor(self.hT[:, 6:8, :], cv[:], proj[:, SB0:SB0 + 2, :], ALU.mult).then_inc(hid, 1)

                @block.gpsimd
                def _(pool):
                    nc.gpsimd.tensor_tensor(pr[:], proj[:, SC0:SC0 + 2, :], proj[:, SX0:SX0 + 2, :], ALU.mult)\
                        .then_inc(pool_s, 1)

                @block.tensor
                def _(pe):
                    pe.wait_ge(loaded, 32)
                    pe.wait_ge(conv_done, 1)
                    for g, w in enumerate((wa, wx)):
                        for n in range(2):
                            nc.tensor.matmul(ps[:, 2 * g + n, :], w[:, n, :], xc[:, n, :], start=True, stop=True)\
                                .then_inc(gates_ps, 1)

                @block.scalar
                def _(act):
                    nc.scalar.activation(e[:], two("lam"), ACT.Abs).then_inc(act_s, 1)
                    act.wait_ge(act_s, 1)
                    nc.scalar.activation(e[:], e[:], ACT.Exp, scale=-1.0).then_inc(abs_done, 1)
                    for g, (out, name) in enumerate(((r, "gate_a_b"), (i_, "gate_x_b"))):
                        for n in range(2):
                            act.wait_ge(gates_ps, 2 * g + n + 1)
                            ins = nc.scalar.activation(out[:, n, :], ps[:, 2 * g + n, :], ACT.Sigmoid,
                                                       bias=two(name)[:, n:n + 1])
                            if g or n:
                                ins.then_inc(act_s, 1)
                    act.wait_ge(loga, 2)
                    nc.scalar.activation(flat(th), flat(r), ACT.Tanh).then_inc(tanh_done, 1)
                    nc.scalar.activation(flat(a), flat(r), ACT.Exp).then_inc(tanh_done, 1)
                    act.wait_ge(mult_in, 1)
                    nc.scalar.activation(flat(mult), flat(mult), ACT.Sqrt).then_inc(rooted, 1)
                    nc.scalar.activation(th[:], proj[:, LG0:LG0 + 2, :], ACT.Gelu_apprx_tanh).then_inc(gelu, 1)

    def store(self):
        nc = self.nc
        with self.stage("store"):
            stored = self.sem("stored")
            with nc.Block() as block:
                @block.sync
                def _(sp):
                    sp.dma_start(self.t["out"].rearrange("(n p) t -> p n t", p=P), self.hT[:]).then_inc(stored, 16)
                    sp.wait_ge(stored, 16)

    def moe(self):
        nc = self.nc
        self.norm(self.hT, self.v("norm2_g"), scale=self.mod[:, 32:40], shift=self.mod[:, 24:32])
        h_rows = nc.dram_tensor("h_rows", (S, D), F32).ap()
        y_rows = nc.dram_tensor("y_rows", (BLK * NBLK, D), F32).ap()
        with ExitStack() as ctx:
            tile = lambda name, shape, dt=F32: ctx.enter_context(nc.sbuf_tensor(name, shape, dt))
            dest, w8 = tile("dest", [P, TT, TOPK], U32), tile("w8", [P, TT, TOPK])
            row_tokens = tile("row_tokens", [P, NBLK], U32)
            block_expert = tile("block_expert", [1, P], I32)
            self.rows_out(h_rows)
            self.route(dest, w8, row_tokens, block_expert)
            self.experts(h_rows, y_rows, row_tokens, block_expert)
            self.shared_expert()
            self.combine(y_rows, dest, w8)

    def rows_out(self, h_rows):
        nc = self.nc
        with self.stage("rows"):
            rows = self.sb("rows", [P, TT, D])
            ps = self.psum("ps", 8)
            turned, copied, stored = self.sems("turned copied stored")
            with nc.Block() as block:
                @block.tensor
                def _(pe):
                    for c in range(TT):
                        for k in range(KD):
                            mm = nc.tensor.transpose(ps[:, 2 * c + k // 4, (k % 4) * P:(k % 4 + 1) * P],
                                                     self.hT[:, k, c * P:(c + 1) * P], self.c("ident"))
                        mm.then_inc(turned, 1)

                @block.scalar
                def _(act):
                    for c in range(TT):
                        act.wait_ge(turned, c + 1)
                        nc.scalar.activation(rows[:, c, :].rearrange("p (b n) -> p b n", b=2), ps[:, 2 * c:2 * c + 2, :], ACT.Copy)\
                            .then_inc(copied, 1)

                @block.sync
                def _(sp):
                    for c in range(TT):
                        sp.wait_ge(copied, c + 1)
                        sp.dma_start(h_rows[c * P:(c + 1) * P, :], rows[:, c, :]).then_inc(stored, 16)
                    sp.wait_ge(stored, 16 * TT)

    def route(self, dest, w8, row_tokens, block_expert):
        nc = self.nc
        M = TT * E
        table = nc.dram_tensor("row_table", (BLK * NBLK, 1), U32).ap()
        expert_column = nc.dram_tensor("expert_column", (1, P), I32).ap()
        with self.stage("route"):
            wr = self.sb("wr", [P, KD, E])
            score, choice, rep, picked, w, place, row = (self.sb(x, [P, TT, E]) for x in
                                                         "score choice rep picked w place row".split())
            top = self.sb("top", [P, TT * GROUPS, 8])
            gs, rank = self.sb("gs", [P, TT, GROUPS]), self.sb("rank", [P, TT, GROUPS])
            above, tie = self.sb("above", [P, TT, 8, 8]), self.sb("tie", [P, TT, 8, 8])
            v8, d8 = self.sb("v8", [P, TT, 8]), self.sb("d8", [P, TT, 8])
            tot = self.sb("tot", [P, TT])
            cnt, nb, incl, first = (self.sb(x, [P, E]) for x in "cnt nb incl first".split())
            junk, eb = self.sb("junk", [P, E]), self.sb("eb", [P, 1])
            ebi = self.sb("ebi", [P, 1], I32)
            zero, tok = self.sb("zero", [P, NBLK], U32), self.sb("tok", [P, TT], U32)
            ps = self.psum("ps", 3)
            loaded, logits, scored, chain_s, zeroed, picked_s, places, ready, table_zero, scattered, experts_out, back = self.sems(
                "loaded logits scored chain zeroed picked places ready table_zero scattered experts_out back")
            cut = lambda x: x[:].rearrange("p c e -> p (c e)")
            with nc.Block() as block:
                @block.sync
                def _(sp):
                    sp.dma_start(wr[:], self.t["router_w"]).then_inc(loaded, 16)
                    sp.wait_ge(zeroed, 1)
                    sp.dma_start(table.rearrange("(p b) a -> p (b a)", b=NBLK), zero[:]).then_inc(table_zero, 16)
                    sp.wait_ge(ready, 1)
                    sp.dma_start(expert_column.rearrange("a p -> p a"), ebi[:]).then_inc(experts_out, 16)
                    sp.wait_ge(experts_out, 16)
                    sp.dma_start(block_expert[:], expert_column).then_inc(back, 16)
                    sp.wait_ge(scattered, 16 * TT * TOPK)
                    sp.dma_start(row_tokens[:], table.rearrange("(p b) a -> p (b a)", b=NBLK)).then_inc(back, 16)
                    sp.wait_ge(back, 32)

                @block.tensor
                def _(pe):
                    pe.wait_ge(loaded, 16)
                    for c in range(TT):
                        for k in range(KD):
                            mm = nc.tensor.matmul(ps[:, 0, c * E:(c + 1) * E], self.hT[:, k, c * P:(c + 1) * P], wr[:, k, :],
                                                  start=k == 0, stop=k == KD - 1)
                    mm.then_inc(logits, 1)
                    pe.wait_ge(picked_s, 1)
                    for c in range(TT):
                        for a in range(c):
                            nc.tensor.matmul(ps[:, 1, c * E:(c + 1) * E], self.ones[:], picked[:, a, :], start=a == 0, stop=False)
                        nc.tensor.matmul(ps[:, 1, c * E:(c + 1) * E], self.c("before"), picked[:, c, :], start=c == 0, stop=True)
                    for a in range(TT):
                        mm = nc.tensor.matmul(ps[:, 2, 0:E], self.ones[:], picked[:, a, :], start=a == 0, stop=a == TT - 1)
                    mm.then_inc(places, 1)

                @block.scalar
                def _(act):
                    act.wait_ge(logits, 1)
                    nc.scalar.activation(cut(score), ps[:, 0, 0:M], ACT.Sigmoid).then_inc(scored, 1)

                @block.gpsimd
                def _(pool):
                    nc.gpsimd.memset(zero[:], 0).then_inc(zeroed, 1)
                    pool.wait_ge(table_zero, 16)
                    pool.wait_ge(ready, 1)
                    for c in range(TT):
                        for k in range(TOPK):
                            nc.gpsimd.indirect_dma_start(
                                out=table, out_offset=bass.IndirectOffsetOnAxis(ap=dest[:, c, k:k + 1], axis=0),
                                in_=tok[:, c:c + 1], in_offset=None).then_inc(scattered, 16)

                @block.vector
                def _(dve):
                    chain = Chain(dve, chain_s)
                    v = nc.vector
                    chain(v.tensor_copy(tok[:], self.c("tokens")))
                    dve.wait_ge(scored, 1)
                    bias = self.v("router_bias").unsqueeze(1).broadcast_to([P, TT, E])
                    chain(v.tensor_tensor(choice[:], score[:], bias, ALU.add))
                    for c in range(TT):
                        for g in range(GROUPS):
                            ins = v.max(top[:, c * GROUPS + g, :], choice[:, c, g * 8:(g + 1) * 8])
                    chain(ins)
                    chain(v.tensor_tensor(gs[:].rearrange("p c g -> p (c g)"), top[:, :, 0], top[:, :, 1], ALU.add))
                    other = gs[:].unsqueeze(2).broadcast_to([P, TT, GROUPS, GROUPS])
                    own = gs[:].unsqueeze(3).broadcast_to([P, TT, GROUPS, GROUPS])
                    lower = self.c("lower8").rearrange("p (a b) -> p a b", a=8).unsqueeze(1).broadcast_to([P, TT, 8, 8])
                    chain(v.tensor_tensor(above[:], other, own, ALU.is_gt))
                    chain(v.tensor_tensor(tie[:], other, own, ALU.is_equal))
                    chain(v.tensor_tensor(tie[:], tie[:], lower, ALU.mult))
                    chain(v.tensor_tensor(above[:], above[:], tie[:], ALU.add))
                    chain(v.tensor_reduce(rank[:], above[:], AX.X, ALU.add))
                    chain(v.tensor_scalar(rank[:], rank[:], float(TOPG), 1e30, ALU.is_lt, ALU.mult))
                    chain(v.tensor_scalar(rank[:], rank[:], -1e30, None, ALU.add))
                    cg = lambda x: x[:].rearrange("p c (g e) -> p (c g) e", g=GROUPS)
                    chain(v.tensor_tensor(cg(choice), cg(choice),
                                          rank[:].rearrange("p c g -> p (c g)").unsqueeze(2).broadcast_to([P, TT * GROUPS, 8]),
                                          ALU.add))
                    for c in range(TT):
                        ins = v.max(v8[:, c, :], choice[:, c, :])
                    chain(ins)
                    for c in range(TT):
                        ins = v.match_replace(rep[:, c, :], v8[:, c, :], choice[:, c, :], -3e38)
                    chain(ins)
                    chain(v.tensor_tensor(picked[:], rep[:], choice[:], ALU.not_equal))
                    dve.sem_inc(picked_s, 1)
                    chain(v.tensor_tensor(w[:], score[:], picked[:], ALU.mult))
                    chain(v.tensor_reduce(tot[:], w[:], AX.X, ALU.add))
                    chain(v.reciprocal(tot[:], tot[:]))
                    chain(v.scalar_tensor_tensor(out=w[:], in0=w[:], scalar=ROUTED_SCALE,
                                                 in1=tot[:].unsqueeze(2).broadcast_to([P, TT, E]), op0=ALU.mult, op1=ALU.mult))
                    dve.wait_ge(places, 1)
                    chain(v.tensor_copy(cnt[:], ps[:, 2, 0:E]))
                    chain(v.tensor_copy(cut(place), ps[:, 1, 0:M]))
                    chain(v.tensor_scalar(nb[:], cnt[:], 0.0, None, ALU.is_gt))
                    for j in range(1, S // BLK):
                        chain(v.scalar_tensor_tensor(out=nb[:], in0=cnt[:], scalar=float(j * BLK), in1=nb[:], op0=ALU.is_gt,
                                                     op1=ALU.add))
                    chain(v.tensor_tensor_scan(incl[:], self.ones[:, 0:E], nb[:], 0.0, ALU.mult, ALU.add))
                    chain(v.tensor_tensor(first[:], incl[:], nb[:], ALU.subtract))
                    chain(v.scalar_tensor_tensor(out=junk[:], in0=incl[:], scalar=self.c("iota"), in1=self.ones[:, 0:E],
                                                 op0=ALU.is_le, op1=ALU.mult, accum_out=eb[:]))
                    chain(v.tensor_scalar(ebi[:], eb[:], float(E - 1), None, ALU.min))
                    chain(v.tensor_scalar(cut(row), cut(place), float(BLK), None, ALU.is_ge))
                    for j in range(2, S // BLK):
                        chain(v.scalar_tensor_tensor(out=cut(row), in0=cut(place), scalar=float(j * BLK), in1=cut(row),
                                                     op0=ALU.is_ge, op1=ALU.add))
                    chain(v.tensor_scalar(cut(row), cut(row), float(1 - BLK * NBLK), 1.0, ALU.mult, ALU.add))
                    chain(v.scalar_tensor_tensor(out=cut(row), in0=cut(place), scalar=float(NBLK), in1=cut(row),
                                                 op0=ALU.mult, op1=ALU.add))
                    chain(v.tensor_tensor(row[:], row[:], first[:].unsqueeze(1).broadcast_to([P, TT, E]), ALU.add))
                    chain(v.tensor_tensor(row[:], row[:], picked[:], ALU.mult))
                    for c in range(TT):
                        ins = v.max(d8[:, c, :], row[:, c, :])
                    chain(ins)
                    chain(v.tensor_scalar(dest[:], d8[:], -1.0, None, ALU.add))
                    dve.sem_inc(ready, 1)
                    for c in range(TT):
                        for k in range(TOPK):
                            chain(v.scalar_tensor_tensor(out=junk[:], in0=row[:, c, :], scalar=d8[:, c, k:k + 1], in1=w[:, c, :],
                                                         op0=ALU.is_equal, op1=ALU.mult, accum_out=w8[:, c, k:k + 1]))

    def experts(self, h_rows, y_rows, row_tokens, block_expert):
        nc, t = self.nc, self.t
        R = NBLK // 2
        with self.stage("experts"):
            wg, wd = self.sb("wg", [P, 2, KD, 2 * EH]), self.sb("wd", [P, 2, 2, D])
            xg, xt = self.sb("xg", [P, 2, D]), self.sb("xt", [P, 2, D])
            idx0, idx1 = self.sb("idx0", [P, 1], U32), self.sb("idx1", [P, 1], U32)
            idx = [idx0, idx1]
            sg, hx, ht, y = self.sb("sg", [P, 2, EH]), self.sb("hx", [P, 2, EH]), self.sb("ht", [P, 2, EH]), self.sb("y", [P, 2, D])
            psX, psG, psH, psY = self.psum("x", 2), self.psum("g", 2), self.psum("h", 1), self.psum("y", 2)
            slot = lambda name: [self.sem(f"{name}{s}") for s in range(2)]
            wg_in, wd_in, gathered, stored = slot("wg_loaded"), slot("wd_loaded"), slot("gathered"), slot("stored")
            idx_ready, idx_seen, x_turned, x_copied, gu_done, silu_done, hid_done, h_turned, h_copied, y_done, y_low, y_high = self.sems(
                "idx_ready idx_seen x_turned x_copied gu_done silu_done hid_done h_turned h_copied y_done y_low y_high")
            out_rows = y_rows.rearrange("(p b) d -> p b d", b=NBLK)
            ident = self.c("ident")

            def pipelined(eng, front, back):
                front(0, 0)
                with eng.Fori(0, R - 1) as r:
                    front(r, 1)
                    back(r, 0)
                    front(r + 1, 0)
                    back(r, 1)
                front(R - 1, 1)
                back(R - 1, 0)
                back(R - 1, 1)

            with nc.Block() as block:
                @block.sync
                def _(sp):
                    def load(r, s, again=True):
                        n = 2 * r + s
                        e = sp.value_load(block_expert[0:1, bass.ds(n, 1)], min_val=0, max_val=E - 1)
                        if again:
                            sp.wait_ge(gu_done, n - 1)
                        sp.dma_start(wg[:, s], t["exp_gu"][bass.ds(e, 1)].rearrange("a p k n -> (a p) k n"))\
                            .then_inc(wg_in[s], 16)
                        if again:
                            sp.wait_ge(y_done, n - 1)
                        sp.dma_start(wd[:, s], t["exp_dn"][bass.ds(e, 1)].rearrange("a p k n -> (a p) k n"))\
                            .then_inc(wd_in[s], 16)
                    load(0, 0, again=False)
                    load(0, 1, again=False)
                    in_pairs(sp, NBLK, load, first=1)

                @block.gpsimd
                def _(pool):
                    def gather(r, s, again=True):
                        n = 2 * r + s
                        if again:
                            pool.wait_ge(x_turned, n - 1)
                        nc.gpsimd.tensor_copy(idx[s][:], row_tokens[:, bass.ds(n, 1)]).then_inc(idx_ready, 1)
                        pool.wait_ge(idx_ready, n + 1)
                        pool.sem_inc(idx_seen, 1)
                        nc.gpsimd.indirect_dma_start(out=xg[:, s, :], out_offset=None, in_=h_rows,
                                                     in_offset=bass.IndirectOffsetOnAxis(ap=idx[s][:, 0:1], axis=0))\
                            .then_inc(gathered[s], 16)
                    gather(0, 0, again=False)
                    gather(0, 1, again=False)
                    in_pairs(pool, NBLK, gather, first=1)

                @block.tensor
                def _(pe):
                    def front(r, s):
                        n = 2 * r + s
                        pe.wait_ge(gathered[s], 16 * (r + 1))
                        pe.wait_ge(x_copied, n + 1)
                        for k in range(KD):
                            mm = nc.tensor.transpose(psX[:, k // 4, (k % 4) * P:(k % 4 + 1) * P], xg[:, s, k * P:(k + 1) * P], ident)
                        mm.then_inc(x_turned, 1)
                        pe.wait_ge(x_copied, n + 2)
                        pe.wait_ge(wg_in[s], 16 * (r + 1))
                        for k in range(KD):
                            mm = nc.tensor.matmul(psG[:, s, :], xt[:, s, k * P:(k + 1) * P], wg[:, s, k, :], start=k == 0,
                                                  stop=k == KD - 1)
                        mm.then_inc(gu_done, 1)

                    def back(r, s):
                        n = 2 * r + s
                        pe.wait_ge(hid_done, n + 1)
                        for k in range(2):
                            mm = nc.tensor.transpose(psH[:, 0, k * P:(k + 1) * P], hx[:, s, k * P:(k + 1) * P], ident)
                        mm.then_inc(h_turned, 1)
                        pe.wait_ge(wd_in[s], 16 * (r + 1))
                        pe.wait_ge(h_copied, n + 1)
                        pe.wait_ge(y_low, n + 1)
                        pe.wait_ge(y_high, n + 1)
                        for half in range(2):
                            for k in range(2):
                                mm = nc.tensor.matmul(psY[:, half, :], ht[:, s, k * P:(k + 1) * P], wd[:, s, k, half * S:(half + 1) * S],
                                                      start=k == 0, stop=k == 1)
                        mm.then_inc(y_done, 1)
                    pipelined(pe, front, back)

                @block.scalar
                def _(act):
                    act.sem_inc(x_copied, 1)
                    act.sem_inc(y_high, 1)
                    for s in range(2):
                        act.sem_inc(stored[s], 16)

                    def front(r, s):
                        n = 2 * r + s
                        act.wait_ge(x_turned, n + 1)
                        nc.scalar.activation(xt[:, s, :].rearrange("p (b n) -> p b n", b=2), psX[:], ACT.Copy).then_inc(x_copied, 1)
                        act.wait_ge(gu_done, n + 1)
                        nc.scalar.activation(sg[:, s, :], psG[:, s, 0:EH], ACT.Silu).then_inc(silu_done, 1)

                    def back(r, s):
                        n = 2 * r + s
                        act.wait_ge(y_done, n + 1)
                        act.wait_ge(stored[s], 16 * (r + 1))
                        nc.scalar.activation(y[:, s, S:D], psY[:, 1, :], ACT.Copy).then_inc(y_high, 1)
                        act.wait_ge(y_high, n + 2)
                        act.wait_ge(y_low, n + 2)
                        act.dma_start(out_rows[:, bass.ds(n, 1), :].rearrange("p a d -> p (a d)"), y[:, s, :]).then_inc(stored[s], 16)
                    pipelined(act, front, back)
                    for s in range(2):
                        act.wait_ge(stored[s], 16 * (R + 1))

                @block.vector
                def _(dve):
                    dve.sem_inc(y_low, 1)

                    def front(r, s):
                        n = 2 * r + s
                        dve.wait_ge(silu_done, n + 1)
                        nc.vector.tensor_tensor(hx[:, s, :], sg[:, s, :], psG[:, s, EH:2 * EH], ALU.mult).then_inc(hid_done, 1)

                    def back(r, s):
                        n = 2 * r + s
                        dve.wait_ge(h_turned, n + 1)
                        nc.vector.tensor_copy(ht[:, s, :], psH[:, 0, 0:EH]).then_inc(h_copied, 1)
                        dve.wait_ge(y_done, n + 1)
                        dve.wait_ge(stored[s], 16 * (r + 1))
                        nc.vector.tensor_copy(y[:, s, 0:S], psY[:, 0, :]).then_inc(y_low, 1)
                    pipelined(dve, front, back)

    def shared_expert(self):
        nc, xT, hT, gate = self.nc, self.xT, self.hT, self.mod[:, 40:48]
        with self.stage("shared"):
            wg, wd = self.sb("wg", [P, KD, 2 * EH]), self.sb("wd", [P, 2, D])
            sg, hid = self.sb("sg", [P, 2, S]), self.sb("hid", [P, 2, S])
            ps = self.psum("ps", 8)
            loaded, up, silu, hidden, down, added = self.sems("loaded up_done silu_done hidden_done down_done added")
            with nc.Block() as block:
                @block.sync
                def _(sp):
                    sp.dma_start(wg[:], self.t["sh_gu"]).then_inc(loaded, 16)
                    sp.dma_start(wd[:], self.t["sh_dn"]).then_inc(loaded, 16)

                @block.tensor
                def _(pe):
                    pe.wait_ge(loaded, 32)
                    for i in (0, 2, 1, 3):
                        for k in range(KD):
                            mm = nc.tensor.matmul(ps[:, i, :], wg[:, k, i * P:(i + 1) * P], hT[:, k, :], start=k == 0, stop=k == KD - 1)
                        mm.then_inc(up, 1)
                    pe.wait_ge(hidden, 2)
                    for n in (4, 5, 6, 7, 0, 1, 2, 3):
                        for k in range(2):
                            mm = nc.tensor.matmul(ps[:, n, :], wd[:, k, n * P:(n + 1) * P], hid[:, k, :], start=k == 0, stop=k == 1)
                        mm.then_inc(down, 1)

                @block.scalar
                def _(act):
                    for i in range(2):
                        act.wait_ge(up, 2 * i + 1)
                        nc.scalar.activation(sg[:, i, :], ps[:, i, :], ACT.Silu).then_inc(silu, 1)

                @block.vector
                def _(dve):
                    for i in range(2):
                        dve.wait_ge(up, 2 * i + 2)
                        dve.wait_ge(silu, i + 1)
                        nc.vector.tensor_tensor(hid[:, i, :], sg[:, i, :], ps[:, 2 + i, :], ALU.mult).then_inc(hidden, 1)
                    for i, n in enumerate((4, 5, 6, 7, 0, 1, 2, 3)):
                        dve.wait_ge(down, i + 1)
                        nc.vector.scalar_tensor_tensor(out=xT[:, n, :], in0=ps[:, n, :], scalar=gate[:, n:n + 1],
                                                       in1=xT[:, n, :], op0=ALU.mult, op1=ALU.add).then_inc(added, 1)

    def combine(self, y_rows, dest, w8):
        nc, xT, gate = self.nc, self.xT, self.mod[:, 40:48]
        SLOTS = 4
        with self.stage("combine"):
            g, acc = self.sb("g", [P, SLOTS, D]), self.sb("acc", [P, 2, D])
            ps = self.psum("ps", 4)
            gathered = [self.sem(f"gathered{s}") for s in range(SLOTS)]
            summed, turned, added = self.sems("summed turned added")
            with nc.Block() as block:
                @block.gpsimd
                def _(pool):
                    for i in range(TT * TOPK):
                        if i >= SLOTS:
                            pool.wait_ge(summed, i - SLOTS + 1)
                        nc.gpsimd.indirect_dma_start(
                            out=g[:, i % SLOTS, :], out_offset=None, in_=y_rows,
                            in_offset=bass.IndirectOffsetOnAxis(ap=dest[:, i // TOPK, i % TOPK:i % TOPK + 1], axis=0))\
                            .then_inc(gathered[i % SLOTS], 16)

                @block.vector
                def _(dve):
                    def into_x(c):
                        dve.wait_ge(turned, c + 1)
                        for n in range(KD):
                            o = xT[:, n, c * P:(c + 1) * P]
                            nc.vector.scalar_tensor_tensor(out=o, in0=ps[:, 2 * (c % 2) + n // 4, (n % 4) * P:(n % 4 + 1) * P],
                                                           scalar=gate[:, n:n + 1], in1=o, op0=ALU.mult, op1=ALU.add)\
                                .then_inc(added, 1)
                    for c in range(TT):
                        a = acc[:, c % 2, :]
                        for k in range(TOPK):
                            i = c * TOPK + k
                            dve.wait_ge(gathered[i % SLOTS], 16 * (i // SLOTS + 1))
                            if k == 0:
                                nc.vector.tensor_scalar(a, g[:, i % SLOTS, :], w8[:, c, 0:1], None, ALU.mult).then_inc(summed, 1)
                            else:
                                dve.wait_ge(summed, i)
                                nc.vector.scalar_tensor_tensor(out=a, in0=g[:, i % SLOTS, :], scalar=w8[:, c, k:k + 1], in1=a,
                                                               op0=ALU.mult, op1=ALU.add).then_inc(summed, 1)
                        if c:
                            into_x(c - 1)
                    into_x(TT - 1)

                @block.tensor
                def _(pe):
                    for c in range(TT):
                        pe.wait_ge(summed, TOPK * (c + 1))
                        if c >= 2:
                            pe.wait_ge(added, KD * (c - 1))
                        for n in range(KD):
                            mm = nc.tensor.transpose(ps[:, 2 * (c % 2) + n // 4, (n % 4) * P:(n % 4 + 1) * P],
                                                     acc[:, c % 2, n * P:(n + 1) * P], self.c("ident"))
                        mm.then_inc(turned, 1)


def vec_cols(x):
    x = np.asarray(x)
    return np.ascontiguousarray(x.reshape(-1, P).T)


def pair_groups(w):
    k, n = w.shape
    return np.ascontiguousarray(w.reshape(k // P, P, n // 256, 256).transpose(2, 1, 0, 3))


def constants():
    f = np.float32
    a = np.zeros((P, NCON), f)

    def put(name, x):
        lo, hi = CON[name]
        a[:, lo:hi] = x
    p = np.arange(P)
    put("ident", np.eye(P))
    put("before", p[:, None] < p[None, :])
    rot = np.zeros((P, P))
    for m in range(P):
        if m % 64 < 32:
            rot[m + 32, m] = -1.0
        else:
            rot[m - 32, m] = 1.0
    put("rot", rot)
    inv = (f(10000.0) ** (-np.arange(32, dtype=f) / f(32))).astype(f)
    ang = np.arange(S, dtype=f)[None, :] * inv[p % 32][:, None]
    put("cos", np.cos(ang))
    put("sin", np.sin(ang))
    levels = np.zeros((P, 8, P))
    for i in range(7):
        m = 64 >> i
        s, t = p[:, None], p[None, :]
        levels[:, i] = (s // (2 * m) == t // (2 * m)) & (s % (2 * m) < m) & (t % (2 * m) >= m)
    levels[:, 7] = np.eye(P)
    put("levels", levels.reshape(P, -1))
    put("causal", np.where(p[None, :] <= p[:, None], 0.0, NEG))
    tok = np.arange(TT)[None, :, None] * P + p[:, None, None]
    seen = np.arange(N_CMP)[None, None, :] * CMP_STRIDE + CMP_BLOCK - 1 <= tok
    put("cmp_add", np.where(seen, 0.0, NEG).reshape(P, -1))
    put("cmp_keep", seen[:, 0])
    g = np.arange(8)
    put("lower8", np.broadcast_to((g[None, :] < g[:, None]).reshape(1, 64), (P, 64)))
    put("iota", p[:, None])
    put("tokens", tok[:, :, 0])
    return a


def alibi():
    slopes = (2.0 ** (-8.0 * np.arange(1, 9) / 8)).astype(np.float32)
    dist = np.arange(P)[:, None] + P - np.arange(2 * P)[None, :]
    out = np.empty((P, 8, 2 * P), np.float32)
    for i in range(8):
        h = (i % 2) * 4 + i // 2
        out[:, i] = np.where((dist >= 0) & (dist < P), -slopes[h] * dist.astype(np.float32), np.float32(NEG))
    return out


PAIRED = np.concatenate([np.arange(64) + 64 * (4 * g + j) for j in range(4) for g in range(2)])


def layout(i):
    i = {k: np.asarray(v) for k, v in i.items()}
    w = i["w_in"][0]
    at = np.cumsum([0, 512, 512, 512, 512, 512, 128, 128, 128, 128, 128, 128, 24])
    hq, hf, hi, hgt, nq, kc, vc, ks, vs, kw, vw, ng = (w[:, at[n]:at[n + 1]] for n in range(12))
    fm = np.concatenate([hq, hf, hgt, nq[:, PAIRED], kc, vc, ks, kw, hi, vs, vw], axis=1)
    a = {"xT": np.ascontiguousarray(i["x"][0].T), "w_ada": i["w_ada"][0], "w_in": pair_groups(fm),
         "w_gates": np.ascontiguousarray(ng.reshape(KD, P, 24).transpose(1, 0, 2))}
    wo = i["w_out"][0]
    a["w_out"] = pair_groups(np.concatenate([wo[:512], wo[512:][PAIRED]]))
    for x in "kv":
        w1 = i[f"cmp_w1_{x}"][0].reshape(2, 16, 64, 256)
        a[f"w1_{x}"] = np.ascontiguousarray(w1.transpose(0, 2, 1, 3).reshape(P, 16, 256))
        a[f"w2_{x}"] = np.ascontiguousarray(i[f"cmp_w2_{x}"][0].reshape(2, P, 64).transpose(1, 0, 2))
        a[f"pos_{x}"] = np.ascontiguousarray(i[f"cmp_pos_{x}"][0].reshape(2, 16, 64).transpose(0, 2, 1).reshape(P, 16))
    a["router_w"] = np.ascontiguousarray(i["router_w"][0].reshape(KD, P, E).transpose(1, 0, 2))
    a["exp_gu"] = np.ascontiguousarray(i["w_exp_gu"][0].reshape(E, KD, P, 2 * EH).transpose(0, 2, 1, 3))
    a["exp_dn"] = np.ascontiguousarray(i["w_exp_dn"][0].reshape(E, 2, P, D).transpose(0, 2, 1, 3))
    a["sh_gu"] = np.ascontiguousarray(i["w_sh_gu"][0].reshape(KD, P, 2 * EH).transpose(1, 0, 2))
    a["sh_dn"] = np.ascontiguousarray(i["w_sh_dn"][0].reshape(2, P, D).transpose(1, 0, 2))
    a["w_mod"] = i["w_mod_2"]
    for n in (1, 2):
        gu = i[f"w_ffn{n}_gu_2"].reshape(2, KD, P, 2, FT, P)
        a[f"ffn{n}_gu"] = np.ascontiguousarray(gu.transpose(0, 4, 2, 1, 3, 5).reshape(2, FT, P, KD, 2 * P))
        a[f"ffn{n}_dn"] = np.ascontiguousarray(i[f"w_ffn{n}_down_2"].reshape(2, FT, P, D))
    at = np.cumsum([0, 512, 128, 128, 256, 256, 256, 256, 256])
    a["w_in_2"] = np.stack([pair_groups(np.concatenate([x[:, :512][:, PAIRED], x[:, 512:]], axis=1)) for x in i["w_in_2"]])
    a["w_out_2"] = np.stack([pair_groups(np.concatenate([x[:512][PAIRED], x[512:]])) for x in i["w_out_2"]])
    for x in "ax":
        g = i[f"lru_gate_{x}_w_2"]
        b = np.zeros((2, P, 2, P), g.dtype)
        for h in range(4):
            r = slice(64 * (h % 2), 64 * (h % 2) + 64)
            b[:, r, h // 2, r] = g[:, h]
        a[f"gate_{x}"] = b
    vecs = {
        "c": i["c"][0], "b_ada": i["b_ada"][0], "norm1_g": i["norm1_g"][0], "lb0": i["hg_lb_logits"][0],
        "lb1": i["hg_lb_logits"][1], "hg_norm_g": i["hg_norm_g"][0], "b1_k": i["cmp_b1_k"][0], "b1_v": i["cmp_b1_v"][0],
        "norm2_g": i["norm2_g"][0], "final_g": i["final_g"], "c_2": i["c_2"][0], "b_mod0": i["b_mod_2"][0],
        "b_mod1": i["b_mod_2"][1], "g_norm": i["g_norm_2"], "conv_w": i["lru_conv_w_2"], "conv_b": i["lru_conv_b_2"],
        "gate_a_b": i["lru_gate_a_b_2"], "gate_x_b": i["lru_gate_x_b_2"], "lam": i["lru_lambda_2"],
        "sc_conv_w": i["sc_conv_w_2"], "g_final": i["g_final_2"],
    }
    cols = [vec_cols(vecs[name]) for name, _ in VEC_COLS[:-2]]
    order = [4 * (n % 2) + n // 2 for n in range(8)]
    for row in (i["router_bias"][0], i["attn_sinks_2"][:, order].reshape(-1)):
        cols.append(np.broadcast_to(row[None, :], (P, row.size)))
    a["vecs"] = np.ascontiguousarray(np.concatenate(cols, axis=1))
    a["consts"] = constants()
    a["alibi"] = alibi()
    return a


def build(nc, t, stop=None):
    k = Kernel(nc, t)
    k.setup()
    k.modulation(t["w_ada"], k.v("c"), k.v("b_ada"), 48)
    k.first_mixer()
    if stop:
        return k
    k.moe()
    k.norm(k.xT, k.v("final_g"))
    for layer in range(2):
        k.modulation(t["w_mod"][layer], k.v("c_2"), k.v(f"b_mod{layer}"), 72)
        k.feed_forward(layer, 0, t["ffn1_gu"][layer], t["ffn1_dn"][layer])
        k.second_mixer(layer)
        k.feed_forward(layer, 2, t["ffn2_gu"][layer], t["ffn2_dn"][layer])
    k.norm(k.hT, k.v("g_final"))
    k.store()
    return k


def kernel(**inputs):
    import concourse.bacc as bacc
    from concourse.bass_utils import run_bass_kernel_spmd

    nc = bacc.Bacc("TRN2", target_bir_lowering=False, num_devices=1)
    arrays = layout(inputs)
    t = {name: nc.dram_tensor("in_" + name, a.shape, mybir.dt.from_np(a.dtype), kind="ExternalInput").ap()
         for name, a in arrays.items()}
    t["out"] = nc.dram_tensor("out", (D, S), F32, kind="ExternalOutput").ap()
    build(nc, t)
    result = run_bass_kernel_spmd(nc, [{"in_" + name: a for name, a in arrays.items()}], core_ids=[0])
    return np.ascontiguousarray(result.results[0]["out"].T)[None]
```

```python
from contextlib import ExitStack, contextmanager

import numpy as np

import concourse.bass as bass
from concourse import mybir

F32 = mybir.dt.float32
F32R = mybir.dt.float32r
I32 = mybir.dt.int32
U32 = mybir.dt.uint32
ACT = mybir.ActivationFunctionType
ALU = mybir.AluOpType
AX = mybir.AxisListType

P = 128
S = 512
D = 1024
KD = D // P
TT = S // P
EPS = 1e-6
HEADS = 4
NSA_PAIRS = 4
N_CMP, CMP_STRIDE, CMP_BLOCK = 31, 16, 32
E, TOPK, GROUPS, TOPG = 64, 8, 8, 4
EH = 256
BLK = 128
NBLK = S * TOPK // BLK + E
ROUTED_SCALE = 2.5
FT = 22
NEG = -1e30
LN_FLOOR = 2.0 ** -63

Q0, F0, G0, NQ0, KC, VC, KS, KW, HI0, VS, VW = 0, 4, 8, 12, 16, 17, 18, 19, 20, 24, 25
IN_TILES = 26
AQ0, AK, AV, LX0, LG0, SB0, SC0, SX0 = 0, 4, 5, 6, 8, 10, 12, 14
IN_TILES_2 = 16

VEC_COLS = [
    ("c", 8), ("b_ada", 48), ("norm1_g", 8), ("lb0", 4), ("lb1", 4), ("hg_norm_g", 4), ("b1_k", 2), ("b1_v", 2),
    ("norm2_g", 8), ("final_g", 8), ("c_2", 8), ("b_mod0", 72), ("b_mod1", 72), ("g_norm", 48), ("conv_w", 16),
    ("conv_b", 4), ("gate_a_b", 4), ("gate_x_b", 4), ("lam", 4), ("sc_conv_w", 12), ("g_final", 8),
    ("router_bias", 64), ("sinks", 16),
]
CONST_COLS = [
    ("ident", 128), ("before", 128), ("rot", 128), ("cos", 512), ("sin", 512), ("levels", 8 * 128), ("causal", 128),
    ("cmp_add", 4 * 31), ("cmp_keep", 31), ("lower8", 64), ("iota", 1), ("tokens", 4), ("pairs", NBLK // 2),
]


def offsets(cols):
    out, at = {}, 0
    for name, n in cols:
        out[name] = (at, at + n)
        at += n
    return out, at


VEC, NVEC = offsets(VEC_COLS)
CON, NCON = offsets(CONST_COLS)


class Chain:

    def __init__(self, eng, sem, base=0):
        self.eng, self.sem, self.base, self.n = eng, sem, base, 0

    def __call__(self, ins):
        self.n += 1
        ins.then_inc(self.sem, 1)
        self.eng.wait_ge(self.sem, self.base + self.n)


def in_pairs(eng, n, body, first=0):
    if n // 2 > first:
        with eng.Fori(first, n // 2) as r:
            body(r, 0)
            body(r, 1)
    if n % 2:
        body(n // 2, 0)


class Modulation:
    CHUNK = 1024

    def __init__(self, k, w, c, b, out, ps, wk=None, slots=2):
        self.nc, self.w, self.c, self.b, self.out, self.ps, self.ones = k.nc, w, c, b, out, ps, k.ones
        self.slots = slots
        self.wk = k.sb("mod_rows", [P, slots, self.CHUNK])[:] if wk is None else wk
        self.acc, self.ca = k.sb("mod_sum", [P, self.CHUNK]), k.sb("mod_c", [P, KD])
        self.loaded = [k.sem(f"mod_loaded{s}") for s in range(slots)]
        self.c_ready, self.summed, self.turned = k.sems("mod_c_ready mod_rows_summed mod_turned")

    def start(self, act):
        self.nc.scalar.activation(self.ca[:], self.c, ACT.Silu).then_inc(self.c_ready, 1)

    def free(self, dve):
        dve.sem_inc(self.summed, self.slots)
        dve.wait_ge(self.c_ready, 1)

    def load(self, dma, g, pieces):
        for i in pieces:
            dma.wait_ge(self.summed, KD * g + i + 1)
            dma.dma_start(self.wk[:, i % self.slots, :], self.w[i * P:(i + 1) * P, bass.ds(self.CHUNK * g, self.CHUNK)])\
                .then_inc(self.loaded[i % self.slots], 16)

    def multiply(self, dve, g, pieces):
        nc, acc, ca, n = self.nc, self.acc, self.ca, self.slots
        for i in pieces:
            dve.wait_ge(self.loaded[i % n], 16 * (KD // n * g + i // n + 1))
            if i == 0:
                nc.vector.tensor_scalar(acc[:], self.wk[:, 0, :], ca[:, 0:1], None, ALU.mult).then_inc(self.summed, 1)
            else:
                dve.wait_ge(self.summed, KD * g + i + n)
                nc.vector.scalar_tensor_tensor(out=acc[:], in0=self.wk[:, i % n, :], scalar=ca[:, i:i + 1], in1=acc[:],
                                               op0=ALU.mult, op1=ALU.add).then_inc(self.summed, 1)

    def reduce(self, pe, g):
        pe.wait_ge(self.summed, KD * g + KD + self.slots)
        for i in range(self.CHUNK // P):
            mm = self.nc.tensor.matmul(self.ps[:, i:i + 1], self.acc[:, i * P:(i + 1) * P], self.ones[:, 0:1], start=True, stop=True)
        mm.then_inc(self.turned, 1)

    def finish(self, dve, g):
        n = self.CHUNK // P
        dve.wait_ge(self.turned, g + 1)
        self.nc.vector.tensor_tensor(self.out[:, bass.ds(n * g, n)], self.ps[:, 0:n], self.b[:, bass.ds(n * g, n)], ALU.add)


class Kernel:
    def __init__(self, nc, t):
        self.nc, self.t = nc, t
        sb = nc.alloc_sbuf_tensor
        self.xT = sb("xT", [P, KD, S], F32)
        self.vec = sb("vec", [P, NVEC], F32)
        self.con = sb("con", [P, NCON], F32)
        self.ones = sb("ones", [P, P], F32)
        self.eps = sb("eps", [P, 1], F32)
        self.mods = sb("mod", [P, 72], F32), sb("mod_next", [P, 72], F32)
        self.mod = self.mods[0]
        self.pre = sb("pre", [P, KD], F32)

        self.stages = 0
        self.h_rows = nc.dram_tensor("h_rows", (S, D), F32).ap()
        self.y_rows = nc.dram_tensor("y_rows", (BLK * NBLK, D), F32).ap()

    @contextmanager
    def stage(self, name):
        self.stages += 1
        self.tag = f"{name}{self.stages}_"
        with self.nc.cleanup_on_exit():
            yield

    def sem(self, name):
        return self.nc.alloc_semaphore(self.tag + name)

    def sems(self, names):
        return [self.sem(n) for n in names.split()]

    def sb(self, name, shape, dt=F32):
        return self.nc.alloc_sbuf_tensor(self.tag + name, shape, dt)

    def psum(self, name, banks):
        return self.nc.alloc_psum_tensor(self.tag + name + "_psum", [P, banks, S], F32)

    def v(self, name, a=0, b=None):
        lo, hi = VEC[name]
        return self.vec[:, lo + a:(hi if b is None else lo + b)]

    def c(self, name):
        lo, hi = CON[name]
        return self.con[:, lo:hi]

    def setup(self):
        nc, t = self.nc, self.t
        with self.stage("load"):
            loaded = self.sem("loaded")
            with nc.Block() as block:
                @block.sync
                def _(sp):
                    sp.dma_start(self.vec[:], t["vecs"]).then_inc(loaded, 16)
                    sp.dma_start(self.con[:], t["consts"]).then_inc(loaded, 16)
                    sp.dma_start(self.xT[:], t["xT"].rearrange("(n p) t -> p n t", p=P)).then_inc(loaded, 16)
                    sp.wait_ge(loaded, 48)

                @block.gpsimd
                def _(pool):
                    nc.gpsimd.memset(self.ones[:], 1.0)
                    nc.gpsimd.memset(self.eps[:], EPS)

    def modulation(self, w, c, b, tiles):
        nc = self.nc
        n = tiles * P
        with self.stage("mod"):
            wk = self.sb("wk", [P, 2, n])
            acc = self.sb("acc", [P, n])
            ca = self.sb("ca", [P, KD])
            ps = self.psum("ps", 1)[:, 0, :]
            loaded = [self.sem(f"loaded{s}") for s in range(2)]
            act_done, summed, turned = self.sems("c_ready rows_summed turned")
            with nc.Block() as block:
                @block.sync
                def _(sp):
                    for k in range(KD):
                        if k >= 2:
                            sp.wait_ge(summed, k - 1)
                        sp.dma_start(wk[:, k % 2, :], w[k * P:(k + 1) * P, :]).then_inc(loaded[k % 2], 16)

                @block.scalar
                def _(act):
                    nc.scalar.activation(ca[:], c, ACT.Silu).then_inc(act_done, 1)

                @block.vector
                def _(dve):
                    dve.wait_ge(act_done, 1)
                    for k in range(KD):
                        dve.wait_ge(loaded[k % 2], 16 * (k // 2 + 1))
                        if k == 0:
                            nc.vector.tensor_scalar(acc[:], wk[:, 0, :], ca[:, 0:1], None, ALU.mult).then_inc(summed, 1)
                        else:
                            dve.wait_ge(summed, k)
                            nc.vector.scalar_tensor_tensor(out=acc[:], in0=wk[:, k % 2, :], scalar=ca[:, k:k + 1],
                                                           in1=acc[:], op0=ALU.mult, op1=ALU.add).then_inc(summed, 1)
                    dve.wait_ge(turned, 1)
                    nc.vector.tensor_tensor(self.mod[:, 0:tiles], ps[:, 0:tiles], b, ALU.add)

                @block.tensor
                def _(pe):
                    pe.wait_ge(summed, KD)
                    for i in range(tiles):
                        last = nc.tensor.matmul(ps[:, i:i + 1], acc[:, i * P:(i + 1) * P], self.ones[:, 0:1],
                                                start=True, stop=True)
                    last.then_inc(turned, 1)

    def norm(self, dst, g, scale=None, shift=None, parts=None):
        nc, xT = self.nc, self.xT
        with self.stage("norm"):
            sq = self.sb("sq", [P, 2, S])
            rstd = self.sb("rstd", [P, S])
            xn = self.sb("xn", [P, 2, S])
            if dst is None:
                h = self.sb("h", [P, 2, S])
                whole = lambda k: h[:, k % 2, :]
            else:
                whole = lambda k: dst[:, k, :]
            ps = self.psum("ps", 1)[:, 0, :]
            squared, summed, rooted, inverted, pre_done, xn_ready, done, high_done, low_done = self.sems(
                "squared summed rooted inverted pre_done xn_ready done high_done low_done")
            with nc.Block() as block:
                @block.scalar
                def _(act):
                    for k in range(KD):
                        if k >= 2:
                            act.wait_ge(summed, k - 1)
                        nc.scalar.activation(sq[:, k % 2, :], xT[:, k, :], ACT.Square).then_inc(squared, 1)
                    act.wait_ge(summed, KD)
                    nc.scalar.activation(rstd[:], ps, ACT.Sqrt, bias=self.eps[:, 0:1], scale=1.0 / D).then_inc(rooted, 1)
                    act.wait_ge(pre_done, 1)
                    for k in range(KD):
                        act.wait_ge(xn_ready, k + 1)
                        if dst is None and k >= 2:
                            act.wait_ge(low_done, k - 1)
                        if shift is None:
                            nc.scalar.activation(whole(k), xn[:, k % 2, :], ACT.Copy, scale=self.pre[:, k:k + 1])\
                                .then_inc(done, 1)
                        else:
                            nc.scalar.activation(whole(k), xn[:, k % 2, :], ACT.Identity, bias=shift[:, k:k + 1],
                                                 scale=self.pre[:, k:k + 1]).then_inc(done, 1)

                @block.tensor
                def _(pe):
                    for k in range(KD):
                        pe.wait_ge(squared, k + 1)
                        nc.tensor.matmul(ps, self.ones[:], sq[:, k % 2, :], start=k == 0, stop=k == KD - 1).then_inc(summed, 1)

                if parts:
                    @block.gpsimd
                    def _(pool):
                        for k in range(KD):
                            pool.wait_ge(done, k + 1)
                            nc.gpsimd.tensor_copy(parts[0][:, k, :], whole(k)).then_inc(high_done, 1)

                @block.vector
                def _(dve):
                    def low(k):
                        dve.wait_ge(high_done, k + 1)
                        nc.vector.tensor_tensor(parts[1][:, k, :], whole(k), parts[0][:, k, :].bitcast(F32), ALU.subtract)\
                            .then_inc(low_done, 1)
                    if scale is None:
                        nc.vector.tensor_copy(self.pre[:], g).then_inc(pre_done, 1)
                    else:
                        nc.vector.scalar_tensor_tensor(out=self.pre[:], in0=scale, scalar=1.0, in1=g, op0=ALU.add,
                                                       op1=ALU.mult).then_inc(pre_done, 1)
                    dve.wait_ge(rooted, 1)
                    nc.vector.reciprocal(rstd[:], rstd[:]).then_inc(inverted, 1)
                    dve.wait_ge(inverted, 1)
                    for k in range(KD):
                        if k >= 2:
                            dve.wait_ge(done, k - 1)
                        nc.vector.tensor_tensor(xn[:, k % 2, :], xT[:, k, :], rstd[:], ALU.mult).then_inc(xn_ready, 1)
                        if parts and k:
                            low(k - 1)
                    if parts:
                        low(KD - 1)

    @contextmanager
    def parts(self, name):
        with self.nc.sbuf_tensor(f"h_high_{name}", [P, KD, S], F32R) as high, \
                self.nc.sbuf_tensor(f"h_low_{name}", [P, KD, S], F32R) as low:
            yield high, low

    def mm3(self, out, w, x, start, stop):
        mm = self.nc.tensor.matmul
        mm(out, w[0], x[0], start=start, stop=False)
        mm(out, w[0], x[1], start=False, stop=False)
        return mm(out, w[1], x[0], start=False, stop=stop)

    def project(self, w, pairs, h, out, beside=None):
        nc = self.nc
        with self.stage("proj"):
            wt, high, low = (self.sb(n, [P, 2, KD, 2 * P], dt) for n, dt in (("wt", F32), ("high", F32R), ("low", F32R)))
            ps = self.psum("ps", 5)
            rounds = 0
            if beside:
                rounds, mod = beside[-1], Modulation(self, *beside[:-1], ps[:, 4, :])
            loaded = [self.sem(f"loaded{s}") for s in range(2)]
            high_done, low_done, tile_done, bank_free = self.sems("high_done low_done tile_done bank_free")
            with nc.Block() as block:
                @block.sync
                def _(sp):
                    def load(r, s):
                        sp.dma_start(wt[:, s], w[bass.ds(2 * r + s, 1)].rearrange("a p k n -> (a p) k n"))\
                            .then_inc(loaded[s], 16)

                    def load_again(r, s):
                        sp.wait_ge(low_done, 2 * r + s - 1)
                        load(r, s)
                    load(0, 0)
                    load(0, 1)
                    if beside:
                        with sp.Fori(0, rounds) as r:
                            mod.load(sp, r, (0, 1))
                            load_again(r + 1, 0)
                            mod.load(sp, r, (2, 3, 4, 5))
                            load_again(r + 1, 1)
                            mod.load(sp, r, (6, 7))
                    in_pairs(sp, pairs, load_again, first=1 + rounds)

                @block.vector
                def _(dve):
                    def split(r, s):
                        dve.wait_ge(high_done, 2 * r + s + 1)
                        nc.vector.tensor_tensor(low[:, s], wt[:, s], high[:, s].bitcast(F32), ALU.subtract).then_inc(low_done, 1)
                    split(0, 0)
                    if beside:
                        mod.free(dve)
                        with dve.Fori(0, rounds) as r:
                            mod.multiply(dve, r, range(4))
                            split(r, 1)
                            mod.multiply(dve, r, range(4, 8))
                            split(r + 1, 0)
                            mod.finish(dve, r)
                    split(rounds, 1)
                    in_pairs(dve, pairs, split, first=rounds + 1)

                @block.tensor
                def _(pe):
                    pe.sem_inc(tile_done, 4)

                    def tiles(r, s):
                        pe.wait_ge(low_done, 2 * r + s + 1)
                        for u in range(2):
                            pe.wait_ge(bank_free, 4 * r + 2 * s + u + 1)
                            for k in range(KD):
                                c = slice(u * P, (u + 1) * P)
                                mm = self.mm3(ps[:, 2 * s + u, :], (high[:, s, k, c], low[:, s, k, c]), (h[0][:, k, :], h[1][:, k, :]),
                                              start=k == 0, stop=k == KD - 1)
                            mm.then_inc(tile_done, 1)
                    if beside:
                        with pe.Fori(0, rounds) as r:
                            tiles(r, 0)
                            tiles(r, 1)
                            mod.reduce(pe, r)
                    in_pairs(pe, pairs, tiles, first=rounds)

                @block.scalar
                def _(act):
                    act.sem_inc(bank_free, 4)
                    if beside:
                        mod.start(act)

                    def split(r, s):
                        act.wait_ge(loaded[s], 16 * (r + 1))
                        act.wait_ge(tile_done, 4 * r + 2 * s + 2)
                        nc.scalar.activation(high[:, s], wt[:, s], ACT.Copy).then_inc(high_done, 1)

                    def evacuate(r, s):
                        for u in range(2):
                            act.wait_ge(tile_done, 4 * r + 2 * s + u + 5)
                            nc.scalar.activation(out[:, bass.ds(4 * r + 2 * s + u, 1), :].rearrange("p a t -> p (a t)"),
                                                 ps[:, 2 * s + u, :], ACT.Copy).then_inc(bank_free, 1)
                    split(0, 0)
                    with act.Fori(0, (pairs - 1) // 2) as r:
                        split(r, 1)
                        evacuate(r, 0)
                        split(r + 1, 0)
                        evacuate(r, 1)
                    r = (pairs - 1) // 2
                    if pairs % 2 == 0:
                        split(r, 1)
                    evacuate(r, 0)
                    if pairs % 2 == 0:
                        evacuate(r, 1)

    def turn_tiles(self, proj, tiles, out):
        nc = self.nc
        with self.stage("turn"):
            ps = self.psum("ps", 4)
            turned, bank_free = self.sems("turned bank_free")
            with nc.Block() as block:
                @block.tensor
                def _(pe):
                    for n, tile in enumerate(tiles):
                        if n >= 4:
                            pe.wait_ge(bank_free, n - 3)
                        for c in range(TT):
                            mm = nc.tensor.transpose(ps[:, n % 4, c * P:(c + 1) * P], proj[:, tile, c * P:(c + 1) * P],
                                                     self.c("ident"))
                        mm.then_inc(turned, 1)

                @block.scalar
                def _(act):
                    for n in range(len(tiles)):
                        act.wait_ge(turned, n + 1)
                        nc.scalar.activation(out[:, :, n * P:(n + 1) * P],
                                             ps[:, n % 4, :].rearrange("p (c f) -> p c f", c=TT), ACT.Copy)\
                            .then_inc(bank_free, 1)

    def attention_gates(self, gates):
        nc = self.nc
        with self.stage("gates"):
            wg = self.sb("wg", [P, KD, 24])
            ps = self.psum("ps", 1)[:, 0, :]
            loaded, done = self.sems("loaded done")
            with nc.Block() as block:
                @block.sync
                def _(sp):
                    sp.dma_start(wg[:], self.t["w_gates"]).then_inc(loaded, 16)

                @block.tensor
                def _(pe):
                    pe.wait_ge(loaded, 16)
                    for c in range(TT):
                        for k in range(KD):
                            mm = nc.tensor.matmul(ps[:, c * 24:(c + 1) * 24], self.hT[:, k, c * P:(c + 1) * P], wg[:, k, :],
                                                  start=k == 0, stop=k == KD - 1)
                    mm.then_inc(done, 1)

                @block.scalar
                def _(act):
                    act.wait_ge(done, 1)
                    nc.scalar.activation(gates[:].rearrange("p c n -> p (c n)"), ps[:, 0:TT * 24], ACT.Sigmoid)

    def hgrn(self, proj, vals):
        nc = self.nc
        W = HEADS * S
        with self.stage("hgrn"):
            f, b, ed, kk, qs, ql, kl = (self.sb(x, [P, HEADS, S]) for x in "f b ed kk qs ql kl".split())
            prod, at = self.sb("prod", [P, W]), self.sb("at", [P, W])
            qe, kend = f, ed
            kend_t = self.sb("kend_t", [P, HEADS, 3, P])
            state = self.sb("state", [P, 3, HEADS, P])
            dec = self.sb("dec", [P, HEADS, TT])
            lb, oml = self.sb("lb", [P, HEADS]), self.sb("oml", [P, HEADS])
            ps = self.psum("ps", 8)
            (lb_sub, lb_done, sig, f_done, log_done, scanned, k_done, q_done, shifted, decayed, ql_done, kl_done, mm_done,
             masked, added, s_chain, qe_done, kend_done, dec_done, k_turned, k_copied, sv_done, st_done) = self.sems(
                "lb_sub lb_done sig f_done log_done scanned k_done q_done shifted decayed ql_done kl_done mm_done masked "
                "added chain qe_done kend_done dec_done k_turned k_copied sv_done st_done")
            flat = lambda x: x[:].rearrange("p h t -> p (h t)")
            halves = lambda x, m: x[:].rearrange("p h (g m) -> p (h g) m", m=2 * m)
            LEVELS = [64 >> i for i in range(7)] + [0]

            with nc.Block() as block:
                def mask(dve, i):
                    dve.wait_ge(mm_done, i + 1)
                    lev = self.c("levels")[:, i * P:(i + 1) * P].rearrange("p (a t) -> p a t", a=1)
                    src = ps[:, 4 * (i % 2):4 * (i % 2) + 4, :].rearrange("p b (c t) -> p (b c) t", t=P)
                    if i:
                        dve.wait_ge(added, i + 1)
                    nc.vector.tensor_tensor(prod[:].rearrange("p (c t) -> p c t", t=P), src,
                                            lev.broadcast_to([P, HEADS * TT, P]), ALU.mult).then_inc(masked, 1)

                def add(pool, i):
                    pool.wait_ge(masked, i + 1)
                    pool.wait_ge(added, i + 1)
                    nc.gpsimd.tensor_tensor(at[:], at[:], prod[:], ALU.add).then_inc(added, 1)

                @block.scalar
                def _(act):
                    act.wait_ge(lb_sub, 1)
                    nc.scalar.activation(lb[:], lb[:], ACT.Sigmoid).then_inc(lb_done, 1)
                    nc.scalar.activation(flat(f), proj[:, F0:F0 + HEADS, :].rearrange("p h t -> p (h t)"), ACT.Sigmoid)\
                        .then_inc(sig, 1)
                    act.wait_ge(f_done, HEADS + 1)
                    nc.scalar.activation(flat(ql), flat(f), ACT.Ln).then_inc(log_done, 1)
                    for i, m in enumerate(LEVELS[:-1]):
                        act.wait_ge(shifted, 2 * i + 2)
                        nc.scalar.activation(flat(ed), flat(ed), ACT.Exp).then_inc(decayed, 1)
                    act.wait_ge(f_done, HEADS + 1)
                    act.wait_ge(k_done, 1)
                    nc.scalar.activation(flat(qe), flat(b), ACT.Exp).then_inc(qe_done, 1)
                    act.wait_ge(shifted, 15)
                    nc.scalar.activation(flat(kend), flat(kend), ACT.Exp).then_inc(kend_done, 1)
                    nc.scalar.activation(dec[:], b[:].rearrange("p h (c t) -> p h c t", t=P)[:, :, :, P - 1], ACT.Exp)\
                        .then_inc(dec_done, 1)
                    for h in range(HEADS):
                        act.wait_ge(k_turned, h + 1)
                        nc.scalar.activation(kend_t[:, h].rearrange("p c d -> p (c d)"), ps[:, h, 0:3 * P], ACT.Copy)\
                            .then_inc(k_copied, 1)

                @block.vector
                def _(dve):
                    chain = Chain(dve, s_chain)
                    nc.vector.tensor_tensor(lb[:], self.v("lb0"), self.v("lb1"), ALU.subtract).then_inc(lb_sub, 1)
                    dve.wait_ge(lb_done, 1)
                    chain(nc.vector.tensor_scalar(oml[:], lb[:], -1.0, 1.0, ALU.mult, ALU.add))
                    dve.wait_ge(sig, 1)
                    for h in range(HEADS):
                        nc.vector.tensor_scalar(f[:, h, :], f[:, h, :], oml[:, h:h + 1], lb[:, h:h + 1], ALU.mult, ALU.add)\
                            .then_inc(f_done, 1)
                    dve.wait_ge(f_done, HEADS)
                    nc.vector.tensor_scalar(flat(kk), flat(f), -1.0, 1.0, ALU.mult, ALU.add).then_inc(k_done, 1)
                    dve.wait_ge(k_done, 1)
                    nc.vector.tensor_scalar(flat(f), flat(f), LN_FLOOR, None, ALU.max).then_inc(f_done, 1)
                    nc.vector.tensor_scalar(flat(qs), proj[:, Q0:Q0 + HEADS, :].rearrange("p h t -> p (h t)"), P ** -0.5,
                                            None, ALU.mult).then_inc(q_done, 1)
                    dve.wait_ge(log_done, 1)
                    for h in range(HEADS):
                        for c in range(TT):
                            nc.vector.tensor_tensor_scan(b[:, h, c * P:(c + 1) * P], self.ones[:], ql[:, h, c * P:(c + 1) * P],
                                                         0.0, ALU.mult, ALU.add).then_inc(scanned, 1)
                    dve.wait_ge(scanned, HEADS * TT)
                    dve.wait_ge(q_done, 1)
                    for i, m in enumerate(LEVELS):
                        if m:
                            bh, eh = halves(b, m), halves(ed, m)
                            ref = bh[:, :, m - 1:m].broadcast_to([P, W // (2 * m), m])
                            if i:
                                dve.wait_ge(kl_done, i)
                                dve.wait_ge(ql_done, i)
                            nc.vector.tensor_tensor(eh[:, :, 0:m], ref, bh[:, :, 0:m], ALU.subtract).then_inc(shifted, 1)
                            nc.vector.tensor_tensor(eh[:, :, m:2 * m], bh[:, :, m:2 * m], ref, ALU.subtract)\
                                .then_inc(shifted, 1)
                            if i:
                                dve.wait_ge(mm_done, i)
                            dve.wait_ge(decayed, i + 1)
                            nc.vector.tensor_tensor(flat(ql), flat(qs), flat(ed), ALU.mult).then_inc(ql_done, 1)
                        if i:
                            mask(dve, i - 1)
                    bc = b[:].rearrange("p h (c t) -> p (h c) t", t=P)
                    dve.wait_ge(ql_done, 7)
                    dve.wait_ge(kl_done, 7)
                    nc.vector.tensor_tensor(kend[:].rearrange("p h (c t) -> p (h c) t", t=P),
                                            bc[:, :, P - 1:P].broadcast_to([P, HEADS * TT, P]), bc, ALU.subtract)\
                        .then_inc(shifted, 1)
                    mask(dve, 7)
                    dve.wait_ge(qe_done, 1)
                    nc.vector.tensor_tensor(flat(qe), flat(qe), flat(qs), ALU.mult).then_inc(qe_done, 1)
                    dve.wait_ge(kend_done, 1)
                    nc.vector.tensor_tensor(flat(kend), flat(kend), flat(kk), ALU.mult).then_inc(kend_done, 1)
                    dve.wait_ge(dec_done, 1)
                    for c in range(3):
                        dve.wait_ge(sv_done, c + 1)
                        pc = ps[:, 4 + c, :]
                        if c == 0:
                            nc.vector.tensor_copy(state[:, 0].rearrange("p h e -> p (h e)"), pc).then_inc(st_done, HEADS)
                        else:
                            dve.wait_ge(st_done, HEADS * c)
                            for h in range(HEADS):
                                nc.vector.scalar_tensor_tensor(out=state[:, c, h, :], in0=state[:, c - 1, h, :],
                                                               scalar=dec[:, h, c:c + 1], in1=pc[:, h * P:(h + 1) * P],
                                                               op0=ALU.mult, op1=ALU.add).then_inc(st_done, 1)

                @block.gpsimd
                def _(pool):
                    pool.wait_ge(k_done, 1)
                    nc.gpsimd.memset(at[:], 0.0).then_inc(added, 1)
                    for i in range(len(LEVELS)):
                        if LEVELS[i]:
                            pool.wait_ge(decayed, i + 1)
                            if i:
                                pool.wait_ge(mm_done, i)
                            nc.gpsimd.tensor_tensor(flat(kl), flat(kk), flat(ed), ALU.mult).then_inc(kl_done, 1)
                        if i:
                            add(pool, i - 1)
                    add(pool, 7)

                @block.tensor
                def _(pe):
                    for i, m in enumerate(LEVELS):
                        if m:
                            pe.wait_ge(ql_done, i + 1)
                            pe.wait_ge(kl_done, i + 1)
                        if i >= 2:
                            pe.wait_ge(masked, i - 1)
                        q, k = (ql, kl) if m else (qs, kk)
                        for h in range(HEADS):
                            for c in range(TT):
                                r = slice(c * P, (c + 1) * P)
                                mm = nc.tensor.matmul(ps[:, 4 * (i % 2) + h, r], k[:, h, r], q[:, h, r], start=True, stop=True)
                        mm.then_inc(mm_done, 1)
                    pe.wait_ge(kend_done, 2)
                    pe.wait_ge(masked, 7)
                    for h in range(HEADS):
                        for c in range(3):
                            mm = nc.tensor.transpose(ps[:, h, c * P:(c + 1) * P], kend[:, h, c * P:(c + 1) * P],
                                                     self.c("ident"))
                        mm.then_inc(k_turned, 1)
                    pe.wait_ge(k_copied, HEADS)
                    pe.wait_ge(masked, 8)
                    for c in range(3):
                        for h in range(HEADS):
                            mm = nc.tensor.matmul(ps[:, 4 + c, h * P:(h + 1) * P], kend_t[:, h, c, :],
                                                  vals[:, c, h * P:(h + 1) * P], start=True, stop=True)
                        mm.then_inc(sv_done, 1)
                    pe.wait_ge(added, 9)
                    pe.wait_ge(qe_done, 2)
                    for h in range(HEADS):
                        for c in range(TT):
                            r = slice(c * P, (c + 1) * P)
                            if c:
                                pe.wait_ge(st_done, HEADS * c)
                            nc.tensor.matmul(ps[:, h, r], vals[:, c, h * P:(h + 1) * P], at[:, h * S + c * P:h * S + (c + 1) * P],
                                             start=True, stop=c == 0)
                            if c:
                                nc.tensor.matmul(ps[:, h, r], state[:, c - 1, h, :], qe[:, h, r], start=False, stop=True)
            self.hgrn_out(proj, ps, ed, ql, prod[:, 0:S], prod[:, S:2 * S])

    def hgrn_out(self, proj, ps, o, gate, sq, rstd):
        nc = self.nc
        copied, gated, squared, summed, rooted, inverted, scaled, done = self.sems(
            "o_copied gated squared summed rooted inverted scaled out_done")
        with nc.Block() as block:
            @block.scalar
            def _(act):
                nc.scalar.activation(gate[:].rearrange("p h t -> p (h t)"),
                                     proj[:, G0:G0 + HEADS, :].rearrange("p h t -> p (h t)"), ACT.Silu).then_inc(gated, 1)
                for h in range(HEADS):
                    if h:
                        act.wait_ge(summed, h)
                    nc.scalar.activation(sq[:], ps[:, h, :], ACT.Square).then_inc(squared, 1)
                    act.wait_ge(summed, h + 1)
                    if h:
                        act.wait_ge(scaled, h)
                    nc.scalar.activation(rstd[:], ps[:, 4 + h % 2, :], ACT.Sqrt, bias=self.eps[:, 0:1], scale=1.0 / P)\
                        .then_inc(rooted, 1)

            @block.tensor
            def _(pe):
                for h in range(HEADS):
                    pe.wait_ge(squared, h + 1)
                    if h >= 2:
                        pe.wait_ge(rooted, h - 1)
                    nc.tensor.matmul(ps[:, 4 + h % 2, :], self.ones[:], sq[:], start=True, stop=True).then_inc(summed, 1)

            @block.vector
            def _(dve):
                for h in range(HEADS):
                    dve.wait_ge(rooted, h + 1)
                    nc.vector.reciprocal(rstd[:], rstd[:]).then_inc(inverted, 1)
                    dve.wait_ge(inverted, h + 1)
                    nc.vector.tensor_tensor(o[:, h, :], ps[:, h, :], rstd[:], ALU.mult).then_inc(scaled, 1)
                    dve.wait_ge(scaled, h + 1)
                    dve.wait_ge(gated, 1)
                    nc.vector.scalar_tensor_tensor(out=self.hT[:, h, :], in0=o[:, h, :], scalar=self.v("hg_norm_g")[:, h:h + 1],
                                                   in1=gate[:, h, :], op0=ALU.mult, op1=ALU.mult).then_inc(done, 1)

    def rope(self, proj, rot):
        nc = self.nc
        tiles = [NQ0, NQ0 + 1, NQ0 + 2, NQ0 + 3, KS, KW]
        with self.stage("rope"):
            ps = self.psum("ps", 6)
            crossed = self.sb("crossed", [P, 2, S])
            scaled, turned, straight, cross, done = self.sems("q_scaled turned straight crossed done")
            with nc.Block() as block:
                @block.scalar
                def _(act):
                    q = proj[:, NQ0:NQ0 + 4, :]
                    nc.scalar.mul(q, q, 0.125).then_inc(scaled, 1)

                @block.tensor
                def _(pe):
                    pe.wait_ge(scaled, 1)
                    for n, tile in enumerate(tiles):
                        nc.tensor.matmul(ps[:, n, :], self.c("rot"), proj[:, tile, :], start=True, stop=True)\
                            .then_inc(turned, 1)

                @block.gpsimd
                def _(pool):
                    pool.wait_ge(scaled, 1)
                    for n, tile in enumerate(tiles):
                        nc.gpsimd.tensor_tensor(rot[:, n, :], proj[:, tile, :], self.c("cos"), ALU.mult).then_inc(straight, 1)

                @block.vector
                def _(dve):
                    for n in range(len(tiles)):
                        dve.wait_ge(turned, n + 1)
                        if n >= 2:
                            dve.wait_ge(done, n - 1)
                        nc.vector.tensor_tensor(crossed[:, n % 2, :], ps[:, n, :], self.c("sin"), ALU.mult).then_inc(cross, 1)
                        dve.wait_ge(cross, n + 1)
                        dve.wait_ge(straight, n + 1)
                        nc.vector.tensor_tensor(rot[:, n, :], rot[:, n, :], crossed[:, n % 2, :], ALU.add).then_inc(done, 1)

    def compress(self, proj, k_cmp, v_cmp):
        nc, t = self.nc, self.t
        N = S - 16
        B = 3 * N_CMP
        with self.stage("compress"):
            x = self.sb("x", [P, 2, 3, N])
            w1, w2 = self.sb("w1", [P, 2, 16, 256]), self.sb("w2", [P, 2, 2, 64])
            bias, hid = self.sb("bias", [P, 4]), self.sb("hid", [P, 2, 2, 2 * N_CMP])
            ps = self.psum("ps", 6)
            zeroed, loaded, hid_ps, bias_done, hid_done, out_ps = self.sems("zeroed loaded hidden_products bias_done hid_done out_products")
            with nc.Block() as block:
                @block.gpsimd
                def _(pool):
                    nc.gpsimd.memset(x[:, :, 2, :], 0.0).then_inc(zeroed, 1)
                    nc.gpsimd.memset(v_cmp[:], 0.0).then_inc(zeroed, 1)

                @block.sync
                def _(sp):
                    sp.wait_ge(zeroed, 1)
                    for n, (tile, name) in enumerate(((KC, "k"), (VC, "v"))):
                        for g in range(2):
                            rows = slice(64 * g, 64 * g + 64)
                            sp.dma_start(x[0:64, n, g, :], proj[rows, tile, 0:N]).then_inc(loaded, 16)
                            sp.dma_start(x[64:128, n, g, :], proj[rows, tile, 16:S]).then_inc(loaded, 16)
                        sp.dma_start(x[:, n, 2, 0:16], t[f"pos_{name}"]).then_inc(loaded, 16)
                        sp.dma_start(w1[:, n], t[f"w1_{name}"]).then_inc(loaded, 16)
                        sp.dma_start(w2[:, n], t[f"w2_{name}"]).then_inc(loaded, 16)

                @block.tensor
                def _(pe):
                    pe.wait_ge(loaded, 14 * 16)
                    for n in range(2):
                        for m in range(2):
                            for l in range(16):
                                mm = nc.tensor.matmul(ps[:, 2 * n + m, 0:B].rearrange("p (g c) -> p g c", g=3),
                                                      w1[:, n, l, m * P:(m + 1) * P],
                                                      x[:, n, :, l:l + CMP_STRIDE * (N_CMP - 1) + 1:CMP_STRIDE],
                                                      start=l == 0, stop=l == 15)
                            mm.then_inc(hid_ps, 1)
                    pe.wait_ge(hid_done, 4)
                    for g in range(2):
                        for m in range(2):
                            mm = nc.tensor.matmul(ps[64 * g:64 * g + 64, 4, 0:N_CMP], w2[:, 0, m, :],
                                                  hid[:, 0, m, g * N_CMP:(g + 1) * N_CMP], start=m == 0, stop=m == 1)
                    for g in range(2):
                        for m in range(2):
                            mm = nc.tensor.matmul(ps[0:N_CMP, 5, 64 * g:64 * g + 64], hid[:, 1, m, g * N_CMP:(g + 1) * N_CMP],
                                                  w2[:, 1, m, :], start=m == 0, stop=m == 1)
                    mm.then_inc(out_ps, 1)

                @block.vector
                def _(dve):
                    for i in range(4):
                        dve.wait_ge(hid_ps, i + 1)
                        b1 = self.v("b1_k" if i < 2 else "b1_v")
                        nc.vector.tensor_tensor(bias[:, i:i + 1], ps[:, i, 2 * N_CMP:2 * N_CMP + 1], b1[:, i % 2:i % 2 + 1],
                                                ALU.add).then_inc(bias_done, 1)
                    dve.wait_ge(out_ps, 1)
                    dve.wait_ge(zeroed, 2)
                    nc.vector.tensor_copy(k_cmp[:], ps[:, 4, 0:N_CMP])
                    nc.vector.tensor_copy(v_cmp[0:N_CMP, :], ps[0:N_CMP, 5, 0:P])

                @block.scalar
                def _(act):
                    for i in range(4):
                        act.wait_ge(bias_done, i + 1)
                        nc.scalar.activation(hid[:, i // 2, i % 2, :], ps[:, i, 0:2 * N_CMP], ACT.Gelu_apprx_tanh,
                                             bias=bias[:, i:i + 1]).then_inc(hid_done, 1)

    def attend(self, items, out_tile, sink=None, clear=False, beside=None):
        nc = self.nc
        n_items = len(items)
        with self.stage("attend"):
            p = self.sb("p", [P, 4, S])
            pt = self.sb("pt", [P, 2, S])
            top, den, fac = (self.sb(x, [P, n_items]) for x in "top den fac".split())
            es = self.sb("es", [P, n_items])
            psS, psT, psO, psM = self.psum("scores", 3), self.psum("turned", 2), self.psum("outs", 2), self.psum("mod", 1)
            if beside:
                chunks, mod = beside[-1], Modulation(self, *beside[:-1], psM[:, 0, :], slots=4)
            (zeroed, scores, masked, topped, expd, facd, scaled, turned, copied, products, moved, kept, raw_top, sunk) = self.sems(
                "zeroed scores masked topped expd fac_ready scaled turned copied products moved kept raw_top sunk")
            if clear:
                blank, blanked, cleared = self.sb("blank", [P, D]), self.sem("blanked"), self.sem("cleared")
            keys = [it["k"].shape[-1] for it in items]
            wide = [-(-n // P) * P for n in keys]
            pairs_before = [sum(x["last"] for x in items[:i]) for i in range(n_items + 1)]

            with nc.Block() as block:
                if clear:
                    @block.sync
                    def _(sp):
                        rows = self.y_rows.rearrange("(p b) d -> p b d", b=NBLK)
                        if beside:
                            with sp.Fori(0, chunks) as g:
                                mod.load(sp, g, range(KD))
                        sp.wait_ge(blanked, 1)
                        with sp.Fori(S * TOPK // BLK, NBLK) as b:
                            sp.dma_start(rows[:, bass.ds(b, 1), :].rearrange("p a d -> p (a d)"), blank[:]).then_inc(cleared, 16)
                        sp.wait_ge(cleared, 16 * (NBLK - S * TOPK // BLK))

                @block.gpsimd
                def _(pool):
                    if clear:
                        nc.gpsimd.memset(blank[:], 0.0).then_inc(blanked, 1)
                    nc.gpsimd.memset(p[:], 0.0).then_inc(zeroed, 1)
                    for i, it in enumerate(items):
                        pool.wait_ge(facd, i + 1)
                        s = p[:, i % 4, 0:wide[i]]
                        if it["keep"] is not None:
                            seen = p[:, i % 4, 0:keys[i]]
                            nc.gpsimd.tensor_tensor(seen, seen, it["keep"], ALU.mult).then_inc(kept, 1)
                            pool.wait_ge(kept, sum(x["keep"] is not None for x in items[:i + 1]))
                        if it["gate"] is None:
                            nc.gpsimd.tensor_scalar(s, s, fac[:, i:i + 1], None, ALU.mult).then_inc(scaled, 1)
                        else:
                            nc.gpsimd.tensor_scalar(s, s, fac[:, i:i + 1], it["gate"], ALU.mult, ALU.mult)\
                                .then_inc(scaled, 1)

                @block.tensor
                def _(pe):
                    def score(i):
                        it = items[i]
                        if i >= 3:
                            pe.wait_ge(expd, i - 2)
                        nc.tensor.matmul(psS[:, i % 3, 0:keys[i]], it["q"], it["k"], start=True, stop=True).then_inc(scores, 1)

                    def turn(i):
                        pe.wait_ge(scaled, i + 1)
                        if i >= 2:
                            pe.wait_ge(copied, i - 1)
                        for b in range(wide[i] // P):
                            mm = nc.tensor.transpose(psT[:, i % 2, b * P:(b + 1) * P], p[:, i % 4, b * P:(b + 1) * P],
                                                     self.c("ident"))
                        mm.then_inc(turned, 1)

                    def multiply(i):
                        it = items[i]
                        pe.wait_ge(copied, i + 1)
                        pair = pairs_before[i]
                        if pair >= 2:
                            pe.wait_ge(moved, pair - 1)
                        lo = it["out"][0]
                        for b, v in enumerate(it["v"]):
                            mm = nc.tensor.matmul(psO[lo:lo + 64, pair % 2, 0:P], v, pt[:, i % 2, b * P:(b + 1) * P],
                                                  start=it["first"] and b == 0, stop=it["ends"] and b == len(it["v"]) - 1)
                        mm.then_inc(products, 1)

                    for i in range(n_items + 4):
                        if i < n_items:
                            score(i)
                        if beside and i % KD == 0 and 1 <= i // KD <= chunks:
                            mod.reduce(pe, i // KD - 1)
                        if 0 <= i - 3 < n_items:
                            turn(i - 3)
                        if i >= 4:
                            multiply(i - 4)

                @block.vector
                def _(dve):
                    def find_top(i):
                        it = items[i]
                        dve.wait_ge(scores, i + 1)
                        s = psS[:, i % 3, 0:keys[i]]
                        if it["mask"] is not None:
                            at, mask = it["mask"]
                            n = mask.shape[-1]
                            nc.vector.tensor_tensor(s[:, at:at + n], s[:, at:at + n], mask, ALU.add).then_inc(masked, 1)
                            dve.wait_ge(masked, i + 1)
                        else:
                            dve.sem_inc(masked, 1)
                        if sink is None:
                            nc.vector.tensor_reduce(top[:, i:i + 1], s, AX.X, ALU.max, negate=True).then_inc(topped, 1)
                        else:
                            nc.vector.tensor_reduce(top[:, i:i + 1], s, AX.X, ALU.max).then_inc(raw_top, 1)
                            dve.wait_ge(raw_top, i + 1)
                            nc.vector.tensor_scalar(top[:, i:i + 1], top[:, i:i + 1], sink(i), -1.0, ALU.max, ALU.mult)\
                                .then_inc(topped, 1)

                    def factor(i):
                        dve.wait_ge(expd, i + 1)
                        d = den[:, i:i + 1]
                        if sink is not None:
                            nc.vector.tensor_tensor(d, d, es[:, i:i + 1], ALU.add).then_inc(sunk, 1)
                            dve.wait_ge(sunk, i + 1)
                        nc.vector.reciprocal(fac[:, i:i + 1], d).then_inc(facd, 1)

                    def move(i):
                        if 0 <= i < n_items and items[i]["last"]:
                            _, j, qt = items[i]["out"]
                            dve.wait_ge(products, i + 1)
                            nc.vector.tensor_copy(self.hT[:, out_tile + j, qt * P:(qt + 1) * P],
                                                  psO[:, pairs_before[i] % 2, 0:P]).then_inc(moved, 1)

                    if beside:
                        mod.free(dve)
                    for i in range(n_items + 5):
                        if i < n_items:
                            find_top(i)
                        if 1 <= i <= n_items:
                            factor(i - 1)
                        move(i - 5)
                        if beside and i >= 1:
                            g, piece = (i - 1) // KD, (i - 1) % KD
                            if piece == 0 and 1 <= g <= chunks:
                                mod.finish(dve, g - 1)
                            if g < chunks:
                                mod.multiply(dve, g, [piece])

                @block.scalar
                def _(act):
                    act.wait_ge(zeroed, 1)
                    if beside:
                        mod.start(act)

                    def exponents(i):
                        act.wait_ge(topped, i + 1)
                        if i >= 4:
                            act.wait_ge(turned, i - 3)
                        if sink is not None:
                            nc.scalar.activation(es[:, i:i + 1], sink(i), ACT.Exp, bias=top[:, i:i + 1])
                        nc.scalar.activation(p[:, i % 4, 0:keys[i]], psS[:, i % 3, 0:keys[i]], ACT.Exp, bias=top[:, i:i + 1],
                                             accum_out=den[:, i:i + 1]).then_inc(expd, 1)

                    def copy(i):
                        act.wait_ge(turned, i + 1)
                        if i >= 2:
                            act.wait_ge(products, i - 1)
                        nc.scalar.activation(pt[:, i % 2, 0:wide[i]], psT[:, i % 2, 0:wide[i]], ACT.Copy).then_inc(copied, 1)

                    for i in range(n_items + 3):
                        if i < n_items:
                            exponents(i)
                        if i >= 3:
                            copy(i - 3)

    def nsa_items(self, proj, rot, k_cmp, v_cmp, vals, gates):
        items = []
        for qt in range(TT):
            cols = slice(qt * P, (qt + 1) * P)
            for j in range(NSA_PAIRS):
                for g in range(2):
                    rows = slice(64 * g, 64 * g + 64)
                    h = 3 * (4 * g + j)
                    gate = [gates[:, qt, h + b:h + b + 1] for b in range(3)]
                    base = {"out": (64 * g, j, qt), "keep": None, "last": False, "first": False, "ends": False}
                    add = self.c("cmp_add")[:, qt * N_CMP:(qt + 1) * N_CMP]
                    items.append(base | {"q": proj[rows, NQ0 + j, cols], "k": k_cmp[rows, :], "v": [v_cmp[:, rows]],
                                         "mask": (0, add), "gate": gate[0], "keep": self.c("cmp_keep") if qt == 0 else None,
                                         "first": True})
                    for n, branch in enumerate((4, 5)):
                        v0 = 512 + 128 * n + 64 * g
                        items.append(base | {"q": rot[rows, j, cols], "k": rot[rows, branch, 0:(qt + 1) * P],
                                             "v": [vals[:, b, v0:v0 + 64] for b in range(qt + 1)],
                                             "mask": (qt * P, self.c("causal")), "gate": gate[1 + n],
                                             "ends": n == 1, "last": n == 1 and g == 1})
        return items

    def feed_forward(self, layer, sub, w_gu, w_dn, beside=None):
        nc, xT = self.nc, self.xT
        m = 24 * sub
        gn = 24 * layer + 8 * sub
        with self.parts(f"f{layer}{sub}") as h:
            self.norm(None, self.v("g_norm", gn, gn + 8), scale=self.mod[:, m + 8:m + 16], shift=self.mod[:, m:m + 8], parts=h)
            self.gated_layer(h, self.mod[:, m + 16:m + 24], w_gu, w_dn, beside)

    def gated_layer(self, h, gate, w_gu, w_dn, beside=None):
        nc, xT = self.nc, self.xT
        HALF = FT // 2
        with self.stage("ffn"):
            wt = self.sb("wt", [P, 2, 2 * D])
            high, low = self.sb("high", [P, 2, 2 * D], F32R), self.sb("low", [P, 2, 2 * D], F32R)
            hid_high, hid_low = self.sb("hid_high", [P, FT, S], F32R), self.sb("hid_low", [P, FT, S], F32R)
            sg = self.sb("sg", [P, 2, S])
            half = self.sb("half", [P, KD])
            ps = self.psum("ps", 8)
            rounds = 0
            if beside:
                at = CON["cos"][0]
                wk = self.con[:, at:at + 2 * Modulation.CHUNK].rearrange("p (s n) -> p s n", s=2)
                rounds, mod = beside[-1], Modulation(self, *beside[:-1], ps[:, 7, :], wk)
            loaded = [self.sem(f"loaded{s}") for s in range(2)]
            high_done, low_done, multiplied, gate_ps, up_ps, silu_done, hid_done, hid_seen, hid_high_done, hid_low_done, half_done, out_done = \
                self.sems("high_done low_done multiplied gate_products up_products silu_done hidden_done hidden_seen hidden_high_done "
                          "hidden_low_done half_done out_done")
            with nc.Block() as block:
                @block.sync
                def _(sp):
                    def up(r, s):
                        sp.dma_start(wt[:, s], w_gu[bass.ds(2 * r + s, 1)].rearrange("a p k n -> (a p) (k n)"))\
                            .then_inc(loaded[s], 16)

                    def up_again(r, s):
                        sp.wait_ge(low_done, 2 * r + s - 1)
                        up(r, s)

                    def down(r, s):
                        sp.wait_ge(low_done, 2 * r + s + FT - 1)
                        sp.dma_start(wt[:, s].rearrange("p (a n) -> p a n", a=2),
                                     w_dn[bass.ds(4 * r + 2 * s, 2)].rearrange("a p n -> p a n")).then_inc(loaded[s], 16)
                    up(0, 0)
                    up(0, 1)
                    if beside:
                        with sp.Fori(0, rounds) as g:
                            up_again(2 * g + 1, 0)
                            mod.load(sp, g, (0, 1))
                            up_again(2 * g + 1, 1)
                            mod.load(sp, g, (2, 3))
                            up_again(2 * g + 2, 0)
                            mod.load(sp, g, (4, 5))
                            up_again(2 * g + 2, 1)
                            mod.load(sp, g, (6, 7))
                    in_pairs(sp, FT, up_again, first=1 + 2 * rounds)
                    in_pairs(sp, HALF, down)

                @block.tensor
                def _(pe):
                    pe.sem_inc(multiplied, 2)

                    def up(r, s):
                        pe.wait_ge(low_done, 2 * r + s + 1)
                        pe.wait_ge(hid_done, 2 * r + s + 1)
                        for bank, sem in ((0, gate_ps), (1, up_ps)):
                            for k in range(KD):
                                c = slice((2 * k + bank) * P, (2 * k + bank + 1) * P)
                                mm = self.mm3(ps[:, 2 * s + bank, :], (high[:, s, c], low[:, s, c]), (h[0][:, k, :], h[1][:, k, :]),
                                              start=k == 0, stop=k == KD - 1)
                            mm.then_inc(sem, 1)
                        pe.wait_ge(up_ps, 2 * r + s + 1)
                        pe.sem_inc(multiplied, 1)

                    def down(r, s, first=False, last=False):
                        pe.wait_ge(low_done, FT + 2 * r + s + 1)
                        for a in range(2):
                            x = [t_[:, bass.ds(4 * r + 2 * s + a, 1), :].rearrange("p a t -> p (a t)") for t_ in (hid_high, hid_low)]
                            for n in range(KD):
                                c = slice(a * D + n * P, a * D + (n + 1) * P)
                                mm = self.mm3(ps[:, n, :], (high[:, s, c], low[:, s, c]), x, start=first and a == 0,
                                              stop=last and a == 1)
                        mm.then_inc(multiplied, 1)
                    if beside:
                        with pe.Fori(0, rounds) as g:
                            for r in (2 * g, 2 * g + 1):
                                up(r, 0)
                                up(r, 1)
                            mod.reduce(pe, g)
                    in_pairs(pe, FT, up, first=2 * rounds)
                    pe.wait_ge(hid_done, FT + 2)
                    pe.wait_ge(hid_low_done, FT + 2)
                    down(0, 0, first=True)
                    down(0, 1)
                    with pe.Fori(1, HALF // 2) as r:
                        down(r, 0)
                        down(r, 1)
                    down(HALF // 2, 0, last=True)

                def ahead(eng, split, finish, first=0):
                    if first == 0:
                        split(0, 0)
                    with eng.Fori(first, HALF) as r:
                        split(r, 1)
                        finish(r, 0)
                        split(r + 1, 0)
                        finish(r, 1)
                    split(HALF, 1)
                    with eng.Fori(HALF + 1, (FT + HALF) // 2) as r:
                        split(r, 0)
                        split(r, 1)
                    split((FT + HALF) // 2, 0)

                @block.scalar
                def _(act):
                    act.sem_inc(hid_low_done, 2)
                    if beside:
                        mod.start(act)

                    def split(r, s):
                        act.wait_ge(loaded[s], 16 * (r + 1))
                        act.wait_ge(multiplied, 2 * r + s + 1)
                        nc.scalar.activation(high[:, s], wt[:, s], ACT.Copy).then_inc(high_done, 1)

                    def finish(r, s):
                        n = 2 * r + s
                        act.wait_ge(gate_ps, n + 1)
                        act.wait_ge(hid_low_done, n + 1)
                        nc.scalar.activation(sg[:, s, :], ps[:, 2 * s, :], ACT.Silu).then_inc(silu_done, 1)
                    ahead(act, split, finish)

                @block.gpsimd
                def _(pool):
                    def hidden_high(r, s):
                        pool.wait_ge(hid_done, 2 * r + s + 3)
                        pool.sem_inc(hid_seen, 1)
                        nc.gpsimd.tensor_copy(hid_high[:, bass.ds(2 * r + s, 1), :].rearrange("p a t -> p (a t)"), sg[:, s, :])\
                            .then_inc(hid_high_done, 1)
                    in_pairs(pool, FT, hidden_high)

                @block.vector
                def _(dve):
                    dve.sem_inc(hid_done, 2)
                    nc.vector.tensor_scalar(half[:], gate, 0.5, None, ALU.mult).then_inc(half_done, 1)

                    def split(r, s):
                        dve.wait_ge(high_done, 2 * r + s + 1)
                        nc.vector.tensor_tensor(low[:, s], wt[:, s], high[:, s].bitcast(F32), ALU.subtract).then_inc(low_done, 1)

                    def finish(r, s):
                        n = 2 * r + s
                        dve.wait_ge(up_ps, n + 1)
                        dve.wait_ge(silu_done, n + 1)
                        nc.vector.tensor_tensor(sg[:, s, :], sg[:, s, :], ps[:, 2 * s + 1, :], ALU.mult).then_inc(hid_done, 1)
                        dve.wait_ge(hid_high_done, n + 1)
                        part = lambda x: x[:, bass.ds(n, 1), :].rearrange("p a t -> p (a t)")
                        nc.vector.tensor_tensor(part(hid_low), sg[:, s, :], part(hid_high).bitcast(F32), ALU.subtract)\
                            .then_inc(hid_low_done, 1)
                    if beside:
                        mod.free(dve)
                        split(0, 0)
                        with dve.Fori(0, rounds) as g:
                            for piece, r in ((0, 2 * g), (4, 2 * g + 1)):
                                split(r, 1)
                                mod.multiply(dve, g, (piece, piece + 1))
                                finish(r, 0)
                                split(r + 1, 0)
                                mod.multiply(dve, g, (piece + 2, piece + 3))
                                finish(r, 1)
                            mod.finish(dve, g)
                    ahead(dve, split, finish, first=2 * rounds)
                    dve.wait_ge(multiplied, FT + HALF + 2)
                    dve.wait_ge(half_done, 1)
                    for n in range(KD):
                        nc.vector.scalar_tensor_tensor(out=xT[:, n, :], in0=ps[:, n, :], scalar=half[:, n:n + 1],
                                                       in1=xT[:, n, :], op0=ALU.mult, op1=ALU.add).then_inc(out_done, 1)

    def project_out(self, w, gate, hT):
        nc, xT = self.nc, self.xT
        G = KD // 2
        with self.stage("out"):
            wt, high, low = (self.sb(n, [P, 2, KD, 2 * P], dt) for n, dt in (("wt", F32), ("high", F32R), ("low", F32R)))
            hh, hl = self.sb("hh", [P, KD, S], F32R), self.sb("hl", [P, KD, S], F32R)
            ps = self.psum("ps", 8)
            loaded = [self.sem(f"loaded{s}") for s in range(2)]
            high_done, low_done, h_high, h_low, tile_done, added = self.sems("high_done low_done h_high h_low tile_done added")
            with nc.Block() as block:
                @block.sync
                def _(sp):
                    for g in range(G):
                        if g >= 2:
                            sp.wait_ge(low_done, g - 1)
                        sp.dma_start(wt[:, g % 2], w[g]).then_inc(loaded[g % 2], 16)

                @block.scalar
                def _(act):
                    for g in range(G):
                        act.wait_ge(loaded[g % 2], 16 * (g // 2 + 1))
                        if g >= 2:
                            act.wait_ge(tile_done, 2 * g - 2)
                        nc.scalar.activation(high[:, g % 2], wt[:, g % 2], ACT.Copy).then_inc(high_done, 1)

                @block.gpsimd
                def _(pool):
                    for k in range(KD):
                        nc.gpsimd.tensor_copy(hh[:, k, :], hT[:, k, :]).then_inc(h_high, 1)

                @block.vector
                def _(dve):
                    def split(g):
                        dve.wait_ge(high_done, g + 1)
                        nc.vector.tensor_tensor(low[:, g % 2], wt[:, g % 2], high[:, g % 2].bitcast(F32), ALU.subtract)\
                            .then_inc(low_done, 1)
                    for k in range(KD):
                        dve.wait_ge(h_high, k + 1)
                        nc.vector.tensor_tensor(hl[:, k, :], hT[:, k, :], hh[:, k, :].bitcast(F32), ALU.subtract).then_inc(h_low, 1)
                    split(0)
                    for n in range(KD):
                        if n % 2 == 0 and n // 2 + 1 < G:
                            split(n // 2 + 1)
                        dve.wait_ge(tile_done, n + 1)
                        nc.vector.scalar_tensor_tensor(out=xT[:, n, :], in0=ps[:, n, :], scalar=gate[:, n:n + 1],
                                                       in1=xT[:, n, :], op0=ALU.mult, op1=ALU.add).then_inc(added, 1)

                @block.tensor
                def _(pe):
                    pe.wait_ge(h_low, KD)
                    for g in range(G):
                        pe.wait_ge(low_done, g + 1)
                        for u in range(2):
                            for k in range(KD):
                                c = slice(u * P, (u + 1) * P)
                                mm = self.mm3(ps[:, 2 * g + u, :], (high[:, g % 2, k, c], low[:, g % 2, k, c]), (hh[:, k, :], hl[:, k, :]),
                                              start=k == 0, stop=k == KD - 1)
                            mm.then_inc(tile_done, 1)

    def first_mixer(self):
        nc, t = self.nc, self.t
        with ExitStack() as ctx:
            tile = lambda name, shape: ctx.enter_context(nc.sbuf_tensor(name, shape, F32))
            self.hT = tile("hT_1", [P, KD, S])
            proj, gates = tile("proj", [P, IN_TILES, S]), tile("gates", [P, TT, 24])
            k_cmp, v_cmp = tile("k_cmp", [P, N_CMP]), tile("v_cmp", [P, P])
            with self.parts("1") as h:
                self.norm(self.hT, self.v("norm1_g"), scale=self.mod[:, 8:16], shift=self.mod[:, 0:8], parts=h)
                self.project(t["w_in"], IN_TILES // 2, h, proj,
                             beside=(t["w_ada"][:, 16 * P:], self.v("c"), self.v("b_ada", 16), self.mod[:, 16:48], 4))
            vals, rot = tile("vals", [P, TT, 768]), tile("rot", [P, 6, S])
            self.attention_gates(gates)
            self.turn_tiles(proj, [HI0, HI0 + 1, HI0 + 2, HI0 + 3, VS, VW], vals)
            self.rope(proj, rot)
            self.compress(proj, k_cmp, v_cmp)
            self.hgrn(proj, vals)
            self.attend(self.nsa_items(proj, rot, k_cmp, v_cmp, vals, gates), 4, clear=True,
                        beside=(t["w_mod"][0], self.v("c_2"), self.v("b_mod0"), self.mods[1], 9))
            self.project_out(t["w_out"], self.mod[:, 16:24], self.hT)

    def second_mixer(self, layer):
        nc, t = self.nc, self.t
        with ExitStack() as ctx:
            tile = lambda name, shape: ctx.enter_context(nc.sbuf_tensor(f"{name}_{layer}", shape, F32))
            self.hT = tile("hT_2", [P, KD, S])
            proj, vals, bias = tile("proj2", [P, IN_TILES_2, S]), tile("vals2", [P, TT, P]), tile("alibi", [P, 8, 2 * P])
            with self.parts(f"2{layer}") as h:
                self.norm(None, self.v("g_norm", 24 * layer + 8, 24 * layer + 16), scale=self.mod[:, 32:40],
                          shift=self.mod[:, 24:32], parts=h)
                self.project(t["w_in_2"][layer], IN_TILES_2 // 2, h, proj)
            self.scale_queries(proj, bias)
            self.turn_tiles(proj, [AV], vals)
            self.attend(self.window_items(proj, vals, bias), 0,
                        sink=lambda i: self.v("sinks")[:, 8 * layer + i % 8:8 * layer + i % 8 + 1])
            self.recurrence(layer, proj)
            self.project_out(t["w_out_2"][layer], self.mod[:, 40:48], self.hT)

    def scale_queries(self, proj, bias):
        nc = self.nc
        with self.stage("scale"):
            loaded = self.sem("loaded")
            with nc.Block() as block:
                @block.sync
                def _(sp):
                    sp.dma_start(bias[:], self.t["alibi"]).then_inc(loaded, 16)
                    sp.wait_ge(loaded, 16)

                @block.scalar
                def _(act):
                    nc.scalar.mul(proj[:, AQ0:AQ0 + 4, :], proj[:, AQ0:AQ0 + 4, :], 0.125)

    def window_items(self, proj, vals, bias):
        items = []
        for qt in range(TT):
            for j in range(4):
                for g in range(2):
                    rows = slice(64 * g, 64 * g + 64)
                    lo = max(qt - 1, 0)
                    skip = P if qt == 0 else 0
                    items.append({"q": proj[rows, AQ0 + j, qt * P:(qt + 1) * P], "k": proj[rows, AK, lo * P:(qt + 1) * P],
                                  "v": [vals[:, b, rows] for b in range(lo, qt + 1)],
                                  "mask": (0, bias[:, 2 * j + g, skip:]), "gate": None, "keep": None,
                                  "out": (64 * g, j, qt), "first": True, "ends": True, "last": g == 1})
        return items

    def recurrence(self, layer, proj):
        nc = self.nc
        with self.stage("lru"):
            wa, wx = self.sb("wa", [P, 2, P]), self.sb("wx", [P, 2, P])
            xc, r, i_, a, mult, u, th, pr, cv = (self.sb(x, [P, 2, S]) for x in "xc r i a mult u th pr cv".split())
            e, s2, z, pos = (self.sb(x, [P, 2]) for x in "e s2 z pos".split())
            poly = self.sb("poly", [P, 2])
            ps = self.psum("ps", 4)
            flat = lambda x: x[:].rearrange("p n t -> p (n t)")
            loaded, conv_done, gates_ps, chain_s, act_s, pool_s, abs_done, loga, tanh_done, mult_in, rooted, hid, gelu = self.sems(
                "loaded conv_done gate_products chain act_steps pool_steps abs_done log_a tanh_done mult_in rooted hidden gelu")
            w4 = lambda k, n: self.v("conv_w")[:, 8 * layer + 2 * k + n:8 * layer + 2 * k + n + 1]
            w3 = lambda k, n: self.v("sc_conv_w")[:, 6 * layer + 2 * k + n:6 * layer + 2 * k + n + 1]
            two = lambda name: self.v(name)[:, 2 * layer:2 * layer + 2]
            with nc.Block() as block:
                @block.sync
                def _(sp):
                    sp.dma_start(wa[:], self.t["gate_a"][layer]).then_inc(loaded, 16)
                    sp.dma_start(wx[:], self.t["gate_x"][layer]).then_inc(loaded, 16)

                @block.vector
                def _(dve):
                    chain = Chain(dve, chain_s)
                    for n in range(2):
                        x = proj[:, LX0 + n, :]
                        chain(nc.vector.tensor_scalar(xc[:, n, :], x, w4(3, n), two("conv_b")[:, n:n + 1], ALU.mult, ALU.add))
                        for k in range(3):
                            d = 3 - k
                            chain(nc.vector.scalar_tensor_tensor(out=xc[:, n, d:], in0=x[:, 0:S - d], scalar=w4(k, n),
                                                                 in1=xc[:, n, d:], op0=ALU.mult, op1=ALU.add))
                    dve.sem_inc(conv_done, 1)
                    lam = two("lam")
                    dve.wait_ge(abs_done, 1)
                    chain(nc.vector.tensor_scalar(z[:], e[:], 2.0, None, ALU.add))
                    chain(nc.vector.reciprocal(z[:], z[:]))
                    chain(nc.vector.tensor_tensor(z[:], z[:], e[:], ALU.mult))
                    chain(nc.vector.tensor_tensor(s2[:], z[:], z[:], ALU.mult))
                    chain(nc.vector.tensor_scalar(poly[:], s2[:], 2.0 / 17, 2.0 / 15, ALU.mult, ALU.add))
                    for k in (13, 11, 9, 7, 5, 3, 1):
                        chain(nc.vector.tensor_tensor(poly[:], poly[:], s2[:], ALU.mult))
                        chain(nc.vector.tensor_scalar(poly[:], poly[:], 2.0 / k, None, ALU.add))
                    chain(nc.vector.tensor_tensor(poly[:], poly[:], z[:], ALU.mult))
                    chain(nc.vector.tensor_scalar(pos[:], lam, -1.0, 0.0, ALU.mult, ALU.max))
                    chain(nc.vector.tensor_tensor(poly[:], poly[:], pos[:], ALU.add))
                    chain(nc.vector.tensor_scalar(poly[:], poly[:], -8.0, None, ALU.mult))
                    dve.wait_ge(act_s, 4)
                    for n in range(2):
                        nc.vector.tensor_scalar(r[:, n, :], r[:, n, :], poly[:, n:n + 1], None, ALU.mult).then_inc(loga, 1)
                    chain(nc.vector.tensor_tensor(flat(u), flat(i_), flat(xc), ALU.mult))
                    dve.wait_ge(tanh_done, 1)
                    chain(nc.vector.tensor_scalar(flat(mult), flat(th), -1.0, 1.0, ALU.mult, ALU.add))
                    chain(nc.vector.reciprocal(flat(mult), flat(mult)))
                    chain(nc.vector.scalar_tensor_tensor(out=flat(mult), in0=flat(th), scalar=-2.0, in1=flat(mult),
                                                         op0=ALU.mult, op1=ALU.mult))
                    nc.vector.tensor_scalar(flat(mult), flat(mult), 1e-30, None, ALU.max).then_inc(mult_in, 1)
                    dve.wait_ge(rooted, 1)
                    chain(nc.vector.memset(mult[:, :, 0:1], 1.0))
                    chain(nc.vector.tensor_tensor(flat(u), flat(u), flat(mult), ALU.mult))
                    for n in range(2):
                        nc.vector.tensor_tensor_scan(mult[:, n, :], a[:, n, :], u[:, n, :], 0.0, ALU.mult, ALU.add)\
                            .then_inc(hid, 1)
                    dve.wait_ge(hid, 2)
                    dve.wait_ge(gelu, 1)
                    nc.vector.tensor_tensor(self.hT[:, 4:6, :], mult[:], th[:], ALU.mult).then_inc(hid, 1)
                    dve.wait_ge(pool_s, 1)
                    for n in range(2):
                        chain(nc.vector.tensor_scalar(cv[:, n, :], pr[:, n, :], w3(2, n), None, ALU.mult))
                        for k in range(2):
                            d = 2 - k
                            chain(nc.vector.scalar_tensor_tensor(out=cv[:, n, d:], in0=pr[:, n, 0:S - d], scalar=w3(k, n),
                                                                 in1=cv[:, n, d:], op0=ALU.mult, op1=ALU.add))
                    nc.vector.tensor_tensor(self.hT[:, 6:8, :], cv[:], proj[:, SB0:SB0 + 2, :], ALU.mult).then_inc(hid, 1)

                @block.gpsimd
                def _(pool):
                    nc.gpsimd.tensor_tensor(pr[:], proj[:, SC0:SC0 + 2, :], proj[:, SX0:SX0 + 2, :], ALU.mult)\
                        .then_inc(pool_s, 1)

                @block.tensor
                def _(pe):
                    pe.wait_ge(loaded, 32)
                    pe.wait_ge(conv_done, 1)
                    for g, w in enumerate((wa, wx)):
                        for n in range(2):
                            nc.tensor.matmul(ps[:, 2 * g + n, :], w[:, n, :], xc[:, n, :], start=True, stop=True)\
                                .then_inc(gates_ps, 1)

                @block.scalar
                def _(act):
                    nc.scalar.activation(e[:], two("lam"), ACT.Abs).then_inc(act_s, 1)
                    act.wait_ge(act_s, 1)
                    nc.scalar.activation(e[:], e[:], ACT.Exp, scale=-1.0).then_inc(abs_done, 1)
                    for g, (out, name) in enumerate(((r, "gate_a_b"), (i_, "gate_x_b"))):
                        for n in range(2):
                            act.wait_ge(gates_ps, 2 * g + n + 1)
                            ins = nc.scalar.activation(out[:, n, :], ps[:, 2 * g + n, :], ACT.Sigmoid,
                                                       bias=two(name)[:, n:n + 1])
                            if g or n:
                                ins.then_inc(act_s, 1)
                    act.wait_ge(loga, 2)
                    nc.scalar.activation(flat(th), flat(r), ACT.Tanh).then_inc(tanh_done, 1)
                    nc.scalar.activation(flat(a), flat(r), ACT.Exp).then_inc(tanh_done, 1)
                    act.wait_ge(mult_in, 1)
                    nc.scalar.activation(flat(mult), flat(mult), ACT.Sqrt).then_inc(rooted, 1)
                    nc.scalar.activation(th[:], proj[:, LG0:LG0 + 2, :], ACT.Gelu_apprx_tanh).then_inc(gelu, 1)

    def store(self, out_T):
        nc = self.nc
        with self.stage("store"):
            stored = self.sem("stored")
            with nc.Block() as block:
                @block.sync
                def _(sp):
                    sp.dma_start(self.t["out"].rearrange("(n p) t -> p n t", p=P), out_T[:]).then_inc(stored, 16)
                    sp.wait_ge(stored, 16)

    def moe(self):
        nc = self.nc
        h_rows, y_rows = self.h_rows, self.y_rows
        with ExitStack() as ctx:
            tile = lambda name, shape, dt=F32: ctx.enter_context(nc.sbuf_tensor(name, shape, dt))
            self.hT = tile("hT_m", [P, KD, S])
            self.norm(self.hT, self.v("norm2_g"), scale=self.mod[:, 32:40], shift=self.mod[:, 24:32])
            dest, w8 = tile("dest", [P, TT, TOPK], U32), tile("w8", [P, TT, TOPK])
            row_tokens = tile("row_tokens", [P, NBLK], U32)
            block_expert, used_pairs = tile("block_expert", [1, P], I32), tile("used_pairs", [1, 1], I32)
            self.rows_out(h_rows)
            self.route(dest, w8, row_tokens, block_expert, used_pairs)
            self.experts(h_rows, y_rows, row_tokens, block_expert, used_pairs)
            self.shared_expert()
            self.combine(y_rows, dest, w8)

    def rows_out(self, h_rows):
        nc = self.nc
        with self.stage("rows"):
            rows = self.sb("rows", [P, TT, D])
            ps = self.psum("ps", 8)
            turned, copied, stored = self.sems("turned copied stored")
            with nc.Block() as block:
                @block.tensor
                def _(pe):
                    for c in range(TT):
                        for k in range(KD):
                            mm = nc.tensor.transpose(ps[:, 2 * c + k // 4, (k % 4) * P:(k % 4 + 1) * P],
                                                     self.hT[:, k, c * P:(c + 1) * P], self.c("ident"))
                        mm.then_inc(turned, 1)

                @block.scalar
                def _(act):
                    for c in range(TT):
                        act.wait_ge(turned, c + 1)
                        nc.scalar.activation(rows[:, c, :].rearrange("p (b n) -> p b n", b=2), ps[:, 2 * c:2 * c + 2, :], ACT.Copy)\
                            .then_inc(copied, 1)

                @block.sync
                def _(sp):
                    for c in range(TT):
                        sp.wait_ge(copied, c + 1)
                        sp.dma_start(h_rows[c * P:(c + 1) * P, :], rows[:, c, :]).then_inc(stored, 16)
                    sp.wait_ge(stored, 16 * TT)

    def route(self, dest, w8, row_tokens, block_expert, used_pairs):
        nc = self.nc
        M = TT * E
        table = nc.dram_tensor("row_table", (BLK * NBLK, 1), U32).ap()
        expert_column = nc.dram_tensor("expert_column", (1, P), I32).ap()
        with self.stage("route"):
            wr = self.sb("wr", [P, KD, E])
            score, choice, rep, picked, w, place, row = (self.sb(x, [P, TT, E]) for x in
                                                         "score choice rep picked w place row".split())
            top = self.sb("top", [P, TT * GROUPS, 8])
            gs, rank = self.sb("gs", [P, TT, GROUPS]), self.sb("rank", [P, TT, GROUPS])
            above, tie = self.sb("above", [P, TT, 8, 8]), self.sb("tie", [P, TT, 8, 8])
            v8, d8 = self.sb("v8", [P, TT, 8]), self.sb("d8", [P, TT, 8])
            tot = self.sb("tot", [P, TT])
            cnt, nb, incl, first = (self.sb(x, [P, E]) for x in "cnt nb incl first".split())
            junk, eb = self.sb("junk", [P, E]), self.sb("eb", [P, 1])
            ebi = self.sb("ebi", [P, 1], I32)
            half, rest = self.sb("half", [P, 1]), self.sb("rest", [P, NBLK // 2])
            zero, tok = self.sb("zero", [P, NBLK], U32), self.sb("tok", [P, TT], U32)
            ps = self.psum("ps", 3)
            loaded, logits, scored, chain_s, zeroed, picked_s, places, ready, table_zero, scattered, experts_out, back = self.sems(
                "loaded logits scored chain zeroed picked places ready table_zero scattered experts_out back")
            cut = lambda x: x[:].rearrange("p c e -> p (c e)")
            with nc.Block() as block:
                @block.sync
                def _(sp):
                    sp.dma_start(wr[:], self.t["router_w"]).then_inc(loaded, 16)
                    sp.wait_ge(zeroed, 1)
                    sp.dma_start(table.rearrange("(p b) a -> p (b a)", b=NBLK), zero[:]).then_inc(table_zero, 16)
                    sp.wait_ge(ready, 1)
                    sp.dma_start(expert_column.rearrange("a p -> p a"), ebi[:]).then_inc(experts_out, 16)
                    sp.wait_ge(experts_out, 16)
                    sp.dma_start(block_expert[:], expert_column).then_inc(back, 16)
                    sp.wait_ge(scattered, 16 * TT * TOPK)
                    sp.dma_start(row_tokens[:], table.rearrange("(p b) a -> p (b a)", b=NBLK)).then_inc(back, 16)
                    sp.wait_ge(back, 32)

                @block.tensor
                def _(pe):
                    pe.wait_ge(loaded, 16)
                    for c in range(TT):
                        for k in range(KD):
                            mm = nc.tensor.matmul(ps[:, 0, c * E:(c + 1) * E], self.hT[:, k, c * P:(c + 1) * P], wr[:, k, :],
                                                  start=k == 0, stop=k == KD - 1)
                    mm.then_inc(logits, 1)
                    pe.wait_ge(picked_s, 1)
                    for c in range(TT):
                        for a in range(c):
                            nc.tensor.matmul(ps[:, 1, c * E:(c + 1) * E], self.ones[:], picked[:, a, :], start=a == 0, stop=False)
                        nc.tensor.matmul(ps[:, 1, c * E:(c + 1) * E], self.c("before"), picked[:, c, :], start=c == 0, stop=True)
                    for a in range(TT):
                        mm = nc.tensor.matmul(ps[:, 2, 0:E], self.ones[:], picked[:, a, :], start=a == 0, stop=a == TT - 1)
                    mm.then_inc(places, 1)

                @block.scalar
                def _(act):
                    act.wait_ge(logits, 1)
                    nc.scalar.activation(cut(score), ps[:, 0, 0:M], ACT.Sigmoid).then_inc(scored, 1)

                @block.gpsimd
                def _(pool):
                    nc.gpsimd.memset(zero[:], 0).then_inc(zeroed, 1)
                    pool.wait_ge(table_zero, 16)
                    pool.wait_ge(ready, 1)
                    for c in range(TT):
                        for k in range(TOPK):
                            nc.gpsimd.indirect_dma_start(
                                out=table, out_offset=bass.IndirectOffsetOnAxis(ap=dest[:, c, k:k + 1], axis=0),
                                in_=tok[:, c:c + 1], in_offset=None).then_inc(scattered, 16)

                @block.vector
                def _(dve):
                    chain = Chain(dve, chain_s)
                    v = nc.vector
                    chain(v.tensor_copy(tok[:], self.c("tokens")))
                    dve.wait_ge(scored, 1)
                    bias = self.v("router_bias").unsqueeze(1).broadcast_to([P, TT, E])
                    chain(v.tensor_tensor(choice[:], score[:], bias, ALU.add))
                    for c in range(TT):
                        for g in range(GROUPS):
                            ins = v.max(top[:, c * GROUPS + g, :], choice[:, c, g * 8:(g + 1) * 8])
                    chain(ins)
                    chain(v.tensor_tensor(gs[:].rearrange("p c g -> p (c g)"), top[:, :, 0], top[:, :, 1], ALU.add))
                    other = gs[:].unsqueeze(2).broadcast_to([P, TT, GROUPS, GROUPS])
                    own = gs[:].unsqueeze(3).broadcast_to([P, TT, GROUPS, GROUPS])
                    lower = self.c("lower8").rearrange("p (a b) -> p a b", a=8).unsqueeze(1).broadcast_to([P, TT, 8, 8])
                    chain(v.tensor_tensor(above[:], other, own, ALU.is_gt))
                    chain(v.tensor_tensor(tie[:], other, own, ALU.is_equal))
                    chain(v.tensor_tensor(tie[:], tie[:], lower, ALU.mult))
                    chain(v.tensor_tensor(above[:], above[:], tie[:], ALU.add))
                    chain(v.tensor_reduce(rank[:], above[:], AX.X, ALU.add))
                    chain(v.tensor_scalar(rank[:], rank[:], float(TOPG), 1e30, ALU.is_lt, ALU.mult))
                    chain(v.tensor_scalar(rank[:], rank[:], -1e30, None, ALU.add))
                    cg = lambda x: x[:].rearrange("p c (g e) -> p (c g) e", g=GROUPS)
                    chain(v.tensor_tensor(cg(choice), cg(choice),
                                          rank[:].rearrange("p c g -> p (c g)").unsqueeze(2).broadcast_to([P, TT * GROUPS, 8]),
                                          ALU.add))
                    for c in range(TT):
                        ins = v.max(v8[:, c, :], choice[:, c, :])
                    chain(ins)
                    for c in range(TT):
                        ins = v.match_replace(rep[:, c, :], v8[:, c, :], choice[:, c, :], -3e38)
                    chain(ins)
                    chain(v.tensor_tensor(picked[:], rep[:], choice[:], ALU.not_equal))
                    dve.sem_inc(picked_s, 1)
                    chain(v.tensor_tensor(w[:], score[:], picked[:], ALU.mult))
                    chain(v.tensor_reduce(tot[:], w[:], AX.X, ALU.add))
                    chain(v.reciprocal(tot[:], tot[:]))
                    chain(v.scalar_tensor_tensor(out=w[:], in0=w[:], scalar=ROUTED_SCALE,
                                                 in1=tot[:].unsqueeze(2).broadcast_to([P, TT, E]), op0=ALU.mult, op1=ALU.mult))
                    dve.wait_ge(places, 1)
                    chain(v.tensor_copy(cnt[:], ps[:, 2, 0:E]))
                    chain(v.tensor_copy(cut(place), ps[:, 1, 0:M]))
                    chain(v.tensor_scalar(nb[:], cnt[:], 0.0, None, ALU.is_gt))
                    for j in range(1, S // BLK):
                        chain(v.scalar_tensor_tensor(out=nb[:], in0=cnt[:], scalar=float(j * BLK), in1=nb[:], op0=ALU.is_gt,
                                                     op1=ALU.add))
                    chain(v.tensor_tensor_scan(incl[:], self.ones[:, 0:E], nb[:], 0.0, ALU.mult, ALU.add))
                    chain(v.tensor_tensor(first[:], incl[:], nb[:], ALU.subtract))
                    chain(v.scalar_tensor_tensor(out=junk[:], in0=incl[:], scalar=self.c("iota"), in1=self.ones[:, 0:E],
                                                 op0=ALU.is_le, op1=ALU.mult, accum_out=eb[:]))
                    chain(v.tensor_scalar(ebi[:], eb[:], float(E - 1), None, ALU.min))
                    chain(v.tensor_scalar(half[:], incl[:, E - 1:E], 0.5, None, ALU.mult))
                    chain(v.scalar_tensor_tensor(out=rest[:], in0=self.c("pairs"), scalar=half[:], in1=self.ones[:, 0:NBLK // 2],
                                                 op0=ALU.is_lt, op1=ALU.mult, accum_out=eb[:]))
                    chain(v.tensor_copy(used_pairs[:], eb[0:1, :]))
                    chain(v.tensor_scalar(cut(row), cut(place), float(BLK), None, ALU.is_ge))
                    for j in range(2, S // BLK):
                        chain(v.scalar_tensor_tensor(out=cut(row), in0=cut(place), scalar=float(j * BLK), in1=cut(row),
                                                     op0=ALU.is_ge, op1=ALU.add))
                    chain(v.tensor_scalar(cut(row), cut(row), float(1 - BLK * NBLK), 1.0, ALU.mult, ALU.add))
                    chain(v.scalar_tensor_tensor(out=cut(row), in0=cut(place), scalar=float(NBLK), in1=cut(row),
                                                 op0=ALU.mult, op1=ALU.add))
                    chain(v.tensor_tensor(row[:], row[:], first[:].unsqueeze(1).broadcast_to([P, TT, E]), ALU.add))
                    chain(v.tensor_tensor(row[:], row[:], picked[:], ALU.mult))
                    for c in range(TT):
                        ins = v.max(d8[:, c, :], row[:, c, :])
                    chain(ins)
                    chain(v.tensor_scalar(dest[:], d8[:], -1.0, None, ALU.add))
                    dve.sem_inc(ready, 1)
                    for c in range(TT):
                        for k in range(TOPK):
                            chain(v.scalar_tensor_tensor(out=junk[:], in0=row[:, c, :], scalar=d8[:, c, k:k + 1], in1=w[:, c, :],
                                                         op0=ALU.is_equal, op1=ALU.mult, accum_out=w8[:, c, k:k + 1]))

    def experts(self, h_rows, y_rows, row_tokens, block_expert, used_pairs):
        nc, t = self.nc, self.t
        R = NBLK // 2
        with self.stage("experts"):
            wg, wd = self.sb("wg", [P, 2, KD, 2 * EH]), self.sb("wd", [P, 2, 2, D])
            xg, xt = self.sb("xg", [P, 2, D]), self.sb("xt", [P, 2, D])
            idx0, idx1 = self.sb("idx0", [P, 1], U32), self.sb("idx1", [P, 1], U32)
            idx = [idx0, idx1]
            sg, hx, ht, y = self.sb("sg", [P, 2, EH]), self.sb("hx", [P, 2, EH]), self.sb("ht", [P, 2, EH]), self.sb("y", [P, 2, D])
            psX, psG, psH, psY = self.psum("x", 2), self.psum("g", 2), self.psum("h", 1), self.psum("y", 2)
            slot = lambda name: [self.sem(f"{name}{s}") for s in range(2)]
            wg_in, wd_in, gathered, stored = slot("wg_loaded"), slot("wd_loaded"), slot("gathered"), slot("stored")
            idx_ready, idx_seen, x_turned, x_copied, gu_done, silu_done, hid_done, h_turned, h_copied, y_done, y_low, y_high, rows_stored = self.sems(
                "idx_ready idx_seen x_turned x_copied gu_done silu_done hid_done h_turned h_copied y_done y_low y_high rows_stored")
            out_rows = y_rows.rearrange("(p b) d -> p b d", b=NBLK)
            ident = self.c("ident")

            def used(eng):
                return eng.value_load(used_pairs[0:1, 0:1], min_val=S * TOPK // BLK // 2, max_val=R)

            def pipelined(eng, *steps):
                pairs = used(eng)
                for n in range(2):
                    for ahead, step in sorted(steps, key=lambda x: x[0] == 1):
                        if n < ahead:
                            step(0, n)
                with eng.Fori(0, R) as r:
                    with eng.If(r < pairs):
                        for s in range(2):
                            for ahead, step in steps:
                                if s + ahead < 2:
                                    step(r, s + ahead)
                                else:
                                    with eng.If(r + 1 < pairs):
                                        step(r + 1, (s + ahead) % 2)
                return pairs

            with nc.Block() as block:
                @block.sync
                def _(sp):
                    def load(r, s, again=True):
                        n = 2 * r + s
                        e = sp.value_load(block_expert[0:1, bass.ds(n, 1)], min_val=0, max_val=E - 1)
                        if again:
                            sp.wait_ge(gu_done, n - 1)
                        sp.dma_start(wg[:, s], t["exp_gu"][bass.ds(e, 1)].rearrange("a p k n -> (a p) k n"))\
                            .then_inc(wg_in[s], 16)
                        if again:
                            sp.wait_ge(y_done, n - 1)
                        sp.dma_start(wd[:, s], t["exp_dn"][bass.ds(e, 1)].rearrange("a p k n -> (a p) k n"))\
                            .then_inc(wd_in[s], 16)
                    load(0, 0, again=False)
                    load(0, 1, again=False)
                    pairs = used(sp)
                    with sp.Fori(1, R) as r:
                        with sp.If(r < pairs):
                            load(r, 0)
                            load(r, 1)

                @block.gpsimd
                def _(pool):
                    def gather(r, s, again=True):
                        n = 2 * r + s
                        if again:
                            pool.wait_ge(x_turned, n - 1)
                        nc.gpsimd.tensor_copy(idx[s][:], row_tokens[:, bass.ds(n, 1)]).then_inc(idx_ready, 1)
                        pool.wait_ge(idx_ready, n + 1)
                        pool.sem_inc(idx_seen, 1)
                        nc.gpsimd.indirect_dma_start(out=xg[:, s, :], out_offset=None, in_=h_rows,
                                                     in_offset=bass.IndirectOffsetOnAxis(ap=idx[s][:, 0:1], axis=0))\
                            .then_inc(gathered[s], 16)
                    gather(0, 0, again=False)
                    gather(0, 1, again=False)
                    pairs = used(pool)
                    with pool.Fori(1, R) as r:
                        with pool.If(r < pairs):
                            gather(r, 0)
                            gather(r, 1)

                @block.tensor
                def _(pe):
                    def turn_x(r, s):
                        n = 2 * r + s
                        pe.wait_ge(gathered[s], 16 * (r + 1))
                        pe.wait_ge(x_copied, n + 1)
                        for k in range(KD):
                            mm = nc.tensor.transpose(psX[:, k // 4, (k % 4) * P:(k % 4 + 1) * P], xg[:, s, k * P:(k + 1) * P], ident)
                        mm.then_inc(x_turned, 1)

                    def gate_up(r, s):
                        n = 2 * r + s
                        pe.wait_ge(x_copied, n + 2)
                        pe.wait_ge(wg_in[s], 16 * (r + 1))
                        for k in range(KD):
                            mm = nc.tensor.matmul(psG[:, s, :], xt[:, s, k * P:(k + 1) * P], wg[:, s, k, :], start=k == 0,
                                                  stop=k == KD - 1)
                        mm.then_inc(gu_done, 1)

                    def turn_h(r, s):
                        pe.wait_ge(hid_done, 2 * r + s + 1)
                        for k in range(2):
                            mm = nc.tensor.transpose(psH[:, 0, k * P:(k + 1) * P], hx[:, s, k * P:(k + 1) * P], ident)
                        mm.then_inc(h_turned, 1)

                    def down(r, s):
                        n = 2 * r + s
                        pe.wait_ge(wd_in[s], 16 * (r + 1))
                        pe.wait_ge(h_copied, n + 1)
                        pe.wait_ge(y_low, n + 1)
                        pe.wait_ge(y_high, n + 1)
                        for half in range(2):
                            for k in range(2):
                                mm = nc.tensor.matmul(psY[:, half, :], ht[:, s, k * P:(k + 1) * P], wd[:, s, k, half * S:(half + 1) * S],
                                                      start=k == 0, stop=k == 1)
                        mm.then_inc(y_done, 1)
                    pipelined(pe, (1, gate_up), (0, turn_h), (2, turn_x), (0, down))

                @block.scalar
                def _(act):
                    act.sem_inc(x_copied, 1)
                    act.sem_inc(y_high, 1)
                    for s in range(2):
                        act.sem_inc(stored[s], 16)

                    def silu(r, s):
                        act.wait_ge(gu_done, 2 * r + s + 1)
                        nc.scalar.activation(sg[:, s, :], psG[:, s, 0:EH], ACT.Silu).then_inc(silu_done, 1)

                    def copy_x(r, s):
                        act.wait_ge(x_turned, 2 * r + s + 1)
                        nc.scalar.activation(xt[:, s, :].rearrange("p (b n) -> p b n", b=2), psX[:], ACT.Copy).then_inc(x_copied, 1)

                    def store_y(r, s):
                        n = 2 * r + s
                        act.wait_ge(y_done, n + 1)
                        act.wait_ge(stored[s], 16 * (r + 1))
                        nc.scalar.activation(y[:, s, S:D], psY[:, 1, :], ACT.Copy).then_inc(y_high, 1)
                        act.wait_ge(y_high, n + 2)
                        act.wait_ge(y_low, n + 2)
                        act.dma_start(out_rows[:, bass.ds(n, 1), :].rearrange("p a d -> p (a d)"), y[:, s, :]).then_inc(stored[s], 16)
                    pairs = pipelined(act, (1, silu), (2, copy_x), (0, store_y))
                    for s in range(2):
                        act.wait_ge(stored[s], 16 * pairs + 16)
                        act.sem_inc(rows_stored, 1)

                @block.vector
                def _(dve):
                    dve.sem_inc(y_low, 1)

                    def copy_h(r, s):
                        dve.wait_ge(h_turned, 2 * r + s + 1)
                        nc.vector.tensor_copy(ht[:, s, :], psH[:, 0, 0:EH]).then_inc(h_copied, 1)

                    def hidden(r, s):
                        dve.wait_ge(silu_done, 2 * r + s + 1)
                        nc.vector.tensor_tensor(hx[:, s, :], sg[:, s, :], psG[:, s, EH:2 * EH], ALU.mult).then_inc(hid_done, 1)

                    def copy_y(r, s):
                        dve.wait_ge(y_done, 2 * r + s + 1)
                        dve.wait_ge(stored[s], 16 * (r + 1))
                        nc.vector.tensor_copy(y[:, s, 0:S], psY[:, 0, :]).then_inc(y_low, 1)
                    pipelined(dve, (0, copy_h), (1, hidden), (0, copy_y))

    def shared_expert(self):
        nc, xT, hT, gate = self.nc, self.xT, self.hT, self.mod[:, 40:48]
        with self.stage("shared"):
            wg, wd = self.sb("wg", [P, KD, 2 * EH]), self.sb("wd", [P, 2, D])
            sg, hid = self.sb("sg", [P, 2, S]), self.sb("hid", [P, 2, S])
            ps = self.psum("ps", 8)
            loaded, up, silu, hidden, down, added = self.sems("loaded up_done silu_done hidden_done down_done added")
            with nc.Block() as block:
                @block.sync
                def _(sp):
                    sp.dma_start(wg[:], self.t["sh_gu"]).then_inc(loaded, 16)
                    sp.dma_start(wd[:], self.t["sh_dn"]).then_inc(loaded, 16)

                @block.tensor
                def _(pe):
                    pe.wait_ge(loaded, 32)
                    for i in (0, 2, 1, 3):
                        for k in range(KD):
                            mm = nc.tensor.matmul(ps[:, i, :], wg[:, k, i * P:(i + 1) * P], hT[:, k, :], start=k == 0, stop=k == KD - 1)
                        mm.then_inc(up, 1)
                    pe.wait_ge(hidden, 2)
                    for n in (4, 5, 6, 7, 0, 1, 2, 3):
                        for k in range(2):
                            mm = nc.tensor.matmul(ps[:, n, :], wd[:, k, n * P:(n + 1) * P], hid[:, k, :], start=k == 0, stop=k == 1)
                        mm.then_inc(down, 1)

                @block.scalar
                def _(act):
                    for i in range(2):
                        act.wait_ge(up, 2 * i + 1)
                        nc.scalar.activation(sg[:, i, :], ps[:, i, :], ACT.Silu).then_inc(silu, 1)

                @block.vector
                def _(dve):
                    for i in range(2):
                        dve.wait_ge(up, 2 * i + 2)
                        dve.wait_ge(silu, i + 1)
                        nc.vector.tensor_tensor(hid[:, i, :], sg[:, i, :], ps[:, 2 + i, :], ALU.mult).then_inc(hidden, 1)
                    for i, n in enumerate((4, 5, 6, 7, 0, 1, 2, 3)):
                        dve.wait_ge(down, i + 1)
                        nc.vector.scalar_tensor_tensor(out=xT[:, n, :], in0=ps[:, n, :], scalar=gate[:, n:n + 1],
                                                       in1=xT[:, n, :], op0=ALU.mult, op1=ALU.add).then_inc(added, 1)

    def combine(self, y_rows, dest, w8):
        nc, xT, gate = self.nc, self.xT, self.mod[:, 40:48]
        SLOTS = 4
        with self.stage("combine"):
            g, acc = self.sb("g", [P, SLOTS, D]), self.sb("acc", [P, 2, D])
            ps = self.psum("ps", 4)
            gathered = [self.sem(f"gathered{s}") for s in range(SLOTS)]
            summed, turned, added = self.sems("summed turned added")
            with nc.Block() as block:
                @block.gpsimd
                def _(pool):
                    for i in range(TT * TOPK):
                        if i >= SLOTS:
                            pool.wait_ge(summed, i - SLOTS + 1)
                        nc.gpsimd.indirect_dma_start(
                            out=g[:, i % SLOTS, :], out_offset=None, in_=y_rows,
                            in_offset=bass.IndirectOffsetOnAxis(ap=dest[:, i // TOPK, i % TOPK:i % TOPK + 1], axis=0))\
                            .then_inc(gathered[i % SLOTS], 16)

                @block.vector
                def _(dve):
                    def into_x(c):
                        dve.wait_ge(turned, c + 1)
                        for n in range(KD):
                            o = xT[:, n, c * P:(c + 1) * P]
                            nc.vector.scalar_tensor_tensor(out=o, in0=ps[:, 2 * (c % 2) + n // 4, (n % 4) * P:(n % 4 + 1) * P],
                                                           scalar=gate[:, n:n + 1], in1=o, op0=ALU.mult, op1=ALU.add)\
                                .then_inc(added, 1)
                    for c in range(TT):
                        a = acc[:, c % 2, :]
                        for k in range(TOPK):
                            i = c * TOPK + k
                            dve.wait_ge(gathered[i % SLOTS], 16 * (i // SLOTS + 1))
                            if k == 0:
                                nc.vector.tensor_scalar(a, g[:, i % SLOTS, :], w8[:, c, 0:1], None, ALU.mult).then_inc(summed, 1)
                            else:
                                dve.wait_ge(summed, i)
                                nc.vector.scalar_tensor_tensor(out=a, in0=g[:, i % SLOTS, :], scalar=w8[:, c, k:k + 1], in1=a,
                                                               op0=ALU.mult, op1=ALU.add).then_inc(summed, 1)
                        if c:
                            into_x(c - 1)
                    into_x(TT - 1)

                @block.tensor
                def _(pe):
                    for c in range(TT):
                        pe.wait_ge(summed, TOPK * (c + 1))
                        if c >= 2:
                            pe.wait_ge(added, KD * (c - 1))
                        for n in range(KD):
                            mm = nc.tensor.transpose(ps[:, 2 * (c % 2) + n // 4, (n % 4) * P:(n % 4 + 1) * P],
                                                     acc[:, c % 2, n * P:(n + 1) * P], self.c("ident"))
                        mm.then_inc(turned, 1)


def vec_cols(x):
    x = np.asarray(x)
    return np.ascontiguousarray(x.reshape(-1, P).T)


def pair_groups(w):
    k, n = w.shape
    return np.ascontiguousarray(w.reshape(k // P, P, n // 256, 256).transpose(2, 1, 0, 3))


def constants():
    f = np.float32
    a = np.zeros((P, NCON), f)

    def put(name, x):
        lo, hi = CON[name]
        a[:, lo:hi] = x
    p = np.arange(P)
    put("ident", np.eye(P))
    put("before", p[:, None] < p[None, :])
    rot = np.zeros((P, P))
    for m in range(P):
        if m % 64 < 32:
            rot[m + 32, m] = -1.0
        else:
            rot[m - 32, m] = 1.0
    put("rot", rot)
    inv = (f(10000.0) ** (-np.arange(32, dtype=f) / f(32))).astype(f)
    ang = np.arange(S, dtype=f)[None, :] * inv[p % 32][:, None]
    put("cos", np.cos(ang))
    put("sin", np.sin(ang))
    levels = np.zeros((P, 8, P))
    for i in range(7):
        m = 64 >> i
        s, t = p[:, None], p[None, :]
        levels[:, i] = (s // (2 * m) == t // (2 * m)) & (s % (2 * m) < m) & (t % (2 * m) >= m)
    levels[:, 7] = np.eye(P)
    put("levels", levels.reshape(P, -1))
    put("causal", np.where(p[None, :] <= p[:, None], 0.0, NEG))
    tok = np.arange(TT)[None, :, None] * P + p[:, None, None]
    seen = np.arange(N_CMP)[None, None, :] * CMP_STRIDE + CMP_BLOCK - 1 <= tok
    put("cmp_add", np.where(seen, 0.0, NEG).reshape(P, -1))
    put("cmp_keep", seen[:, 0])
    g = np.arange(8)
    put("lower8", np.broadcast_to((g[None, :] < g[:, None]).reshape(1, 64), (P, 64)))
    put("iota", p[:, None])
    put("tokens", tok[:, :, 0])
    put("pairs", np.arange(NBLK // 2)[None, :])
    return a


def alibi():
    slopes = (2.0 ** (-8.0 * np.arange(1, 9) / 8)).astype(np.float32)
    dist = np.arange(P)[:, None] + P - np.arange(2 * P)[None, :]
    out = np.empty((P, 8, 2 * P), np.float32)
    for i in range(8):
        h = (i % 2) * 4 + i // 2
        out[:, i] = np.where((dist >= 0) & (dist < P), -slopes[h] * dist.astype(np.float32), np.float32(NEG))
    return out


PAIRED = np.concatenate([np.arange(64) + 64 * (4 * g + j) for j in range(4) for g in range(2)])


def layout(i):
    i = {k: np.asarray(v) for k, v in i.items()}
    w = i["w_in"][0]
    at = np.cumsum([0, 512, 512, 512, 512, 512, 128, 128, 128, 128, 128, 128, 24])
    hq, hf, hi, hgt, nq, kc, vc, ks, vs, kw, vw, ng = (w[:, at[n]:at[n + 1]] for n in range(12))
    fm = np.concatenate([hq, hf, hgt, nq[:, PAIRED], kc, vc, ks, kw, hi, vs, vw], axis=1)
    a = {"xT": np.ascontiguousarray(i["x"][0].T), "w_ada": i["w_ada"][0], "w_in": pair_groups(fm),
         "w_gates": np.ascontiguousarray(ng.reshape(KD, P, 24).transpose(1, 0, 2))}
    wo = i["w_out"][0]
    a["w_out"] = pair_groups(np.concatenate([wo[:512], wo[512:][PAIRED]]))
    for x in "kv":
        w1 = i[f"cmp_w1_{x}"][0].reshape(2, 16, 64, 256)
        a[f"w1_{x}"] = np.ascontiguousarray(w1.transpose(0, 2, 1, 3).reshape(P, 16, 256))
        a[f"w2_{x}"] = np.ascontiguousarray(i[f"cmp_w2_{x}"][0].reshape(2, P, 64).transpose(1, 0, 2))
        a[f"pos_{x}"] = np.ascontiguousarray(i[f"cmp_pos_{x}"][0].reshape(2, 16, 64).transpose(0, 2, 1).reshape(P, 16))
    a["router_w"] = np.ascontiguousarray(i["router_w"][0].reshape(KD, P, E).transpose(1, 0, 2))
    a["exp_gu"] = np.ascontiguousarray(i["w_exp_gu"][0].reshape(E, KD, P, 2 * EH).transpose(0, 2, 1, 3))
    a["exp_dn"] = np.ascontiguousarray(i["w_exp_dn"][0].reshape(E, 2, P, D).transpose(0, 2, 1, 3))
    a["sh_gu"] = np.ascontiguousarray(i["w_sh_gu"][0].reshape(KD, P, 2 * EH).transpose(1, 0, 2))
    a["sh_dn"] = np.ascontiguousarray(i["w_sh_dn"][0].reshape(2, P, D).transpose(1, 0, 2))
    a["w_mod"] = i["w_mod_2"]
    for n in (1, 2):
        gu = i[f"w_ffn{n}_gu_2"].reshape(2, KD, P, 2, FT, P)
        a[f"ffn{n}_gu"] = np.ascontiguousarray(gu.transpose(0, 4, 2, 1, 3, 5).reshape(2, FT, P, KD, 2 * P))
        a[f"ffn{n}_dn"] = np.ascontiguousarray(i[f"w_ffn{n}_down_2"].reshape(2, FT, P, D))
    at = np.cumsum([0, 512, 128, 128, 256, 256, 256, 256, 256])
    a["w_in_2"] = np.stack([pair_groups(np.concatenate([x[:, :512][:, PAIRED], x[:, 512:]], axis=1)) for x in i["w_in_2"]])
    a["w_out_2"] = np.stack([pair_groups(np.concatenate([x[:512][PAIRED], x[512:]])) for x in i["w_out_2"]])
    for x in "ax":
        g = i[f"lru_gate_{x}_w_2"]
        b = np.zeros((2, P, 2, P), g.dtype)
        for h in range(4):
            r = slice(64 * (h % 2), 64 * (h % 2) + 64)
            b[:, r, h // 2, r] = g[:, h]
        a[f"gate_{x}"] = b
    vecs = {
        "c": i["c"][0], "b_ada": i["b_ada"][0], "norm1_g": i["norm1_g"][0], "lb0": i["hg_lb_logits"][0],
        "lb1": i["hg_lb_logits"][1], "hg_norm_g": i["hg_norm_g"][0], "b1_k": i["cmp_b1_k"][0], "b1_v": i["cmp_b1_v"][0],
        "norm2_g": i["norm2_g"][0], "final_g": i["final_g"], "c_2": i["c_2"][0], "b_mod0": i["b_mod_2"][0],
        "b_mod1": i["b_mod_2"][1], "g_norm": i["g_norm_2"], "conv_w": i["lru_conv_w_2"], "conv_b": i["lru_conv_b_2"],
        "gate_a_b": i["lru_gate_a_b_2"], "gate_x_b": i["lru_gate_x_b_2"], "lam": i["lru_lambda_2"],
        "sc_conv_w": i["sc_conv_w_2"], "g_final": i["g_final_2"],
    }
    cols = [vec_cols(vecs[name]) for name, _ in VEC_COLS[:-2]]
    order = [4 * (n % 2) + n // 2 for n in range(8)]
    for row in (i["router_bias"][0], i["attn_sinks_2"][:, order].reshape(-1)):
        cols.append(np.broadcast_to(row[None, :], (P, row.size)))
    a["vecs"] = np.ascontiguousarray(np.concatenate(cols, axis=1))
    a["consts"] = constants()
    a["alibi"] = alibi()
    return a


def build(nc, t, stop=None):
    k = Kernel(nc, t)
    k.setup()
    first = 16
    k.modulation(t["w_ada"][:, 0:first * P], k.v("c"), k.v("b_ada", 0, first), first)
    k.first_mixer()
    if stop:
        return k
    k.moe()
    k.norm(k.xT, k.v("final_g"))
    for layer in range(2):
        k.mod = k.mods[1 - layer]
        a, b = 5 * Modulation.CHUNK, 5 * Modulation.CHUNK // P
        beside = (t["w_mod"][1][:, 0:a], k.v("c_2"), k.v("b_mod1", 0, b), k.mods[0][:, 0:b], 5) if layer == 0 else None
        k.feed_forward(layer, 0, t["ffn1_gu"][layer], t["ffn1_dn"][layer], beside)
        k.second_mixer(layer)
        beside = (t["w_mod"][1][:, a:], k.v("c_2"), k.v("b_mod1", b), k.mods[0][:, b:], 4) if layer == 0 else None
        k.feed_forward(layer, 2, t["ffn2_gu"][layer], t["ffn2_dn"][layer], beside)
    with nc.sbuf_tensor("out_T", [P, KD, S], F32) as out_T:
        k.norm(out_T, k.v("g_final"))
        k.store(out_T)
    return k


def kernel(**inputs):
    import concourse.bacc as bacc
    from concourse.bass_utils import run_bass_kernel_spmd

    nc = bacc.Bacc("TRN2", target_bir_lowering=False, num_devices=1)
    arrays = layout(inputs)
    t = {name: nc.dram_tensor("in_" + name, a.shape, mybir.dt.from_np(a.dtype), kind="ExternalInput").ap()
         for name, a in arrays.items()}
    t["out"] = nc.dram_tensor("out", (D, S), F32, kind="ExternalOutput").ap()
    build(nc, t)
    result = run_bass_kernel_spmd(nc, [{"in_" + name: a for name, a in arrays.items()}], core_ids=[0])
    return np.ascontiguousarray(result.results[0]["out"].T)[None]
```

```python
from contextlib import ExitStack, contextmanager

import numpy as np

import concourse.bass as bass
from concourse import mybir

F32 = mybir.dt.float32
F32R = mybir.dt.float32r
I32 = mybir.dt.int32
U32 = mybir.dt.uint32
ACT = mybir.ActivationFunctionType
ALU = mybir.AluOpType
AX = mybir.AxisListType

P = 128
S = 512
D = 1024
KD = D // P
TT = S // P
EPS = 1e-6
HEADS = 4
NSA_PAIRS = 4
N_CMP, CMP_STRIDE, CMP_BLOCK = 31, 16, 32
E, TOPK, GROUPS, TOPG = 64, 8, 8, 4
EH = 256
BLK = 128
NBLK = S * TOPK // BLK + E
ROUTED_SCALE = 2.5
FT = 22
NEG = -1e30
LN_FLOOR = 2.0 ** -63

Q0, F0, G0, NQ0, KC, VC, KS, KW, HI0, VS, VW = 0, 4, 8, 12, 16, 17, 18, 19, 20, 24, 25
IN_TILES = 26
AQ0, AK, AV, LX0, LG0, SB0, SC0, SX0 = 0, 4, 5, 6, 8, 10, 12, 14
IN_TILES_2 = 16

VEC_COLS = [
    ("c", 8), ("b_ada", 48), ("norm1_g", 8), ("lb0", 4), ("lb1", 4), ("hg_norm_g", 4), ("b1_k", 2), ("b1_v", 2),
    ("norm2_g", 8), ("final_g", 8), ("c_2", 8), ("b_mod0", 72), ("b_mod1", 72), ("g_norm", 48), ("conv_w", 16),
    ("conv_b", 4), ("gate_a_b", 4), ("gate_x_b", 4), ("lam", 4), ("sc_conv_w", 12), ("g_final", 8),
    ("router_bias", 64), ("sinks", 16),
]
CONST_COLS = [
    ("ident", 128), ("before", 128), ("rot", 128), ("cos", 512), ("sin", 512), ("levels", 8 * 128), ("causal", 128),
    ("cmp_add", 4 * 31), ("cmp_keep", 31), ("lower8", 64), ("iota", 1), ("tokens", 4), ("pairs", NBLK // 2),
]


def offsets(cols):
    out, at = {}, 0
    for name, n in cols:
        out[name] = (at, at + n)
        at += n
    return out, at


VEC, NVEC = offsets(VEC_COLS)
CON, NCON = offsets(CONST_COLS)


class Chain:

    def __init__(self, eng, sem, base=0):
        self.eng, self.sem, self.base, self.n = eng, sem, base, 0

    def __call__(self, ins):
        self.n += 1
        ins.then_inc(self.sem, 1)
        self.eng.wait_ge(self.sem, self.base + self.n)


def in_pairs(eng, n, body, first=0):
    if n // 2 > first:
        with eng.Fori(first, n // 2) as r:
            body(r, 0)
            body(r, 1)
    if n % 2:
        body(n // 2, 0)


class Modulation:
    CHUNK = 1024

    def __init__(self, k, w, c, b, out, ps, wk=None, slots=2):
        self.nc, self.w, self.c, self.b, self.out, self.ps, self.ones = k.nc, w, c, b, out, ps, k.ones
        self.slots = slots
        self.wk = k.sb("mod_rows", [P, slots, self.CHUNK])[:] if wk is None else wk
        self.acc, self.ca = k.sb("mod_sum", [P, self.CHUNK]), k.sb("mod_c", [P, KD])
        self.loaded = [k.sem(f"mod_loaded{s}") for s in range(slots)]
        self.c_ready, self.summed, self.turned = k.sems("mod_c_ready mod_rows_summed mod_turned")

    def start(self, act):
        self.nc.scalar.activation(self.ca[:], self.c, ACT.Silu).then_inc(self.c_ready, 1)

    def free(self, dve):
        dve.sem_inc(self.summed, self.slots)
        dve.wait_ge(self.c_ready, 1)

    def load(self, dma, g, pieces):
        for i in pieces:
            dma.wait_ge(self.summed, KD * g + i + 1)
            dma.dma_start(self.wk[:, i % self.slots, :], self.w[i * P:(i + 1) * P, bass.ds(self.CHUNK * g, self.CHUNK)])\
                .then_inc(self.loaded[i % self.slots], 16)

    def multiply(self, dve, g, pieces):
        nc, acc, ca, n = self.nc, self.acc, self.ca, self.slots
        for i in pieces:
            dve.wait_ge(self.loaded[i % n], 16 * (KD // n * g + i // n + 1))
            if i == 0:
                nc.vector.tensor_scalar(acc[:], self.wk[:, 0, :], ca[:, 0:1], None, ALU.mult).then_inc(self.summed, 1)
            else:
                dve.wait_ge(self.summed, KD * g + i + n)
                nc.vector.scalar_tensor_tensor(out=acc[:], in0=self.wk[:, i % n, :], scalar=ca[:, i:i + 1], in1=acc[:],
                                               op0=ALU.mult, op1=ALU.add).then_inc(self.summed, 1)

    def reduce(self, pe, g):
        pe.wait_ge(self.summed, KD * g + KD + self.slots)
        for i in range(self.CHUNK // P):
            mm = self.nc.tensor.matmul(self.ps[:, i:i + 1], self.acc[:, i * P:(i + 1) * P], self.ones[:, 0:1], start=True, stop=True)
        mm.then_inc(self.turned, 1)

    def finish(self, dve, g):
        n = self.CHUNK // P
        dve.wait_ge(self.turned, g + 1)
        self.nc.vector.tensor_tensor(self.out[:, bass.ds(n * g, n)], self.ps[:, 0:n], self.b[:, bass.ds(n * g, n)], ALU.add)


class Norm:
    TILES = 11

    def __init__(self, k, scratch, ps, g, scale=None, shift=None, parts=None, dst=None):
        self.k, self.nc, self.xT, self.ps = k, k.nc, k.xT, ps
        self.g, self.scale, self.shift, self.parts, self.dst = g, scale, shift, parts, dst
        self.sq, self.rstd, self.xn, self.h = scratch[0:4], scratch[4], scratch[5:8], scratch[8:11]
        (self.squared, self.paired, self.summed, self.rooted, self.inverted, self.pre_done, self.xn_ready, self.done,
         self.high_act, self.high_pool, self.low_done) = k.sems(
            "norm_squared norm_paired norm_summed norm_rooted norm_inverted norm_pre_done norm_xn_ready norm_done "
            "norm_high_by_act norm_high_by_pool norm_low_done")

    def whole(self, n):
        return self.h[n % 3] if self.dst is None else self.dst[:, n, :]

    def ready(self, pe):
        pe.wait_ge(self.low_done, KD)

    def roots(self, act):
        for n in range(KD):
            if n >= 4:
                act.wait_ge(self.summed, n // 2 - 1)
            self.nc.scalar.activation(self.sq[n % 4], self.xT[:, n, :], ACT.Square).then_inc(self.squared, 1)
        act.wait_ge(self.summed, KD // 2)
        self.nc.scalar.activation(self.rstd, self.ps, ACT.Sqrt, bias=self.k.eps[:, 0:1], scale=1.0 / D).then_inc(self.rooted, 1)

    def scaled(self, act):
        act.wait_ge(self.pre_done, 1)
        pre = self.k.pre
        for n in range(KD):
            act.wait_ge(self.xn_ready, n + 1)
            if self.dst is None and n >= 3:
                act.wait_ge(self.low_done, n - 2)
            if self.shift is None:
                self.nc.scalar.activation(self.whole(n), self.xn[n % 3], ACT.Copy, scale=pre[:, n:n + 1]).then_inc(self.done, 1)
            else:
                self.nc.scalar.activation(self.whole(n), self.xn[n % 3], ACT.Identity, bias=self.shift[:, n:n + 1],
                                          scale=pre[:, n:n + 1]).then_inc(self.done, 1)
            if self.parts and n % 3:
                act.wait_ge(self.done, n + 1)
                self.nc.scalar.activation(self.parts[0][:, n, :], self.whole(n), ACT.Copy).then_inc(self.high_act, 1)

    def sums(self, pe):
        for j in range(KD // 2):
            pe.wait_ge(self.paired, j + 1)
            self.nc.tensor.matmul(self.ps, self.k.ones[:], self.sq[2 * j % 4], start=j == 0, stop=j == KD // 2 - 1)\
                .then_inc(self.summed, 1)

    def high(self, pool):
        for n in range(0, KD, 3):
            pool.wait_ge(self.done, n + 1)
            self.nc.gpsimd.tensor_copy(self.parts[0][:, n, :], self.whole(n)).then_inc(self.high_pool, 1)

    def low(self, dve, n):
        by_pool = n // 3 + 1
        if n % 3:
            dve.wait_ge(self.high_act, n + 1 - by_pool)
        else:
            dve.wait_ge(self.high_pool, by_pool)
        self.nc.vector.tensor_tensor(self.parts[1][:, n, :], self.whole(n), self.parts[0][:, n, :].bitcast(F32), ALU.subtract)\
            .then_inc(self.low_done, 1)

    def vector(self, dve, beside=None):
        v = self.nc.vector
        if self.scale is None:
            v.tensor_copy(self.k.pre[:], self.g).then_inc(self.pre_done, 1)
        else:
            v.scalar_tensor_tensor(out=self.k.pre[:], in0=self.scale, scalar=1.0, in1=self.g, op0=ALU.add,
                                   op1=ALU.mult).then_inc(self.pre_done, 1)
        for j in range(KD // 2):
            a, b = self.sq[2 * j % 4], self.sq[2 * j % 4 + 1]
            dve.wait_ge(self.squared, 2 * j + 2)
            v.tensor_tensor(a, a, b, ALU.add).then_inc(self.paired, 1)
        dve.wait_ge(self.rooted, 1)
        v.reciprocal(self.rstd, self.rstd).then_inc(self.inverted, 1)
        dve.wait_ge(self.inverted, 1)
        for n in range(KD):
            if n >= 3:
                dve.wait_ge(self.done, n - 2)
            v.tensor_tensor(self.xn[n % 3], self.xT[:, n, :], self.rstd, ALU.mult).then_inc(self.xn_ready, 1)
            if n == 2 and beside:
                beside()
            if self.parts and n >= 3:
                self.low(dve, n - 3)
        if self.parts:
            for n in range(KD - 3, KD):
                self.low(dve, n)


class SharedExpert:

    def __init__(self, k, ps):
        self.nc, self.t, self.xT, self.hT, self.gate, self.ps = k.nc, k.t, k.xT, k.hT, k.mod[:, 40:48], ps
        self.wg, self.wd = k.sb("shared_wg", [P, KD, 2 * EH]), k.sb("shared_wd", [P, 2, D])
        self.sg, self.hid = k.sb("shared_sg", [P, 2, S]), k.sb("shared_hid", [P, 2, S])
        self.loaded, self.up, self.silu_done, self.hidden_done, self.down_done, self.added = k.sems(
            "shared_loaded shared_up_done shared_silu_done shared_hidden_done shared_down_done shared_added")

    def load(self, sp):
        sp.dma_start(self.wg[:], self.t["sh_gu"]).then_inc(self.loaded, 16)
        sp.dma_start(self.wd[:], self.t["sh_dn"]).then_inc(self.loaded, 16)

    def gate_up(self, pe, tile):
        if tile == 0:
            pe.wait_ge(self.loaded, 32)
        for i in (tile, tile + 2):
            for k in range(KD):
                mm = self.nc.tensor.matmul(self.ps[:, i, :], self.wg[:, k, i * P:(i + 1) * P], self.hT[:, k, :], start=k == 0,
                                           stop=k == KD - 1)
            mm.then_inc(self.up, 1)

    def down(self, pe):
        pe.wait_ge(self.hidden_done, 2)
        for n in range(KD):
            if n >= 4:
                pe.wait_ge(self.added, n - 3)
            for k in range(2):
                mm = self.nc.tensor.matmul(self.ps[:, n % 4, :], self.wd[:, k, n * P:(n + 1) * P], self.hid[:, k, :], start=k == 0,
                                           stop=k == 1)
            mm.then_inc(self.down_done, 1)

    def silu(self, act):
        for i in range(2):
            act.wait_ge(self.up, 2 * i + 1)
            self.nc.scalar.activation(self.sg[:, i, :], self.ps[:, i, :], ACT.Silu).then_inc(self.silu_done, 1)

    def hidden(self, dve, i):
        dve.wait_ge(self.up, 2 * i + 2)
        dve.wait_ge(self.silu_done, i + 1)
        self.nc.vector.tensor_tensor(self.hid[:, i, :], self.sg[:, i, :], self.ps[:, 2 + i, :], ALU.mult)\
            .then_inc(self.hidden_done, 1)

    def into_x(self, dve, n):
        dve.wait_ge(self.down_done, n + 1)
        self.nc.vector.scalar_tensor_tensor(out=self.xT[:, n, :], in0=self.ps[:, n % 4, :], scalar=self.gate[:, n:n + 1],
                                            in1=self.xT[:, n, :], op0=ALU.mult, op1=ALU.add).then_inc(self.added, 1)


class Kernel:
    def __init__(self, nc, t):
        self.nc, self.t = nc, t
        sb = nc.alloc_sbuf_tensor
        self.xT = sb("xT", [P, KD, S], F32)
        self.vec = sb("vec", [P, NVEC], F32)
        self.con = sb("con", [P, NCON], F32)
        self.ones = sb("ones", [P, P], F32)
        self.eps = sb("eps", [P, 1], F32)
        self.mods = sb("mod", [P, 72], F32), sb("mod_next", [P, 72], F32)
        self.mod = self.mods[0]
        self.pre = sb("pre", [P, KD], F32)

        self.stages = 0
        self.h_rows = nc.dram_tensor("h_rows", (S, D), F32).ap()
        self.y_rows = nc.dram_tensor("y_rows", (BLK * NBLK, D), F32).ap()

    @contextmanager
    def stage(self, name):
        self.stages += 1
        self.tag = f"{name}{self.stages}_"
        with self.nc.cleanup_on_exit():
            yield

    def sem(self, name):
        return self.nc.alloc_semaphore(self.tag + name)

    def sems(self, names):
        return [self.sem(n) for n in names.split()]

    def sb(self, name, shape, dt=F32):
        return self.nc.alloc_sbuf_tensor(self.tag + name, shape, dt)

    def psum(self, name, banks):
        return self.nc.alloc_psum_tensor(self.tag + name + "_psum", [P, banks, S], F32)

    def v(self, name, a=0, b=None):
        lo, hi = VEC[name]
        return self.vec[:, lo + a:(hi if b is None else lo + b)]

    def c(self, name):
        lo, hi = CON[name]
        return self.con[:, lo:hi]

    def setup(self):
        nc, t = self.nc, self.t
        with self.stage("load"):
            loaded = self.sem("loaded")
            with nc.Block() as block:
                @block.sync
                def _(sp):
                    sp.dma_start(self.vec[:], t["vecs"]).then_inc(loaded, 16)
                    sp.wait_ge(loaded, 16)

                @block.gpsimd
                def _(pool):
                    nc.gpsimd.memset(self.ones[:], 1.0)
                    nc.gpsimd.memset(self.eps[:], EPS)

    def modulation(self, w, c, b, tiles):
        nc = self.nc
        n = tiles * P
        with self.stage("mod"):
            SLOTS = 4
            wk = self.sb("wk", [P, SLOTS, n])
            acc = self.sb("acc", [P, n])
            ca = self.sb("ca", [P, KD])
            ps = self.psum("ps", 1)[:, 0, :]
            loaded = [self.sem(f"loaded{s}") for s in range(SLOTS)]
            rest_loaded = self.sem("x_and_constants_loaded")
            act_done, summed, turned = self.sems("c_ready rows_summed turned")
            with nc.Block() as block:
                @block.sync
                def _(sp):
                    for k in range(KD):
                        if k >= SLOTS:
                            sp.wait_ge(summed, k - SLOTS + 1)
                        sp.dma_start(wk[:, k % SLOTS, :], w[k * P:(k + 1) * P, :]).then_inc(loaded[k % SLOTS], 16)
                    sp.dma_start(self.xT[:], self.t["xT"].rearrange("(n p) t -> p n t", p=P)).then_inc(rest_loaded, 16)
                    sp.dma_start(self.con[:], self.t["consts"]).then_inc(rest_loaded, 16)
                    sp.wait_ge(rest_loaded, 32)

                @block.scalar
                def _(act):
                    nc.scalar.activation(ca[:], c, ACT.Silu).then_inc(act_done, 1)

                @block.vector
                def _(dve):
                    dve.wait_ge(act_done, 1)
                    for k in range(KD):
                        dve.wait_ge(loaded[k % SLOTS], 16 * (k // SLOTS + 1))
                        if k == 0:
                            nc.vector.tensor_scalar(acc[:], wk[:, 0, :], ca[:, 0:1], None, ALU.mult).then_inc(summed, 1)
                        else:
                            dve.wait_ge(summed, k)
                            nc.vector.scalar_tensor_tensor(out=acc[:], in0=wk[:, k % SLOTS, :], scalar=ca[:, k:k + 1],
                                                           in1=acc[:], op0=ALU.mult, op1=ALU.add).then_inc(summed, 1)
                    dve.wait_ge(turned, 1)
                    nc.vector.tensor_tensor(self.mod[:, 0:tiles], ps[:, 0:tiles], b, ALU.add)

                @block.tensor
                def _(pe):
                    pe.wait_ge(summed, KD)
                    for i in range(tiles):
                        last = nc.tensor.matmul(ps[:, i:i + 1], acc[:, i * P:(i + 1) * P], self.ones[:, 0:1],
                                                start=True, stop=True)
                    last.then_inc(turned, 1)

    def norm(self, dst, g, scale=None, shift=None):
        with self.stage("norm"):
            scratch, ps = self.sb("scratch", [P, Norm.TILES, S]), self.psum("ps", 1)
            norm = Norm(self, [scratch[:, n, :] for n in range(Norm.TILES)], ps[:, 0, :], g, scale, shift, dst=dst)
            with self.nc.Block() as block:
                @block.scalar
                def _(act):
                    norm.roots(act)
                    norm.scaled(act)

                @block.tensor
                def _(pe):
                    norm.sums(pe)

                @block.vector
                def _(dve):
                    norm.vector(dve)

    @contextmanager
    def parts(self, name):
        with self.nc.sbuf_tensor(f"h_high_{name}", [P, KD, S], F32R) as high, \
                self.nc.sbuf_tensor(f"h_low_{name}", [P, KD, S], F32R) as low:
            yield high, low

    def mm3(self, out, w, x, start, stop):
        mm = self.nc.tensor.matmul
        mm(out, w[0], x[0], start=start, stop=False)
        mm(out, w[0], x[1], start=False, stop=False)
        return mm(out, w[1], x[0], start=False, stop=stop)

    def project(self, w, pairs, norm_of, out, beside=None):
        nc = self.nc
        with self.stage("proj"):
            wt, high, low = (self.sb(n, [P, 2, KD, 2 * P], dt) for n, dt in (("wt", F32), ("high", F32R), ("low", F32R)))
            ps = self.psum("ps", 6)
            h, last = norm_of["parts"], 2 * pairs
            norm = Norm(self, [out[:, n, :] for n in range(last - Norm.TILES, last)], ps[:, 5, :], **norm_of)
            rounds = 0
            if beside:
                rounds, mod = beside[-1], Modulation(self, *beside[:-1], ps[:, 4, :], slots=4)
            loaded = [self.sem(f"loaded{s}") for s in range(2)]
            high_done, low_done, tile_done, bank_free = self.sems("high_done low_done tile_done bank_free")
            with nc.Block() as block:
                @block.sync
                def _(sp):
                    def load(r, s):
                        sp.dma_start(wt[:, s], w[bass.ds(2 * r + s, 1)].rearrange("a p k n -> (a p) k n"))\
                            .then_inc(loaded[s], 16)

                    def load_again(r, s):
                        sp.wait_ge(low_done, 2 * r + s - 1)
                        load(r, s)
                    load(0, 0)
                    load(0, 1)
                    if beside:
                        with sp.Fori(0, rounds) as r:
                            load_again(r + 1, 0)
                            mod.load(sp, r, range(KD))
                            load_again(r + 1, 1)
                    in_pairs(sp, pairs, load_again, first=1 + rounds)

                @block.vector
                def _(dve):
                    def split(r, s):
                        dve.wait_ge(high_done, 2 * r + s + 1)
                        nc.vector.tensor_tensor(low[:, s], wt[:, s], high[:, s].bitcast(F32), ALU.subtract).then_inc(low_done, 1)
                    norm.vector(dve, beside=lambda: split(0, 0))
                    if beside:
                        mod.free(dve)
                        with dve.Fori(0, rounds) as r:
                            mod.multiply(dve, r, range(4))
                            split(r, 1)
                            mod.multiply(dve, r, range(4, 8))
                            split(r + 1, 0)
                            mod.finish(dve, r)
                    split(rounds, 1)
                    in_pairs(dve, pairs, split, first=rounds + 1)

                @block.tensor
                def _(pe):
                    pe.sem_inc(tile_done, 4)
                    norm.sums(pe)
                    norm.ready(pe)

                    def tiles(r, s):
                        pe.wait_ge(low_done, 2 * r + s + 1)
                        for u in range(2):
                            pe.wait_ge(bank_free, 4 * r + 2 * s + u + 1)
                            for k in range(KD):
                                c = slice(u * P, (u + 1) * P)
                                mm = self.mm3(ps[:, 2 * s + u, :], (high[:, s, k, c], low[:, s, k, c]), (h[0][:, k, :], h[1][:, k, :]),
                                              start=k == 0, stop=k == KD - 1)
                            mm.then_inc(tile_done, 1)
                    if beside:
                        with pe.Fori(0, rounds) as r:
                            tiles(r, 0)
                            tiles(r, 1)
                            mod.reduce(pe, r)
                    in_pairs(pe, pairs, tiles, first=rounds)

                @block.gpsimd
                def _(pool):
                    norm.high(pool)

                @block.scalar
                def _(act):
                    act.sem_inc(bank_free, 4)
                    if beside:
                        mod.start(act)

                    def split(r, s):
                        act.wait_ge(loaded[s], 16 * (r + 1))
                        act.wait_ge(tile_done, 4 * r + 2 * s + 2)
                        nc.scalar.activation(high[:, s], wt[:, s], ACT.Copy).then_inc(high_done, 1)

                    def evacuate(r, s):
                        for u in range(2):
                            act.wait_ge(tile_done, 4 * r + 2 * s + u + 5)
                            nc.scalar.activation(out[:, bass.ds(4 * r + 2 * s + u, 1), :].rearrange("p a t -> p (a t)"),
                                                 ps[:, 2 * s + u, :], ACT.Copy).then_inc(bank_free, 1)
                    norm.roots(act)
                    split(0, 0)
                    norm.scaled(act)
                    with act.Fori(0, (pairs - 1) // 2) as r:
                        split(r, 1)
                        evacuate(r, 0)
                        split(r + 1, 0)
                        evacuate(r, 1)
                    r = (pairs - 1) // 2
                    if pairs % 2 == 0:
                        split(r, 1)
                    evacuate(r, 0)
                    if pairs % 2 == 0:
                        evacuate(r, 1)

    def turn_tiles(self, proj, tiles, out, bias=None):
        nc = self.nc
        with self.stage("turn"):
            ps = self.psum("ps", 4)
            turned, bank_free, bias_loaded = self.sems("turned bank_free bias_loaded")
            with nc.Block() as block:
                if bias is not None:
                    @block.sync
                    def _(sp):
                        sp.dma_start(bias[:], self.t["alibi"]).then_inc(bias_loaded, 16)
                        sp.wait_ge(bias_loaded, 16)

                @block.tensor
                def _(pe):
                    for n, tile in enumerate(tiles):
                        if n >= 4:
                            pe.wait_ge(bank_free, n - 3)
                        for c in range(TT):
                            mm = nc.tensor.transpose(ps[:, n % 4, c * P:(c + 1) * P], proj[:, tile, c * P:(c + 1) * P],
                                                     self.c("ident"))
                        mm.then_inc(turned, 1)

                @block.scalar
                def _(act):
                    if bias is not None:
                        nc.scalar.mul(proj[:, AQ0:AQ0 + 4, :], proj[:, AQ0:AQ0 + 4, :], 0.125)
                    for n in range(len(tiles)):
                        act.wait_ge(turned, n + 1)
                        nc.scalar.activation(out[:, :, n * P:(n + 1) * P],
                                             ps[:, n % 4, :].rearrange("p (c f) -> p c f", c=TT), ACT.Copy)\
                            .then_inc(bank_free, 1)

    def attention_gates(self, gates):
        nc = self.nc
        with self.stage("gates"):
            wg = self.sb("wg", [P, KD, 24])
            ps = self.psum("ps", 1)[:, 0, :]
            loaded, done = self.sems("loaded done")
            with nc.Block() as block:
                @block.sync
                def _(sp):
                    sp.dma_start(wg[:], self.t["w_gates"]).then_inc(loaded, 16)

                @block.tensor
                def _(pe):
                    pe.wait_ge(loaded, 16)
                    for c in range(TT):
                        for k in range(KD):
                            mm = nc.tensor.matmul(ps[:, c * 24:(c + 1) * 24], self.hT[:, k, c * P:(c + 1) * P], wg[:, k, :],
                                                  start=k == 0, stop=k == KD - 1)
                    mm.then_inc(done, 1)

                @block.scalar
                def _(act):
                    act.wait_ge(done, 1)
                    nc.scalar.activation(gates[:].rearrange("p c n -> p (c n)"), ps[:, 0:TT * 24], ACT.Sigmoid)

    def hgrn(self, proj, vals):
        nc = self.nc
        W = HEADS * S
        with self.stage("hgrn"):
            f, b, ed, kk, qs, ql, kl = (self.sb(x, [P, HEADS, S]) for x in "f b ed kk qs ql kl".split())
            prod, at = self.sb("prod", [P, W]), self.sb("at", [P, W])
            qe, kend = f, ed
            kend_t = self.sb("kend_t", [P, HEADS, 3, P])
            state = self.sb("state", [P, 3, HEADS, P])
            dec = self.sb("dec", [P, HEADS, TT])
            lb, oml = self.sb("lb", [P, HEADS]), self.sb("oml", [P, HEADS])
            ps = self.psum("ps", 8)
            (lb_sub, lb_done, sig, f_done, log_done, scanned, k_done, q_done, shifted, decayed, ql_done, kl_done, mm_done,
             masked, added, s_chain, qe_done, kend_done, dec_done, k_turned, k_copied, sv_done, st_done) = self.sems(
                "lb_sub lb_done sig f_done log_done scanned k_done q_done shifted decayed ql_done kl_done mm_done masked "
                "added chain qe_done kend_done dec_done k_turned k_copied sv_done st_done")
            blanked, cleared = self.sems("blanked cleared")
            flat = lambda x: x[:].rearrange("p h t -> p (h t)")
            halves = lambda x, m: x[:].rearrange("p h (g m) -> p (h g) m", m=2 * m)
            LEVELS = [64 >> i for i in range(7)] + [0]

            with nc.Block() as block:
                def mask(dve, i):
                    dve.wait_ge(mm_done, i + 1)
                    lev = self.c("levels")[:, i * P:(i + 1) * P].rearrange("p (a t) -> p a t", a=1)
                    src = ps[:, 4 * (i % 2):4 * (i % 2) + 4, :].rearrange("p b (c t) -> p (b c) t", t=P)
                    if i:
                        dve.wait_ge(added, i + 1)
                    nc.vector.tensor_tensor(prod[:].rearrange("p (c t) -> p c t", t=P), src,
                                            lev.broadcast_to([P, HEADS * TT, P]), ALU.mult).then_inc(masked, 1)

                def add(pool, i):
                    pool.wait_ge(masked, i + 1)
                    pool.wait_ge(added, i + 1)
                    nc.gpsimd.tensor_tensor(at[:], at[:], prod[:], ALU.add).then_inc(added, 1)

                @block.scalar
                def _(act):
                    act.wait_ge(lb_sub, 1)
                    nc.scalar.activation(lb[:], lb[:], ACT.Sigmoid).then_inc(lb_done, 1)
                    nc.scalar.activation(flat(f), proj[:, F0:F0 + HEADS, :].rearrange("p h t -> p (h t)"), ACT.Sigmoid)\
                        .then_inc(sig, 1)
                    act.wait_ge(f_done, HEADS + 1)
                    nc.scalar.activation(flat(ql), flat(f), ACT.Ln).then_inc(log_done, 1)
                    for i, m in enumerate(LEVELS[:-1]):
                        act.wait_ge(shifted, 2 * i + 2)
                        nc.scalar.activation(flat(ed), flat(ed), ACT.Exp).then_inc(decayed, 1)
                    act.wait_ge(f_done, HEADS + 1)
                    act.wait_ge(k_done, 1)
                    nc.scalar.activation(flat(qe), flat(b), ACT.Exp).then_inc(qe_done, 1)
                    act.wait_ge(shifted, 15)
                    nc.scalar.activation(flat(kend), flat(kend), ACT.Exp).then_inc(kend_done, 1)
                    nc.scalar.activation(dec[:], b[:].rearrange("p h (c t) -> p h c t", t=P)[:, :, :, P - 1], ACT.Exp)\
                        .then_inc(dec_done, 1)
                    for h in range(HEADS):
                        act.wait_ge(k_turned, h + 1)
                        nc.scalar.activation(kend_t[:, h].rearrange("p c d -> p (c d)"), ps[:, h, 0:3 * P], ACT.Copy)\
                            .then_inc(k_copied, 1)

                @block.vector
                def _(dve):
                    chain = Chain(dve, s_chain)
                    nc.vector.tensor_tensor(lb[:], self.v("lb0"), self.v("lb1"), ALU.subtract).then_inc(lb_sub, 1)
                    dve.wait_ge(lb_done, 1)
                    chain(nc.vector.tensor_scalar(oml[:], lb[:], -1.0, 1.0, ALU.mult, ALU.add))
                    dve.wait_ge(sig, 1)
                    for h in range(HEADS):
                        nc.vector.tensor_scalar(f[:, h, :], f[:, h, :], oml[:, h:h + 1], lb[:, h:h + 1], ALU.mult, ALU.add)\
                            .then_inc(f_done, 1)
                    dve.wait_ge(f_done, HEADS)
                    nc.vector.tensor_scalar(flat(kk), flat(f), -1.0, 1.0, ALU.mult, ALU.add).then_inc(k_done, 1)
                    dve.wait_ge(k_done, 1)
                    nc.vector.tensor_scalar(flat(f), flat(f), LN_FLOOR, None, ALU.max).then_inc(f_done, 1)
                    nc.vector.tensor_scalar(flat(qs), proj[:, Q0:Q0 + HEADS, :].rearrange("p h t -> p (h t)"), P ** -0.5,
                                            None, ALU.mult).then_inc(q_done, 1)
                    dve.wait_ge(log_done, 1)
                    for h in range(HEADS):
                        for c in range(TT):
                            nc.vector.tensor_tensor_scan(b[:, h, c * P:(c + 1) * P], self.ones[:], ql[:, h, c * P:(c + 1) * P],
                                                         0.0, ALU.mult, ALU.add).then_inc(scanned, 1)
                    dve.wait_ge(scanned, HEADS * TT)
                    dve.wait_ge(q_done, 1)
                    for i, m in enumerate(LEVELS):
                        if m:
                            bh, eh = halves(b, m), halves(ed, m)
                            ref = bh[:, :, m - 1:m].broadcast_to([P, W // (2 * m), m])
                            if i:
                                dve.wait_ge(kl_done, i)
                                dve.wait_ge(ql_done, i)
                            nc.vector.tensor_tensor(eh[:, :, 0:m], ref, bh[:, :, 0:m], ALU.subtract).then_inc(shifted, 1)
                            nc.vector.tensor_tensor(eh[:, :, m:2 * m], bh[:, :, m:2 * m], ref, ALU.subtract)\
                                .then_inc(shifted, 1)
                            if i:
                                dve.wait_ge(mm_done, i)
                            dve.wait_ge(decayed, i + 1)
                            nc.vector.tensor_tensor(flat(ql), flat(qs), flat(ed), ALU.mult).then_inc(ql_done, 1)
                        if i:
                            mask(dve, i - 1)
                    bc = b[:].rearrange("p h (c t) -> p (h c) t", t=P)
                    dve.wait_ge(ql_done, 7)
                    dve.wait_ge(kl_done, 7)
                    nc.vector.tensor_tensor(kend[:].rearrange("p h (c t) -> p (h c) t", t=P),
                                            bc[:, :, P - 1:P].broadcast_to([P, HEADS * TT, P]), bc, ALU.subtract)\
                        .then_inc(shifted, 1)
                    mask(dve, 7)
                    dve.wait_ge(qe_done, 1)
                    nc.vector.tensor_tensor(flat(qe), flat(qe), flat(qs), ALU.mult).then_inc(qe_done, 1)
                    dve.wait_ge(kend_done, 1)
                    nc.vector.tensor_tensor(flat(kend), flat(kend), flat(kk), ALU.mult).then_inc(kend_done, 1)
                    dve.wait_ge(dec_done, 1)
                    for c in range(3):
                        dve.wait_ge(sv_done, c + 1)
                        pc = ps[:, 4 + c, :]
                        if c == 0:
                            nc.vector.tensor_copy(state[:, 0].rearrange("p h e -> p (h e)"), pc).then_inc(st_done, HEADS)
                        else:
                            dve.wait_ge(st_done, HEADS * c)
                            for h in range(HEADS):
                                nc.vector.scalar_tensor_tensor(out=state[:, c, h, :], in0=state[:, c - 1, h, :],
                                                               scalar=dec[:, h, c:c + 1], in1=pc[:, h * P:(h + 1) * P],
                                                               op0=ALU.mult, op1=ALU.add).then_inc(st_done, 1)

                @block.sync
                def _(sp):
                    rows = self.y_rows.rearrange("(p b) d -> p b d", b=NBLK)
                    sp.wait_ge(blanked, 1)
                    with sp.Fori(S * TOPK // BLK, NBLK) as b:
                        sp.dma_start(rows[:, bass.ds(b, 1), :].rearrange("p a d -> p (a d)"),
                                     self.hT[:, 4:6, :].rearrange("p n t -> p (n t)")).then_inc(cleared, 16)
                    sp.wait_ge(cleared, 16 * (NBLK - S * TOPK // BLK))

                @block.gpsimd
                def _(pool):
                    nc.gpsimd.memset(self.hT[:, 4:6, :], 0.0).then_inc(blanked, 1)
                    pool.wait_ge(k_done, 1)
                    nc.gpsimd.memset(at[:], 0.0).then_inc(added, 1)
                    for i in range(len(LEVELS)):
                        if LEVELS[i]:
                            pool.wait_ge(decayed, i + 1)
                            if i:
                                pool.wait_ge(mm_done, i)
                            nc.gpsimd.tensor_tensor(flat(kl), flat(kk), flat(ed), ALU.mult).then_inc(kl_done, 1)
                        if i:
                            add(pool, i - 1)
                    add(pool, 7)

                @block.tensor
                def _(pe):
                    for i, m in enumerate(LEVELS):
                        if m:
                            pe.wait_ge(ql_done, i + 1)
                            pe.wait_ge(kl_done, i + 1)
                        if i >= 2:
                            pe.wait_ge(masked, i - 1)
                        q, k = (ql, kl) if m else (qs, kk)
                        for h in range(HEADS):
                            for c in range(TT):
                                r = slice(c * P, (c + 1) * P)
                                mm = nc.tensor.matmul(ps[:, 4 * (i % 2) + h, r], k[:, h, r], q[:, h, r], start=True, stop=True)
                        mm.then_inc(mm_done, 1)
                    pe.wait_ge(kend_done, 2)
                    pe.wait_ge(masked, 7)
                    for h in range(HEADS):
                        for c in range(3):
                            mm = nc.tensor.transpose(ps[:, h, c * P:(c + 1) * P], kend[:, h, c * P:(c + 1) * P],
                                                     self.c("ident"))
                        mm.then_inc(k_turned, 1)
                    pe.wait_ge(k_copied, HEADS)
                    pe.wait_ge(masked, 8)
                    for c in range(3):
                        for h in range(HEADS):
                            mm = nc.tensor.matmul(ps[:, 4 + c, h * P:(h + 1) * P], kend_t[:, h, c, :],
                                                  vals[:, c, h * P:(h + 1) * P], start=True, stop=True)
                        mm.then_inc(sv_done, 1)
                    pe.wait_ge(added, 9)
                    pe.wait_ge(qe_done, 2)
                    for h in range(HEADS):
                        for c in range(TT):
                            r = slice(c * P, (c + 1) * P)
                            if c:
                                pe.wait_ge(st_done, HEADS * c)
                            nc.tensor.matmul(ps[:, h, r], vals[:, c, h * P:(h + 1) * P], at[:, h * S + c * P:h * S + (c + 1) * P],
                                             start=True, stop=c == 0)
                            if c:
                                nc.tensor.matmul(ps[:, h, r], state[:, c - 1, h, :], qe[:, h, r], start=False, stop=True)
            self.hgrn_out(proj, ps, ed, ql, prod[:, 0:S], prod[:, S:2 * S])

    def hgrn_out(self, proj, ps, o, gate, sq, rstd):
        nc = self.nc
        gated, squared, summed, rooted, inverted, scaled, done = self.sems(
            "gated squared summed rooted inverted scaled out_done")
        with nc.Block() as block:
            @block.scalar
            def _(act):
                nc.scalar.activation(gate[:].rearrange("p h t -> p (h t)"),
                                     proj[:, G0:G0 + HEADS, :].rearrange("p h t -> p (h t)"), ACT.Silu).then_inc(gated, 1)
                for h in range(HEADS):
                    if h:
                        act.wait_ge(summed, h)
                    nc.scalar.activation(sq[:], ps[:, h, :], ACT.Square).then_inc(squared, 1)
                    act.wait_ge(summed, h + 1)
                    if h:
                        act.wait_ge(scaled, h)
                    nc.scalar.activation(rstd[:], ps[:, 4 + h % 2, :], ACT.Sqrt, bias=self.eps[:, 0:1], scale=1.0 / P)\
                        .then_inc(rooted, 1)

            @block.tensor
            def _(pe):
                for h in range(HEADS):
                    pe.wait_ge(squared, h + 1)
                    if h >= 2:
                        pe.wait_ge(rooted, h - 1)
                    nc.tensor.matmul(ps[:, 4 + h % 2, :], self.ones[:], sq[:], start=True, stop=True).then_inc(summed, 1)

            @block.vector
            def _(dve):
                for h in range(HEADS):
                    dve.wait_ge(rooted, h + 1)
                    nc.vector.reciprocal(rstd[:], rstd[:]).then_inc(inverted, 1)
                    dve.wait_ge(inverted, h + 1)
                    nc.vector.tensor_tensor(o[:, h, :], ps[:, h, :], rstd[:], ALU.mult).then_inc(scaled, 1)
                    dve.wait_ge(scaled, h + 1)
                    dve.wait_ge(gated, 1)
                    nc.vector.scalar_tensor_tensor(out=self.hT[:, h, :], in0=o[:, h, :], scalar=self.v("hg_norm_g")[:, h:h + 1],
                                                   in1=gate[:, h, :], op0=ALU.mult, op1=ALU.mult).then_inc(done, 1)

    def rope(self, proj, rot):
        nc = self.nc
        tiles = [NQ0, NQ0 + 1, NQ0 + 2, NQ0 + 3, KS, KW]
        with self.stage("rope"):
            ps = self.psum("ps", 6)
            crossed = self.sb("crossed", [P, 2, S])
            scaled, turned, straight, cross, done = self.sems("q_scaled turned straight crossed done")
            with nc.Block() as block:
                @block.scalar
                def _(act):
                    q = proj[:, NQ0:NQ0 + 4, :]
                    nc.scalar.mul(q, q, 0.125).then_inc(scaled, 1)

                @block.tensor
                def _(pe):
                    pe.wait_ge(scaled, 1)
                    for n, tile in enumerate(tiles):
                        nc.tensor.matmul(ps[:, n, :], self.c("rot"), proj[:, tile, :], start=True, stop=True)\
                            .then_inc(turned, 1)

                @block.gpsimd
                def _(pool):
                    pool.wait_ge(scaled, 1)
                    for n, tile in enumerate(tiles):
                        nc.gpsimd.tensor_tensor(rot[:, n, :], proj[:, tile, :], self.c("cos"), ALU.mult).then_inc(straight, 1)

                @block.vector
                def _(dve):
                    for n in range(len(tiles)):
                        dve.wait_ge(turned, n + 1)
                        if n >= 2:
                            dve.wait_ge(done, n - 1)
                        nc.vector.tensor_tensor(crossed[:, n % 2, :], ps[:, n, :], self.c("sin"), ALU.mult).then_inc(cross, 1)
                        dve.wait_ge(cross, n + 1)
                        dve.wait_ge(straight, n + 1)
                        nc.vector.tensor_tensor(rot[:, n, :], rot[:, n, :], crossed[:, n % 2, :], ALU.add).then_inc(done, 1)

    def compress(self, proj, k_cmp, v_cmp):
        nc, t = self.nc, self.t
        N = S - 16
        B = 3 * N_CMP
        with self.stage("compress"):
            x = self.sb("x", [P, 2, 3, N])
            w1, w2 = self.sb("w1", [P, 2, 16, 256]), self.sb("w2", [P, 2, 2, 64])
            bias, hid = self.sb("bias", [P, 4]), self.sb("hid", [P, 2, 2, 2 * N_CMP])
            ps = self.psum("ps", 6)
            loaded = [self.sem(f"loaded_{name}") for name in "kv"]
            zeroed, hid_ps, bias_done, hid_done, out_ps = self.sems("zeroed hidden_products bias_done hid_done out_products")
            with nc.Block() as block:
                @block.gpsimd
                def _(pool):
                    nc.gpsimd.memset(x[:, :, 2, :], 0.0).then_inc(zeroed, 1)
                    nc.gpsimd.memset(v_cmp[:], 0.0).then_inc(zeroed, 1)

                @block.sync
                def _(sp):
                    sp.wait_ge(zeroed, 1)
                    for n, (tile, name) in enumerate(((KC, "k"), (VC, "v"))):
                        for g in range(2):
                            rows = slice(64 * g, 64 * g + 64)
                            sp.dma_start(x[0:64, n, g, :], proj[rows, tile, 0:N]).then_inc(loaded[n], 16)
                            sp.dma_start(x[64:128, n, g, :], proj[rows, tile, 16:S]).then_inc(loaded[n], 16)
                        sp.dma_start(x[:, n, 2, 0:16], t[f"pos_{name}"]).then_inc(loaded[n], 16)

                @block.tensor
                def _(pe):
                    for n in range(2):
                        pe.wait_ge(loaded[n], 7 * 16)
                        for m in range(2):
                            for l in range(16):
                                mm = nc.tensor.matmul(ps[:, 2 * n + m, 0:B].rearrange("p (g c) -> p g c", g=3),
                                                      w1[:, n, l, m * P:(m + 1) * P],
                                                      x[:, n, :, l:l + CMP_STRIDE * (N_CMP - 1) + 1:CMP_STRIDE],
                                                      start=l == 0, stop=l == 15)
                            mm.then_inc(hid_ps, 1)
                    pe.wait_ge(hid_done, 4)
                    for g in range(2):
                        for m in range(2):
                            mm = nc.tensor.matmul(ps[64 * g:64 * g + 64, 4, 0:N_CMP], w2[:, 0, m, :],
                                                  hid[:, 0, m, g * N_CMP:(g + 1) * N_CMP], start=m == 0, stop=m == 1)
                    for g in range(2):
                        for m in range(2):
                            mm = nc.tensor.matmul(ps[0:N_CMP, 5, 64 * g:64 * g + 64], hid[:, 1, m, g * N_CMP:(g + 1) * N_CMP],
                                                  w2[:, 1, m, :], start=m == 0, stop=m == 1)
                    mm.then_inc(out_ps, 1)

                @block.vector
                def _(dve):
                    for i in range(4):
                        dve.wait_ge(hid_ps, i + 1)
                        b1 = self.v("b1_k" if i < 2 else "b1_v")
                        nc.vector.tensor_tensor(bias[:, i:i + 1], ps[:, i, 2 * N_CMP:2 * N_CMP + 1], b1[:, i % 2:i % 2 + 1],
                                                ALU.add).then_inc(bias_done, 1)
                    dve.wait_ge(out_ps, 1)
                    dve.wait_ge(zeroed, 2)
                    nc.vector.tensor_copy(k_cmp[:], ps[:, 4, 0:N_CMP])
                    nc.vector.tensor_copy(v_cmp[0:N_CMP, :], ps[0:N_CMP, 5, 0:P])

                @block.scalar
                def _(act):
                    for n, name in enumerate("kv"):
                        act.dma_start(w1[:, n], t[f"w1_{name}"]).then_inc(loaded[n], 16)
                        act.dma_start(w2[:, n], t[f"w2_{name}"]).then_inc(loaded[n], 16)
                    for i in range(4):
                        act.wait_ge(bias_done, i + 1)
                        nc.scalar.activation(hid[:, i // 2, i % 2, :], ps[:, i, 0:2 * N_CMP], ACT.Gelu_apprx_tanh,
                                             bias=bias[:, i:i + 1]).then_inc(hid_done, 1)

    def attend(self, items, out_tile, sink=None, beside=None):
        nc = self.nc
        n_items = len(items)
        with self.stage("attend"):
            LAG = 4
            SLOTS = LAG + 1
            p = self.sb("p", [P, SLOTS, S])
            pt = self.sb("pt", [P, 2, S])
            top, den, fac = (self.sb(x, [P, n_items]) for x in "top den fac".split())
            es = self.sb("es", [P, n_items])
            psS, psT, psO, psM = self.psum("scores", 3), self.psum("turned", 2), self.psum("outs", 2), self.psum("mod", 1)
            if beside:
                chunks, mod = beside[-1], Modulation(self, *beside[:-1], psM[:, 0, :], slots=4)
            (zeroed, scores, masked, topped, expd, facd, scaled, turned, copied, products, moved, kept, raw_top, sunk) = self.sems(
                "zeroed scores masked topped expd fac_ready scaled turned copied products moved kept raw_top sunk")
            keys = [it["k"].shape[-1] for it in items]
            wide = [-(-n // P) * P for n in keys]
            pairs_before = [sum(x["last"] for x in items[:i]) for i in range(n_items + 1)]

            with nc.Block() as block:
                if beside:
                    @block.sync
                    def _(sp):
                        with sp.Fori(0, chunks) as g:
                            mod.load(sp, g, range(KD))

                @block.gpsimd
                def _(pool):
                    nc.gpsimd.memset(p[:], 0.0).then_inc(zeroed, 1)
                    for i, it in enumerate(items):
                        pool.wait_ge(facd, i + 1)
                        s = p[:, i % SLOTS, 0:wide[i]]
                        if it["keep"] is not None:
                            seen = p[:, i % SLOTS, 0:keys[i]]
                            nc.gpsimd.tensor_tensor(seen, seen, it["keep"], ALU.mult).then_inc(kept, 1)
                            pool.wait_ge(kept, sum(x["keep"] is not None for x in items[:i + 1]))
                        if it["gate"] is None:
                            nc.gpsimd.tensor_scalar(s, s, fac[:, i:i + 1], None, ALU.mult).then_inc(scaled, 1)
                        else:
                            nc.gpsimd.tensor_scalar(s, s, fac[:, i:i + 1], it["gate"], ALU.mult, ALU.mult)\
                                .then_inc(scaled, 1)

                @block.tensor
                def _(pe):
                    def score(i):
                        it = items[i]
                        if i >= 3:
                            pe.wait_ge(expd, i - 2)
                        nc.tensor.matmul(psS[:, i % 3, 0:keys[i]], it["q"], it["k"], start=True, stop=True).then_inc(scores, 1)

                    def turn(i):
                        pe.wait_ge(scaled, i + 1)
                        if i >= 2:
                            pe.wait_ge(copied, i - 1)
                        for b in range(wide[i] // P):
                            mm = nc.tensor.transpose(psT[:, i % 2, b * P:(b + 1) * P], p[:, i % SLOTS, b * P:(b + 1) * P],
                                                     self.c("ident"))
                        mm.then_inc(turned, 1)

                    def multiply(i):
                        it = items[i]
                        pe.wait_ge(copied, i + 1)
                        pair = pairs_before[i]
                        if pair >= 2:
                            pe.wait_ge(moved, pair - 1)
                        lo = it["out"][0]
                        for b, v in enumerate(it["v"]):
                            mm = nc.tensor.matmul(psO[lo:lo + 64, pair % 2, 0:P], v, pt[:, i % 2, b * P:(b + 1) * P],
                                                  start=it["first"] and b == 0, stop=it["ends"] and b == len(it["v"]) - 1)
                        mm.then_inc(products, 1)

                    score(0)
                    for i in range(n_items + LAG + 1):
                        if i + 1 < n_items:
                            score(i + 1)
                        if beside and i % KD == 0 and 1 <= i // KD <= chunks:
                            mod.reduce(pe, i // KD - 1)
                        if 0 <= i - LAG < n_items:
                            turn(i - LAG)
                        if i > LAG:
                            multiply(i - LAG - 1)

                @block.vector
                def _(dve):
                    def find_top(i):
                        it = items[i]
                        dve.wait_ge(scores, i + 1)
                        s = psS[:, i % 3, 0:keys[i]]
                        if it["mask"] is not None:
                            at, mask = it["mask"]
                            n = mask.shape[-1]
                            nc.vector.tensor_tensor(s[:, at:at + n], s[:, at:at + n], mask, ALU.add).then_inc(masked, 1)
                            dve.wait_ge(masked, i + 1)
                        else:
                            dve.sem_inc(masked, 1)
                        if sink is None:
                            nc.vector.tensor_reduce(top[:, i:i + 1], s, AX.X, ALU.max, negate=True).then_inc(topped, 1)
                        else:
                            nc.vector.tensor_reduce(top[:, i:i + 1], s, AX.X, ALU.max).then_inc(raw_top, 1)
                            dve.wait_ge(raw_top, i + 1)
                            nc.vector.tensor_scalar(top[:, i:i + 1], top[:, i:i + 1], sink(i), -1.0, ALU.max, ALU.mult)\
                                .then_inc(topped, 1)

                    def factor(i):
                        dve.wait_ge(expd, i + 1)
                        d = den[:, i:i + 1]
                        if sink is not None:
                            nc.vector.tensor_tensor(d, d, es[:, i:i + 1], ALU.add).then_inc(sunk, 1)
                            dve.wait_ge(sunk, i + 1)
                        nc.vector.reciprocal(fac[:, i:i + 1], d).then_inc(facd, 1)

                    def move(i):
                        if 0 <= i < n_items and items[i]["last"]:
                            _, j, qt = items[i]["out"]
                            dve.wait_ge(products, i + 1)
                            nc.vector.tensor_copy(self.hT[:, out_tile + j, qt * P:(qt + 1) * P],
                                                  psO[:, pairs_before[i] % 2, 0:P]).then_inc(moved, 1)

                    if beside:
                        mod.free(dve)
                    for i in range(n_items + LAG + 2):
                        if i < n_items:
                            find_top(i)
                        if 1 <= i <= n_items:
                            factor(i - 1)
                        move(i - LAG - 2)
                        if beside and i >= 1:
                            g, piece = (i - 1) // KD, (i - 1) % KD
                            if piece == 0 and 1 <= g <= chunks:
                                mod.finish(dve, g - 1)
                            if g < chunks:
                                mod.multiply(dve, g, [piece])

                @block.scalar
                def _(act):
                    act.wait_ge(zeroed, 1)
                    if beside:
                        mod.start(act)

                    def exponents(i):
                        act.wait_ge(topped, i + 1)
                        if i >= SLOTS:
                            act.wait_ge(turned, i - LAG)
                        if sink is not None:
                            nc.scalar.activation(es[:, i:i + 1], sink(i), ACT.Exp, bias=top[:, i:i + 1])
                        nc.scalar.activation(p[:, i % SLOTS, 0:keys[i]], psS[:, i % 3, 0:keys[i]], ACT.Exp, bias=top[:, i:i + 1],
                                             accum_out=den[:, i:i + 1]).then_inc(expd, 1)

                    def copy(i):
                        act.wait_ge(turned, i + 1)
                        if i >= 2:
                            act.wait_ge(products, i - 1)
                        nc.scalar.activation(pt[:, i % 2, 0:wide[i]], psT[:, i % 2, 0:wide[i]], ACT.Copy).then_inc(copied, 1)

                    for i in range(n_items + LAG):
                        if i >= LAG:
                            copy(i - LAG)
                        if i < n_items:
                            exponents(i)

    def nsa_items(self, proj, rot, k_cmp, v_cmp, vals, gates):
        items = []
        for qt in range(TT):
            cols = slice(qt * P, (qt + 1) * P)
            for j in range(NSA_PAIRS):
                for g in range(2):
                    rows = slice(64 * g, 64 * g + 64)
                    h = 3 * (4 * g + j)
                    gate = [gates[:, qt, h + b:h + b + 1] for b in range(3)]
                    base = {"out": (64 * g, j, qt), "keep": None, "last": False, "first": False, "ends": False}
                    add = self.c("cmp_add")[:, qt * N_CMP:(qt + 1) * N_CMP]
                    items.append(base | {"q": proj[rows, NQ0 + j, cols], "k": k_cmp[rows, :], "v": [v_cmp[:, rows]],
                                         "mask": (0, add), "gate": gate[0], "keep": self.c("cmp_keep") if qt == 0 else None,
                                         "first": True})
                    for n, branch in enumerate((4, 5)):
                        v0 = 512 + 128 * n + 64 * g
                        items.append(base | {"q": rot[rows, j, cols], "k": rot[rows, branch, 0:(qt + 1) * P],
                                             "v": [vals[:, b, v0:v0 + 64] for b in range(qt + 1)],
                                             "mask": (qt * P, self.c("causal")), "gate": gate[1 + n],
                                             "ends": n == 1, "last": n == 1 and g == 1})
        return items

    def feed_forward(self, layer, sub, w_gu, w_dn, beside=None):
        m = 24 * sub
        gn = 24 * layer + 8 * sub
        with self.parts(f"f{layer}{sub}") as h:
            norm_of = {"g": self.v("g_norm", gn, gn + 8), "scale": self.mod[:, m + 8:m + 16], "shift": self.mod[:, m:m + 8],
                       "parts": h}
            self.gated_layer(norm_of, self.mod[:, m + 16:m + 24], w_gu, w_dn, beside)

    def gated_layer(self, norm_of, gate, w_gu, w_dn, beside=None):
        nc, xT = self.nc, self.xT
        HALF = FT // 2
        with self.stage("ffn"):
            wt = self.sb("wt", [P, 2, 2 * D])
            high, low = self.sb("high", [P, 2, 2 * D], F32R), self.sb("low", [P, 2, 2 * D], F32R)
            with nc.sbuf_tensor(self.tag + "norm_scratch", [P, Norm.TILES, S], F32) as scratch:
                pass
            hid_high, hid_low = self.sb("hid_high", [P, FT, S], F32R), self.sb("hid_low", [P, FT, S], F32R)
            sg = self.sb("sg", [P, 2, S])
            half = self.sb("half", [P, KD])
            ps = self.psum("ps", 8)
            h = norm_of["parts"]
            norm = Norm(self, [scratch[:, n, :] for n in range(Norm.TILES)], ps[:, 6, :], **norm_of)
            rounds = 0
            if beside:
                at = CON["cos"][0]
                wk = self.con[:, at:at + 2 * Modulation.CHUNK].rearrange("p (s n) -> p s n", s=2)
                rounds, mod = beside[-1], Modulation(self, *beside[:-1], ps[:, 7, :], wk)
            loaded = [self.sem(f"loaded{s}") for s in range(2)]
            high_done, low_done, multiplied, gate_ps, silu_done, hid_done, hid_seen, hid_high_done, hid_low_done, half_done, out_done = \
                self.sems("high_done low_done multiplied gate_products silu_done hidden_done hidden_seen hidden_high_done "
                          "hidden_low_done half_done out_done")
            with nc.Block() as block:
                @block.sync
                def _(sp):
                    def up(r, s):
                        sp.dma_start(wt[:, s], w_gu[bass.ds(2 * r + s, 1)].rearrange("a p k n -> (a p) (k n)"))\
                            .then_inc(loaded[s], 16)

                    def up_again(r, s):
                        sp.wait_ge(low_done, 2 * r + s - 1)
                        up(r, s)

                    def down(r, s):
                        sp.wait_ge(low_done, 2 * r + s + FT - 1)
                        sp.dma_start(wt[:, s].rearrange("p (a n) -> p a n", a=2),
                                     w_dn[bass.ds(4 * r + 2 * s, 2)].rearrange("a p n -> p a n")).then_inc(loaded[s], 16)
                    up(0, 0)
                    up(0, 1)
                    if beside:
                        with sp.Fori(0, rounds) as g:
                            up_again(2 * g + 1, 0)
                            mod.load(sp, g, (0, 1))
                            up_again(2 * g + 1, 1)
                            mod.load(sp, g, (2, 3))
                            up_again(2 * g + 2, 0)
                            mod.load(sp, g, (4, 5))
                            up_again(2 * g + 2, 1)
                            mod.load(sp, g, (6, 7))
                    in_pairs(sp, FT, up_again, first=1 + 2 * rounds)
                    in_pairs(sp, HALF, down)

                @block.tensor
                def _(pe):
                    pe.sem_inc(multiplied, 2)
                    norm.sums(pe)
                    norm.ready(pe)

                    def up(r, s):
                        pe.wait_ge(low_done, 2 * r + s + 1)
                        pe.wait_ge(hid_done, 2 * r + s + 1)
                        for bank, sem in ((0, gate_ps), (1, multiplied)):
                            for k in range(KD):
                                c = slice((2 * k + bank) * P, (2 * k + bank + 1) * P)
                                mm = self.mm3(ps[:, 2 * s + bank, :], (high[:, s, c], low[:, s, c]), (h[0][:, k, :], h[1][:, k, :]),
                                              start=k == 0, stop=k == KD - 1)
                            mm.then_inc(sem, 1)

                    def down(r, s, first=False, last=False):
                        pe.wait_ge(low_done, FT + 2 * r + s + 1)
                        for a in range(2):
                            x = [t_[:, bass.ds(4 * r + 2 * s + a, 1), :].rearrange("p a t -> p (a t)") for t_ in (hid_high, hid_low)]
                            for n in range(KD):
                                c = slice(a * D + n * P, a * D + (n + 1) * P)
                                mm = self.mm3(ps[:, n, :], (high[:, s, c], low[:, s, c]), x, start=first and a == 0,
                                              stop=last and a == 1)
                        mm.then_inc(multiplied, 1)
                    if beside:
                        with pe.Fori(0, rounds) as g:
                            for r in (2 * g, 2 * g + 1):
                                up(r, 0)
                                up(r, 1)
                            mod.reduce(pe, g)
                    in_pairs(pe, FT, up, first=2 * rounds)
                    pe.wait_ge(hid_done, FT + 2)
                    pe.wait_ge(hid_low_done, FT)
                    down(0, 0, first=True)
                    down(0, 1)
                    with pe.Fori(1, HALF // 2) as r:
                        down(r, 0)
                        down(r, 1)
                    pe.wait_ge(hid_low_done, FT + 2)
                    down(HALF // 2, 0, last=True)

                def ahead(eng, split, finish, first=0):
                    with eng.Fori(first, HALF) as r:
                        split(r, 1)
                        finish(r, 0)
                        split(r + 1, 0)
                        finish(r, 1)
                    split(HALF, 1)
                    with eng.Fori(HALF + 1, (FT + HALF) // 2) as r:
                        split(r, 0)
                        split(r, 1)
                    split((FT + HALF) // 2, 0)

                @block.scalar
                def _(act):
                    act.sem_inc(hid_low_done, 2)
                    if beside:
                        mod.start(act)

                    def split(r, s):
                        act.wait_ge(loaded[s], 16 * (r + 1))
                        act.wait_ge(multiplied, 2 * r + s + 1)
                        nc.scalar.activation(high[:, s], wt[:, s], ACT.Copy).then_inc(high_done, 1)

                    def finish(r, s):
                        n = 2 * r + s
                        act.wait_ge(gate_ps, n + 1)
                        act.wait_ge(hid_low_done, n + 1)
                        nc.scalar.activation(sg[:, s, :], ps[:, 2 * s, :], ACT.Silu).then_inc(silu_done, 1)
                    norm.roots(act)
                    split(0, 0)
                    norm.scaled(act)
                    ahead(act, split, finish)

                @block.gpsimd
                def _(pool):
                    norm.high(pool)

                    def hidden_high(r, s):
                        pool.wait_ge(hid_done, 2 * r + s + 3)
                        pool.sem_inc(hid_seen, 1)
                        nc.gpsimd.tensor_copy(hid_high[:, bass.ds(2 * r + s, 1), :].rearrange("p a t -> p (a t)"), sg[:, s, :])\
                            .then_inc(hid_high_done, 1)
                    in_pairs(pool, FT, hidden_high)

                @block.vector
                def _(dve):
                    dve.sem_inc(hid_done, 2)
                    nc.vector.tensor_scalar(half[:], gate, 0.5, None, ALU.mult).then_inc(half_done, 1)

                    def split(r, s):
                        dve.wait_ge(high_done, 2 * r + s + 1)
                        nc.vector.tensor_tensor(low[:, s], wt[:, s], high[:, s].bitcast(F32), ALU.subtract).then_inc(low_done, 1)

                    def finish(r, s):
                        n = 2 * r + s
                        dve.wait_ge(multiplied, n + 3)
                        dve.wait_ge(silu_done, n + 1)
                        nc.vector.tensor_tensor(sg[:, s, :], sg[:, s, :], ps[:, 2 * s + 1, :], ALU.mult).then_inc(hid_done, 1)
                        dve.wait_ge(hid_high_done, n + 1)
                        part = lambda x: x[:, bass.ds(n, 1), :].rearrange("p a t -> p (a t)")
                        nc.vector.tensor_tensor(part(hid_low), sg[:, s, :], part(hid_high).bitcast(F32), ALU.subtract)\
                            .then_inc(hid_low_done, 1)
                    norm.vector(dve, beside=lambda: split(0, 0))
                    if beside:
                        mod.free(dve)
                        with dve.Fori(0, rounds) as g:
                            for piece, r in ((0, 2 * g), (4, 2 * g + 1)):
                                split(r, 1)
                                mod.multiply(dve, g, (piece, piece + 1))
                                finish(r, 0)
                                split(r + 1, 0)
                                mod.multiply(dve, g, (piece + 2, piece + 3))
                                finish(r, 1)
                            mod.finish(dve, g)
                    ahead(dve, split, finish, first=2 * rounds)
                    dve.wait_ge(multiplied, FT + HALF + 2)
                    dve.wait_ge(half_done, 1)
                    for n in range(KD):
                        nc.vector.scalar_tensor_tensor(out=xT[:, n, :], in0=ps[:, n, :], scalar=half[:, n:n + 1],
                                                       in1=xT[:, n, :], op0=ALU.mult, op1=ALU.add).then_inc(out_done, 1)

    def project_out(self, w, gate, hT):
        nc, xT = self.nc, self.xT
        G = KD // 2
        with self.stage("out"):
            wt, high, low = (self.sb(n, [P, 2, KD, 2 * P], dt) for n, dt in (("wt", F32), ("high", F32R), ("low", F32R)))
            hh, hl = self.sb("hh", [P, KD, S], F32R), self.sb("hl", [P, KD, S], F32R)
            ps = self.psum("ps", 8)
            loaded = [self.sem(f"loaded{s}") for s in range(2)]
            high_done, low_done, h_high_act, h_high_pool, h_low, tile_done, added = self.sems(
                "high_done low_done h_high_by_act h_high_by_pool h_low tile_done added")
            with nc.Block() as block:
                @block.sync
                def _(sp):
                    for g in range(G):
                        if g >= 2:
                            sp.wait_ge(low_done, g - 1)
                        sp.dma_start(wt[:, g % 2], w[g]).then_inc(loaded[g % 2], 16)

                @block.scalar
                def _(act):
                    for k in range(1, KD, 2):
                        nc.scalar.activation(hh[:, k, :], hT[:, k, :], ACT.Copy).then_inc(h_high_act, 1)
                    for g in range(G):
                        act.wait_ge(loaded[g % 2], 16 * (g // 2 + 1))
                        if g >= 2:
                            act.wait_ge(tile_done, 2 * g - 2)
                        nc.scalar.activation(high[:, g % 2], wt[:, g % 2], ACT.Copy).then_inc(high_done, 1)

                @block.gpsimd
                def _(pool):
                    for k in range(0, KD, 2):
                        nc.gpsimd.tensor_copy(hh[:, k, :], hT[:, k, :]).then_inc(h_high_pool, 1)

                @block.vector
                def _(dve):
                    def split(g):
                        dve.wait_ge(high_done, g + 1)
                        nc.vector.tensor_tensor(low[:, g % 2], wt[:, g % 2], high[:, g % 2].bitcast(F32), ALU.subtract)\
                            .then_inc(low_done, 1)
                    for k in range(KD):
                        dve.wait_ge(h_high_act if k % 2 else h_high_pool, k // 2 + 1)
                        nc.vector.tensor_tensor(hl[:, k, :], hT[:, k, :], hh[:, k, :].bitcast(F32), ALU.subtract).then_inc(h_low, 1)
                        if k == 5:
                            split(0)
                    for n in range(KD):
                        if n % 2 == 0 and n // 2 + 1 < G:
                            split(n // 2 + 1)
                        dve.wait_ge(tile_done, n + 1)
                        nc.vector.scalar_tensor_tensor(out=xT[:, n, :], in0=ps[:, n, :], scalar=gate[:, n:n + 1],
                                                       in1=xT[:, n, :], op0=ALU.mult, op1=ALU.add).then_inc(added, 1)

                @block.tensor
                def _(pe):
                    for g in range(G):
                        pe.wait_ge(low_done, g + 1)
                        for u in range(2):
                            for k in range(KD):
                                if g == u == 0:
                                    pe.wait_ge(h_low, k + 1)
                                c = slice(u * P, (u + 1) * P)
                                mm = self.mm3(ps[:, 2 * g + u, :], (high[:, g % 2, k, c], low[:, g % 2, k, c]), (hh[:, k, :], hl[:, k, :]),
                                              start=k == 0, stop=k == KD - 1)
                            mm.then_inc(tile_done, 1)

    def first_mixer(self):
        nc, t = self.nc, self.t
        with ExitStack() as ctx:
            tile = lambda name, shape: ctx.enter_context(nc.sbuf_tensor(name, shape, F32))
            self.hT = tile("hT_1", [P, KD, S])
            proj, gates = tile("proj", [P, IN_TILES, S]), tile("gates", [P, TT, 24])
            k_cmp, v_cmp = tile("k_cmp", [P, N_CMP]), tile("v_cmp", [P, P])
            with self.parts("1") as h:
                norm_of = {"g": self.v("norm1_g"), "scale": self.mod[:, 8:16], "shift": self.mod[:, 0:8], "parts": h, "dst": self.hT}
                self.project(t["w_in"], IN_TILES // 2, norm_of, proj,
                             beside=(t["w_ada"][:, 16 * P:], self.v("c"), self.v("b_ada", 16), self.mod[:, 16:48], 4))
            vals, rot = tile("vals", [P, TT, 768]), tile("rot", [P, 6, S])
            self.attention_gates(gates)
            self.turn_tiles(proj, [HI0, HI0 + 1, HI0 + 2, HI0 + 3, VS, VW], vals)
            self.rope(proj, rot)
            self.compress(proj, k_cmp, v_cmp)
            self.hgrn(proj, vals)
            self.attend(self.nsa_items(proj, rot, k_cmp, v_cmp, vals, gates), 4,
                        beside=(t["w_mod"][0], self.v("c_2"), self.v("b_mod0"), self.mods[1], 9))
            self.project_out(t["w_out"], self.mod[:, 16:24], self.hT)

    def second_mixer(self, layer):
        nc, t = self.nc, self.t
        with ExitStack() as ctx:
            tile = lambda name, shape: ctx.enter_context(nc.sbuf_tensor(f"{name}_{layer}", shape, F32))
            self.hT = tile("hT_2", [P, KD, S])
            proj, vals, bias = tile("proj2", [P, IN_TILES_2, S]), tile("vals2", [P, TT, P]), tile("alibi", [P, 8, 2 * P])
            with self.parts(f"2{layer}") as h:
                norm_of = {"g": self.v("g_norm", 24 * layer + 8, 24 * layer + 16), "scale": self.mod[:, 32:40],
                           "shift": self.mod[:, 24:32], "parts": h}
                self.project(t["w_in_2"][layer], IN_TILES_2 // 2, norm_of, proj)
            self.turn_tiles(proj, [AV], vals, bias)
            self.attend(self.window_items(proj, vals, bias), 0,
                        sink=lambda i: self.v("sinks")[:, 8 * layer + i % 8:8 * layer + i % 8 + 1])
            self.recurrence(layer, proj)
            self.project_out(t["w_out_2"][layer], self.mod[:, 40:48], self.hT)

    def window_items(self, proj, vals, bias):
        items = []
        for qt in range(TT):
            for j in range(4):
                for g in range(2):
                    rows = slice(64 * g, 64 * g + 64)
                    lo = max(qt - 1, 0)
                    skip = P if qt == 0 else 0
                    items.append({"q": proj[rows, AQ0 + j, qt * P:(qt + 1) * P], "k": proj[rows, AK, lo * P:(qt + 1) * P],
                                  "v": [vals[:, b, rows] for b in range(lo, qt + 1)],
                                  "mask": (0, bias[:, 2 * j + g, skip:]), "gate": None, "keep": None,
                                  "out": (64 * g, j, qt), "first": True, "ends": True, "last": g == 1})
        return items

    def recurrence(self, layer, proj):
        nc = self.nc
        with self.stage("lru"):
            wa, wx = self.sb("wa", [P, 2, P]), self.sb("wx", [P, 2, P])
            xc, r, i_, a, mult, u, th, pr, cv = (self.sb(x, [P, 2, S]) for x in "xc r i a mult u th pr cv".split())
            e, s2, z, pos = (self.sb(x, [P, 2]) for x in "e s2 z pos".split())
            poly = self.sb("poly", [P, 2])
            ps = self.psum("ps", 4)
            flat = lambda x: x[:].rearrange("p n t -> p (n t)")
            loaded, conv_done, gates_ps, chain_s, act_s, pool_s, abs_done, loga, tanh_done, mult_in, rooted, hid, gelu = self.sems(
                "loaded conv_done gate_products chain act_steps pool_steps abs_done log_a tanh_done mult_in rooted hidden gelu")
            w4 = lambda k, n: self.v("conv_w")[:, 8 * layer + 2 * k + n:8 * layer + 2 * k + n + 1]
            w3 = lambda k, n: self.v("sc_conv_w")[:, 6 * layer + 2 * k + n:6 * layer + 2 * k + n + 1]
            two = lambda name: self.v(name)[:, 2 * layer:2 * layer + 2]
            with nc.Block() as block:
                @block.sync
                def _(sp):
                    sp.dma_start(wa[:], self.t["gate_a"][layer]).then_inc(loaded, 16)
                    sp.dma_start(wx[:], self.t["gate_x"][layer]).then_inc(loaded, 16)

                @block.vector
                def _(dve):
                    chain = Chain(dve, chain_s)
                    for n in range(2):
                        x = proj[:, LX0 + n, :]
                        chain(nc.vector.tensor_scalar(xc[:, n, :], x, w4(3, n), two("conv_b")[:, n:n + 1], ALU.mult, ALU.add))
                        for k in range(3):
                            d = 3 - k
                            chain(nc.vector.scalar_tensor_tensor(out=xc[:, n, d:], in0=x[:, 0:S - d], scalar=w4(k, n),
                                                                 in1=xc[:, n, d:], op0=ALU.mult, op1=ALU.add))
                    dve.sem_inc(conv_done, 1)
                    lam = two("lam")
                    dve.wait_ge(abs_done, 1)
                    chain(nc.vector.tensor_scalar(z[:], e[:], 2.0, None, ALU.add))
                    chain(nc.vector.reciprocal(z[:], z[:]))
                    chain(nc.vector.tensor_tensor(z[:], z[:], e[:], ALU.mult))
                    chain(nc.vector.tensor_tensor(s2[:], z[:], z[:], ALU.mult))
                    chain(nc.vector.tensor_scalar(poly[:], s2[:], 2.0 / 17, 2.0 / 15, ALU.mult, ALU.add))
                    for k in (13, 11, 9, 7, 5, 3, 1):
                        chain(nc.vector.tensor_tensor(poly[:], poly[:], s2[:], ALU.mult))
                        chain(nc.vector.tensor_scalar(poly[:], poly[:], 2.0 / k, None, ALU.add))
                    chain(nc.vector.tensor_tensor(poly[:], poly[:], z[:], ALU.mult))
                    chain(nc.vector.tensor_scalar(pos[:], lam, -1.0, 0.0, ALU.mult, ALU.max))
                    chain(nc.vector.tensor_tensor(poly[:], poly[:], pos[:], ALU.add))
                    chain(nc.vector.tensor_scalar(poly[:], poly[:], -8.0, None, ALU.mult))
                    dve.wait_ge(act_s, 4)
                    for n in range(2):
                        nc.vector.tensor_scalar(r[:, n, :], r[:, n, :], poly[:, n:n + 1], None, ALU.mult).then_inc(loga, 1)
                    chain(nc.vector.tensor_tensor(flat(u), flat(i_), flat(xc), ALU.mult))
                    dve.wait_ge(tanh_done, 1)
                    chain(nc.vector.tensor_scalar(flat(mult), flat(th), -1.0, 1.0, ALU.mult, ALU.add))
                    chain(nc.vector.reciprocal(flat(mult), flat(mult)))
                    chain(nc.vector.scalar_tensor_tensor(out=flat(mult), in0=flat(th), scalar=-2.0, in1=flat(mult),
                                                         op0=ALU.mult, op1=ALU.mult))
                    nc.vector.tensor_scalar(flat(mult), flat(mult), 1e-30, None, ALU.max).then_inc(mult_in, 1)
                    dve.wait_ge(rooted, 1)
                    chain(nc.vector.memset(mult[:, :, 0:1], 1.0))
                    chain(nc.vector.tensor_tensor(flat(u), flat(u), flat(mult), ALU.mult))
                    for n in range(2):
                        nc.vector.tensor_tensor_scan(mult[:, n, :], a[:, n, :], u[:, n, :], 0.0, ALU.mult, ALU.add)\
                            .then_inc(hid, 1)
                    dve.wait_ge(hid, 2)
                    dve.wait_ge(gelu, 1)
                    nc.vector.tensor_tensor(self.hT[:, 4:6, :], mult[:], th[:], ALU.mult).then_inc(hid, 1)
                    dve.wait_ge(pool_s, 1)
                    for n in range(2):
                        chain(nc.vector.tensor_scalar(cv[:, n, :], pr[:, n, :], w3(2, n), None, ALU.mult))
                        for k in range(2):
                            d = 2 - k
                            chain(nc.vector.scalar_tensor_tensor(out=cv[:, n, d:], in0=pr[:, n, 0:S - d], scalar=w3(k, n),
                                                                 in1=cv[:, n, d:], op0=ALU.mult, op1=ALU.add))
                    nc.vector.tensor_tensor(self.hT[:, 6:8, :], cv[:], proj[:, SB0:SB0 + 2, :], ALU.mult).then_inc(hid, 1)

                @block.gpsimd
                def _(pool):
                    nc.gpsimd.tensor_tensor(pr[:], proj[:, SC0:SC0 + 2, :], proj[:, SX0:SX0 + 2, :], ALU.mult)\
                        .then_inc(pool_s, 1)

                @block.tensor
                def _(pe):
                    pe.wait_ge(loaded, 32)
                    pe.wait_ge(conv_done, 1)
                    for g, w in enumerate((wa, wx)):
                        for n in range(2):
                            nc.tensor.matmul(ps[:, 2 * g + n, :], w[:, n, :], xc[:, n, :], start=True, stop=True)\
                                .then_inc(gates_ps, 1)

                @block.scalar
                def _(act):
                    nc.scalar.activation(e[:], two("lam"), ACT.Abs).then_inc(act_s, 1)
                    act.wait_ge(act_s, 1)
                    nc.scalar.activation(e[:], e[:], ACT.Exp, scale=-1.0).then_inc(abs_done, 1)
                    for g, (out, name) in enumerate(((r, "gate_a_b"), (i_, "gate_x_b"))):
                        for n in range(2):
                            act.wait_ge(gates_ps, 2 * g + n + 1)
                            ins = nc.scalar.activation(out[:, n, :], ps[:, 2 * g + n, :], ACT.Sigmoid,
                                                       bias=two(name)[:, n:n + 1])
                            if g or n:
                                ins.then_inc(act_s, 1)
                    act.wait_ge(loga, 2)
                    nc.scalar.activation(flat(th), flat(r), ACT.Tanh).then_inc(tanh_done, 1)
                    nc.scalar.activation(flat(a), flat(r), ACT.Exp).then_inc(tanh_done, 1)
                    act.wait_ge(mult_in, 1)
                    nc.scalar.activation(flat(mult), flat(mult), ACT.Sqrt).then_inc(rooted, 1)
                    nc.scalar.activation(th[:], proj[:, LG0:LG0 + 2, :], ACT.Gelu_apprx_tanh).then_inc(gelu, 1)

    def store(self, out_T):
        nc = self.nc
        with self.stage("store"):
            stored = self.sem("stored")
            with nc.Block() as block:
                @block.sync
                def _(sp):
                    sp.dma_start(self.t["out"].rearrange("(n p) t -> p n t", p=P), out_T[:]).then_inc(stored, 16)
                    sp.wait_ge(stored, 16)

    def moe(self):
        nc = self.nc
        h_rows, y_rows = self.h_rows, self.y_rows
        with ExitStack() as ctx:
            tile = lambda name, shape, dt=F32: ctx.enter_context(nc.sbuf_tensor(name, shape, dt))
            self.hT = tile("hT_m", [P, KD, S])
            self.norm(self.hT, self.v("norm2_g"), scale=self.mod[:, 32:40], shift=self.mod[:, 24:32])
            dest, w8 = tile("dest", [P, TT, TOPK], U32), tile("w8", [P, TT, TOPK])
            row_tokens = tile("row_tokens", [P, NBLK], U32)
            block_expert, used_pairs = tile("block_expert", [1, P], I32), tile("used_pairs", [1, 1], I32)
            self.rows_out(h_rows)
            self.route(dest, w8, row_tokens, block_expert, used_pairs)
            self.experts(h_rows, y_rows, row_tokens, block_expert, used_pairs)
            self.combine(y_rows, dest, w8)

    def rows_out(self, h_rows):
        nc = self.nc
        with self.stage("rows"):
            rows = self.sb("rows", [P, TT, D])
            ps = self.psum("ps", 8)
            turned, copied, stored = self.sems("turned copied stored")
            with nc.Block() as block:
                @block.tensor
                def _(pe):
                    for c in range(TT):
                        for k in range(KD):
                            mm = nc.tensor.transpose(ps[:, 2 * c + k // 4, (k % 4) * P:(k % 4 + 1) * P],
                                                     self.hT[:, k, c * P:(c + 1) * P], self.c("ident"))
                        mm.then_inc(turned, 1)

                @block.scalar
                def _(act):
                    for c in range(TT):
                        act.wait_ge(turned, c + 1)
                        nc.scalar.activation(rows[:, c, :].rearrange("p (b n) -> p b n", b=2), ps[:, 2 * c:2 * c + 2, :], ACT.Copy)\
                            .then_inc(copied, 1)

                @block.sync
                def _(sp):
                    for c in range(TT):
                        sp.wait_ge(copied, c + 1)
                        sp.dma_start(h_rows[c * P:(c + 1) * P, :], rows[:, c, :]).then_inc(stored, 16)
                    sp.wait_ge(stored, 16 * TT)

    def route(self, dest, w8, row_tokens, block_expert, used_pairs):
        nc = self.nc
        M = TT * E
        table = nc.dram_tensor("row_table", (BLK * NBLK, 1), U32).ap()
        expert_column = nc.dram_tensor("expert_column", (1, P), I32).ap()
        with self.stage("route"):
            wr = self.sb("wr", [P, KD, E])
            score, choice, rep, picked, w, place, row = (self.sb(x, [P, TT, E]) for x in
                                                         "score choice rep picked w place row".split())
            top = self.sb("top", [P, TT * GROUPS, 8])
            gs, rank = self.sb("gs", [P, TT, GROUPS]), self.sb("rank", [P, TT, GROUPS])
            above, tie = self.sb("above", [P, TT, 8, 8]), self.sb("tie", [P, TT, 8, 8])
            v8, d8 = self.sb("v8", [P, TT, 8]), self.sb("d8", [P, TT, 8])
            tot = self.sb("tot", [P, TT])
            cnt, nb, incl, first = (self.sb(x, [P, E]) for x in "cnt nb incl first".split())
            junk, eb = self.sb("junk", [P, E]), self.sb("eb", [P, 1])
            ebi = self.sb("ebi", [P, 1], I32)
            half, rest = self.sb("half", [P, 1]), self.sb("rest", [P, NBLK // 2])
            zero, tok = self.sb("zero", [P, NBLK], U32), self.sb("tok", [P, TT], U32)
            ps = self.psum("ps", 7)
            shared = SharedExpert(self, ps[:, 3:7, :])
            loaded, logits, scored, chain_s, zeroed, picked_s, places, ready, table_zero, scattered, experts_out, back = self.sems(
                "loaded logits scored chain zeroed picked places ready table_zero scattered experts_out back")
            cut = lambda x: x[:].rearrange("p c e -> p (c e)")
            with nc.Block() as block:
                @block.sync
                def _(sp):
                    sp.dma_start(wr[:], self.t["router_w"]).then_inc(loaded, 16)
                    shared.load(sp)
                    sp.wait_ge(zeroed, 1)
                    sp.dma_start(table.rearrange("(p b) a -> p (b a)", b=NBLK), zero[:]).then_inc(table_zero, 16)
                    sp.wait_ge(ready, 1)
                    sp.dma_start(expert_column.rearrange("a p -> p a"), ebi[:]).then_inc(experts_out, 16)
                    sp.wait_ge(experts_out, 16)
                    sp.dma_start(block_expert[:], expert_column).then_inc(back, 16)
                    sp.wait_ge(scattered, 16 * TT * TOPK)
                    sp.dma_start(row_tokens[:], table.rearrange("(p b) a -> p (b a)", b=NBLK)).then_inc(back, 16)
                    sp.wait_ge(back, 32)

                @block.tensor
                def _(pe):
                    pe.wait_ge(loaded, 16)
                    for c in range(TT):
                        for k in range(KD):
                            mm = nc.tensor.matmul(ps[:, 0, c * E:(c + 1) * E], self.hT[:, k, c * P:(c + 1) * P], wr[:, k, :],
                                                  start=k == 0, stop=k == KD - 1)
                    mm.then_inc(logits, 1)
                    shared.gate_up(pe, 0)
                    pe.wait_ge(picked_s, 1)
                    for c in range(TT):
                        for a in range(c):
                            nc.tensor.matmul(ps[:, 1, c * E:(c + 1) * E], self.ones[:], picked[:, a, :], start=a == 0, stop=False)
                        nc.tensor.matmul(ps[:, 1, c * E:(c + 1) * E], self.c("before"), picked[:, c, :], start=c == 0, stop=True)
                    for a in range(TT):
                        mm = nc.tensor.matmul(ps[:, 2, 0:E], self.ones[:], picked[:, a, :], start=a == 0, stop=a == TT - 1)
                    mm.then_inc(places, 1)
                    shared.gate_up(pe, 1)
                    shared.down(pe)

                @block.scalar
                def _(act):
                    act.wait_ge(logits, 1)
                    nc.scalar.activation(cut(score), ps[:, 0, 0:M], ACT.Sigmoid).then_inc(scored, 1)
                    shared.silu(act)

                @block.gpsimd
                def _(pool):
                    nc.gpsimd.memset(zero[:], 0).then_inc(zeroed, 1)
                    pool.wait_ge(table_zero, 16)
                    pool.wait_ge(ready, 1)
                    for c in range(TT):
                        for k in range(TOPK):
                            nc.gpsimd.indirect_dma_start(
                                out=table, out_offset=bass.IndirectOffsetOnAxis(ap=dest[:, c, k:k + 1], axis=0),
                                in_=tok[:, c:c + 1], in_offset=None).then_inc(scattered, 16)

                @block.vector
                def _(dve):
                    chain = Chain(dve, chain_s)
                    v = nc.vector
                    chain(v.tensor_copy(tok[:], self.c("tokens")))
                    dve.wait_ge(scored, 1)
                    bias = self.v("router_bias").unsqueeze(1).broadcast_to([P, TT, E])
                    chain(v.tensor_tensor(choice[:], score[:], bias, ALU.add))
                    for c in range(TT):
                        for g in range(GROUPS):
                            ins = v.max(top[:, c * GROUPS + g, :], choice[:, c, g * 8:(g + 1) * 8])
                    chain(ins)
                    chain(v.tensor_tensor(gs[:].rearrange("p c g -> p (c g)"), top[:, :, 0], top[:, :, 1], ALU.add))
                    other = gs[:].unsqueeze(2).broadcast_to([P, TT, GROUPS, GROUPS])
                    own = gs[:].unsqueeze(3).broadcast_to([P, TT, GROUPS, GROUPS])
                    lower = self.c("lower8").rearrange("p (a b) -> p a b", a=8).unsqueeze(1).broadcast_to([P, TT, 8, 8])
                    chain(v.tensor_tensor(above[:], other, own, ALU.is_gt))
                    chain(v.tensor_tensor(tie[:], other, own, ALU.is_equal))
                    chain(v.tensor_tensor(tie[:], tie[:], lower, ALU.mult))
                    chain(v.tensor_tensor(above[:], above[:], tie[:], ALU.add))
                    chain(v.tensor_reduce(rank[:], above[:], AX.X, ALU.add))
                    chain(v.tensor_scalar(rank[:], rank[:], float(TOPG), 1e30, ALU.is_lt, ALU.mult))
                    chain(v.tensor_scalar(rank[:], rank[:], -1e30, None, ALU.add))
                    cg = lambda x: x[:].rearrange("p c (g e) -> p (c g) e", g=GROUPS)
                    chain(v.tensor_tensor(cg(choice), cg(choice),
                                          rank[:].rearrange("p c g -> p (c g)").unsqueeze(2).broadcast_to([P, TT * GROUPS, 8]),
                                          ALU.add))
                    for c in range(TT):
                        ins = v.max(v8[:, c, :], choice[:, c, :])
                    chain(ins)
                    for c in range(TT):
                        ins = v.match_replace(rep[:, c, :], v8[:, c, :], choice[:, c, :], -3e38)
                    chain(ins)
                    chain(v.tensor_tensor(picked[:], rep[:], choice[:], ALU.not_equal))
                    dve.sem_inc(picked_s, 1)
                    chain(v.tensor_tensor(w[:], score[:], picked[:], ALU.mult))
                    chain(v.tensor_reduce(tot[:], w[:], AX.X, ALU.add))
                    chain(v.reciprocal(tot[:], tot[:]))
                    chain(v.scalar_tensor_tensor(out=w[:], in0=w[:], scalar=ROUTED_SCALE,
                                                 in1=tot[:].unsqueeze(2).broadcast_to([P, TT, E]), op0=ALU.mult, op1=ALU.mult))
                    shared.hidden(dve, 0)
                    dve.wait_ge(places, 1)
                    chain(v.tensor_copy(cnt[:], ps[:, 2, 0:E]))
                    chain(v.tensor_copy(cut(place), ps[:, 1, 0:M]))
                    chain(v.tensor_scalar(nb[:], cnt[:], 0.0, None, ALU.is_gt))
                    for j in range(1, S // BLK):
                        chain(v.scalar_tensor_tensor(out=nb[:], in0=cnt[:], scalar=float(j * BLK), in1=nb[:], op0=ALU.is_gt,
                                                     op1=ALU.add))
                    chain(v.tensor_tensor_scan(incl[:], self.ones[:, 0:E], nb[:], 0.0, ALU.mult, ALU.add))
                    chain(v.tensor_tensor(first[:], incl[:], nb[:], ALU.subtract))
                    chain(v.scalar_tensor_tensor(out=junk[:], in0=incl[:], scalar=self.c("iota"), in1=self.ones[:, 0:E],
                                                 op0=ALU.is_le, op1=ALU.mult, accum_out=eb[:]))
                    chain(v.tensor_scalar(ebi[:], eb[:], float(E - 1), None, ALU.min))
                    chain(v.tensor_scalar(half[:], incl[:, E - 1:E], 0.5, None, ALU.mult))
                    chain(v.scalar_tensor_tensor(out=rest[:], in0=self.c("pairs"), scalar=half[:], in1=self.ones[:, 0:NBLK // 2],
                                                 op0=ALU.is_lt, op1=ALU.mult, accum_out=eb[:]))
                    chain(v.tensor_copy(used_pairs[:], eb[0:1, :]))
                    chain(v.tensor_scalar(cut(row), cut(place), float(BLK), None, ALU.is_ge))
                    for j in range(2, S // BLK):
                        chain(v.scalar_tensor_tensor(out=cut(row), in0=cut(place), scalar=float(j * BLK), in1=cut(row),
                                                     op0=ALU.is_ge, op1=ALU.add))
                    chain(v.tensor_scalar(cut(row), cut(row), float(1 - BLK * NBLK), 1.0, ALU.mult, ALU.add))
                    chain(v.scalar_tensor_tensor(out=cut(row), in0=cut(place), scalar=float(NBLK), in1=cut(row),
                                                 op0=ALU.mult, op1=ALU.add))
                    chain(v.tensor_tensor(row[:], row[:], first[:].unsqueeze(1).broadcast_to([P, TT, E]), ALU.add))
                    chain(v.tensor_tensor(row[:], row[:], picked[:], ALU.mult))
                    for c in range(TT):
                        ins = v.max(d8[:, c, :], row[:, c, :])
                    chain(ins)
                    chain(v.tensor_scalar(dest[:], d8[:], -1.0, None, ALU.add))
                    dve.sem_inc(ready, 1)
                    shared.hidden(dve, 1)
                    for c in range(TT):
                        for n in (2 * c - 2, 2 * c - 1):
                            if c:
                                shared.into_x(dve, n)
                        for k in range(TOPK):
                            chain(v.scalar_tensor_tensor(out=junk[:], in0=row[:, c, :], scalar=d8[:, c, k:k + 1], in1=w[:, c, :],
                                                         op0=ALU.is_equal, op1=ALU.mult, accum_out=w8[:, c, k:k + 1]))
                    for n in (6, 7):
                        shared.into_x(dve, n)

    def experts(self, h_rows, y_rows, row_tokens, block_expert, used_pairs):
        nc, t = self.nc, self.t
        R = NBLK // 2
        with self.stage("experts"):
            wg, wd = self.sb("wg", [P, 2, KD, 2 * EH]), self.sb("wd", [P, 2, 2, D])
            xg, xt = self.sb("xg", [P, 2, D]), self.sb("xt", [P, 2, D])
            idx0, idx1 = self.sb("idx0", [P, 1], U32), self.sb("idx1", [P, 1], U32)
            idx = [idx0, idx1]
            sg, hx, ht, y = self.sb("sg", [P, 2, EH]), self.sb("hx", [P, 2, EH]), self.sb("ht", [P, 2, EH]), self.sb("y", [P, 2, D])
            psX, psG, psH, psY = self.psum("x", 2), self.psum("g", 2), self.psum("h", 1), self.psum("y", 2)
            slot = lambda name: [self.sem(f"{name}{s}") for s in range(2)]
            wg_in, wd_in, gathered, stored = slot("wg_loaded"), slot("wd_loaded"), slot("gathered"), slot("stored")
            idx_ready, idx_seen, x_turned, x_copied, gu_done, silu_done, hid_done, h_turned, h_copied, y_done, y_low, y_high, rows_stored = self.sems(
                "idx_ready idx_seen x_turned x_copied gu_done silu_done hid_done h_turned h_copied y_done y_low y_high rows_stored")
            out_rows = y_rows.rearrange("(p b) d -> p b d", b=NBLK)
            ident = self.c("ident")

            def used(eng):
                return eng.value_load(used_pairs[0:1, 0:1], min_val=S * TOPK // BLK // 2, max_val=R)

            def pipelined(eng, *steps):
                pairs = used(eng)
                for n in range(2):
                    for ahead, step in sorted(steps, key=lambda x: x[0] == 1):
                        if n < ahead:
                            step(0, n)
                with eng.Fori(0, R) as r:
                    with eng.If(r < pairs):
                        for s in range(2):
                            for ahead, step in steps:
                                if s + ahead < 2:
                                    step(r, s + ahead)
                                else:
                                    with eng.If(r + 1 < pairs):
                                        step(r + 1, (s + ahead) % 2)
                return pairs

            with nc.Block() as block:
                @block.sync
                def _(sp):
                    def load(r, s, again=True):
                        n = 2 * r + s
                        e = sp.value_load(block_expert[0:1, bass.ds(n, 1)], min_val=0, max_val=E - 1)
                        if again:
                            sp.wait_ge(gu_done, n - 1)
                        sp.dma_start(wg[:, s], t["exp_gu"][bass.ds(e, 1)].rearrange("a p k n -> (a p) k n"))\
                            .then_inc(wg_in[s], 16)
                        if again:
                            sp.wait_ge(y_done, n - 1)
                        sp.dma_start(wd[:, s], t["exp_dn"][bass.ds(e, 1)].rearrange("a p k n -> (a p) k n"))\
                            .then_inc(wd_in[s], 16)
                    load(0, 0, again=False)
                    load(0, 1, again=False)
                    pairs = used(sp)
                    with sp.Fori(1, R) as r:
                        with sp.If(r < pairs):
                            load(r, 0)
                            load(r, 1)

                @block.gpsimd
                def _(pool):
                    def gather(r, s, again=True):
                        n = 2 * r + s
                        if again:
                            pool.wait_ge(x_turned, n - 1)
                        nc.gpsimd.tensor_copy(idx[s][:], row_tokens[:, bass.ds(n, 1)]).then_inc(idx_ready, 1)
                        pool.wait_ge(idx_ready, n + 1)
                        pool.sem_inc(idx_seen, 1)
                        nc.gpsimd.indirect_dma_start(out=xg[:, s, :], out_offset=None, in_=h_rows,
                                                     in_offset=bass.IndirectOffsetOnAxis(ap=idx[s][:, 0:1], axis=0))\
                            .then_inc(gathered[s], 16)
                    gather(0, 0, again=False)
                    gather(0, 1, again=False)
                    pairs = used(pool)
                    with pool.Fori(1, R) as r:
                        with pool.If(r < pairs):
                            gather(r, 0)
                            gather(r, 1)

                @block.tensor
                def _(pe):
                    def turn_x(r, s):
                        n = 2 * r + s
                        pe.wait_ge(gathered[s], 16 * (r + 1))
                        pe.wait_ge(x_copied, n + 1)
                        for k in range(KD):
                            mm = nc.tensor.transpose(psX[:, k // 4, (k % 4) * P:(k % 4 + 1) * P], xg[:, s, k * P:(k + 1) * P], ident)
                        mm.then_inc(x_turned, 1)

                    def gate_up(r, s):
                        n = 2 * r + s
                        pe.wait_ge(x_copied, n + 2)
                        pe.wait_ge(wg_in[s], 16 * (r + 1))
                        for k in range(KD):
                            mm = nc.tensor.matmul(psG[:, s, :], xt[:, s, k * P:(k + 1) * P], wg[:, s, k, :], start=k == 0,
                                                  stop=k == KD - 1)
                        mm.then_inc(gu_done, 1)

                    def turn_h(r, s):
                        pe.wait_ge(hid_done, 2 * r + s + 1)
                        for k in range(2):
                            mm = nc.tensor.transpose(psH[:, 0, k * P:(k + 1) * P], hx[:, s, k * P:(k + 1) * P], ident)
                        mm.then_inc(h_turned, 1)

                    def down(r, s):
                        n = 2 * r + s
                        pe.wait_ge(wd_in[s], 16 * (r + 1))
                        pe.wait_ge(h_copied, n + 1)
                        pe.wait_ge(y_low, n + 1)
                        pe.wait_ge(y_high, n + 1)
                        for half in range(2):
                            for k in range(2):
                                mm = nc.tensor.matmul(psY[:, half, :], ht[:, s, k * P:(k + 1) * P], wd[:, s, k, half * S:(half + 1) * S],
                                                      start=k == 0, stop=k == 1)
                        mm.then_inc(y_done, 1)
                    pipelined(pe, (1, gate_up), (0, turn_h), (2, turn_x), (0, down))

                @block.scalar
                def _(act):
                    act.sem_inc(x_copied, 1)
                    act.sem_inc(y_high, 1)
                    for s in range(2):
                        act.sem_inc(stored[s], 16)

                    def silu(r, s):
                        act.wait_ge(gu_done, 2 * r + s + 1)
                        nc.scalar.activation(sg[:, s, :], psG[:, s, 0:EH], ACT.Silu).then_inc(silu_done, 1)

                    def copy_x(r, s):
                        act.wait_ge(x_turned, 2 * r + s + 1)
                        nc.scalar.activation(xt[:, s, :].rearrange("p (b n) -> p b n", b=2), psX[:], ACT.Copy).then_inc(x_copied, 1)

                    def store_y(r, s):
                        n = 2 * r + s
                        act.wait_ge(y_done, n + 1)
                        act.wait_ge(stored[s], 16 * (r + 1))
                        nc.scalar.activation(y[:, s, S:D], psY[:, 1, :], ACT.Copy).then_inc(y_high, 1)
                        act.wait_ge(y_high, n + 2)
                        act.wait_ge(y_low, n + 2)
                        act.dma_start(out_rows[:, bass.ds(n, 1), :].rearrange("p a d -> p (a d)"), y[:, s, :]).then_inc(stored[s], 16)
                    pairs = pipelined(act, (1, silu), (2, copy_x), (0, store_y))
                    for s in range(2):
                        act.wait_ge(stored[s], 16 * pairs + 16)
                        act.sem_inc(rows_stored, 1)

                @block.vector
                def _(dve):
                    dve.sem_inc(y_low, 1)

                    def copy_h(r, s):
                        dve.wait_ge(h_turned, 2 * r + s + 1)
                        nc.vector.tensor_copy(ht[:, s, :], psH[:, 0, 0:EH]).then_inc(h_copied, 1)

                    def hidden(r, s):
                        dve.wait_ge(silu_done, 2 * r + s + 1)
                        nc.vector.tensor_tensor(hx[:, s, :], sg[:, s, :], psG[:, s, EH:2 * EH], ALU.mult).then_inc(hid_done, 1)

                    def copy_y(r, s):
                        dve.wait_ge(y_done, 2 * r + s + 1)
                        dve.wait_ge(stored[s], 16 * (r + 1))
                        nc.vector.tensor_copy(y[:, s, 0:S], psY[:, 0, :]).then_inc(y_low, 1)
                    pipelined(dve, (0, copy_h), (1, hidden), (0, copy_y))

    def combine(self, y_rows, dest, w8):
        nc, xT, gate = self.nc, self.xT, self.mod[:, 40:48]
        SLOTS = 4
        with self.stage("combine"):
            g, acc = self.sb("g", [P, SLOTS, D]), self.sb("acc", [P, 2, D])
            ps = self.psum("ps", 4)
            gathered = [self.sem(f"gathered{s}") for s in range(SLOTS)]
            summed, turned, added = self.sems("summed turned added")
            with nc.Block() as block:
                @block.gpsimd
                def _(pool):
                    for i in range(TT * TOPK):
                        if i >= SLOTS:
                            pool.wait_ge(summed, i - SLOTS + 1)
                        nc.gpsimd.indirect_dma_start(
                            out=g[:, i % SLOTS, :], out_offset=None, in_=y_rows,
                            in_offset=bass.IndirectOffsetOnAxis(ap=dest[:, i // TOPK, i % TOPK:i % TOPK + 1], axis=0))\
                            .then_inc(gathered[i % SLOTS], 16)

                @block.vector
                def _(dve):
                    def into_x(c):
                        dve.wait_ge(turned, c + 1)
                        for n in range(KD):
                            o = xT[:, n, c * P:(c + 1) * P]
                            nc.vector.scalar_tensor_tensor(out=o, in0=ps[:, 2 * (c % 2) + n // 4, (n % 4) * P:(n % 4 + 1) * P],
                                                           scalar=gate[:, n:n + 1], in1=o, op0=ALU.mult, op1=ALU.add)\
                                .then_inc(added, 1)
                    for c in range(TT):
                        a = acc[:, c % 2, :]
                        for k in range(TOPK):
                            i = c * TOPK + k
                            dve.wait_ge(gathered[i % SLOTS], 16 * (i // SLOTS + 1))
                            if k == 0:
                                nc.vector.tensor_scalar(a, g[:, i % SLOTS, :], w8[:, c, 0:1], None, ALU.mult).then_inc(summed, 1)
                            else:
                                dve.wait_ge(summed, i)
                                nc.vector.scalar_tensor_tensor(out=a, in0=g[:, i % SLOTS, :], scalar=w8[:, c, k:k + 1], in1=a,
                                                               op0=ALU.mult, op1=ALU.add).then_inc(summed, 1)
                        if c:
                            into_x(c - 1)
                    into_x(TT - 1)

                @block.tensor
                def _(pe):
                    for c in range(TT):
                        pe.wait_ge(summed, TOPK * (c + 1))
                        if c >= 2:
                            pe.wait_ge(added, KD * (c - 1))
                        for n in range(KD):
                            mm = nc.tensor.transpose(ps[:, 2 * (c % 2) + n // 4, (n % 4) * P:(n % 4 + 1) * P],
                                                     acc[:, c % 2, n * P:(n + 1) * P], self.c("ident"))
                        mm.then_inc(turned, 1)


def vec_cols(x):
    x = np.asarray(x)
    return np.ascontiguousarray(x.reshape(-1, P).T)


def pair_groups(w):
    k, n = w.shape
    return np.ascontiguousarray(w.reshape(k // P, P, n // 256, 256).transpose(2, 1, 0, 3))


def constants():
    f = np.float32
    a = np.zeros((P, NCON), f)

    def put(name, x):
        lo, hi = CON[name]
        a[:, lo:hi] = x
    p = np.arange(P)
    put("ident", np.eye(P))
    put("before", p[:, None] < p[None, :])
    rot = np.zeros((P, P))
    for m in range(P):
        if m % 64 < 32:
            rot[m + 32, m] = -1.0
        else:
            rot[m - 32, m] = 1.0
    put("rot", rot)
    inv = (f(10000.0) ** (-np.arange(32, dtype=f) / f(32))).astype(f)
    ang = np.arange(S, dtype=f)[None, :] * inv[p % 32][:, None]
    put("cos", np.cos(ang))
    put("sin", np.sin(ang))
    levels = np.zeros((P, 8, P))
    for i in range(7):
        m = 64 >> i
        s, t = p[:, None], p[None, :]
        levels[:, i] = (s // (2 * m) == t // (2 * m)) & (s % (2 * m) < m) & (t % (2 * m) >= m)
    levels[:, 7] = np.eye(P)
    put("levels", levels.reshape(P, -1))
    put("causal", np.where(p[None, :] <= p[:, None], 0.0, NEG))
    tok = np.arange(TT)[None, :, None] * P + p[:, None, None]
    seen = np.arange(N_CMP)[None, None, :] * CMP_STRIDE + CMP_BLOCK - 1 <= tok
    put("cmp_add", np.where(seen, 0.0, NEG).reshape(P, -1))
    put("cmp_keep", seen[:, 0])
    g = np.arange(8)
    put("lower8", np.broadcast_to((g[None, :] < g[:, None]).reshape(1, 64), (P, 64)))
    put("iota", p[:, None])
    put("tokens", tok[:, :, 0])
    put("pairs", np.arange(NBLK // 2)[None, :])
    return a


def alibi():
    slopes = (2.0 ** (-8.0 * np.arange(1, 9) / 8)).astype(np.float32)
    dist = np.arange(P)[:, None] + P - np.arange(2 * P)[None, :]
    out = np.empty((P, 8, 2 * P), np.float32)
    for i in range(8):
        h = (i % 2) * 4 + i // 2
        out[:, i] = np.where((dist >= 0) & (dist < P), -slopes[h] * dist.astype(np.float32), np.float32(NEG))
    return out


PAIRED = np.concatenate([np.arange(64) + 64 * (4 * g + j) for j in range(4) for g in range(2)])


def layout(i):
    i = {k: np.asarray(v) for k, v in i.items()}
    w = i["w_in"][0]
    at = np.cumsum([0, 512, 512, 512, 512, 512, 128, 128, 128, 128, 128, 128, 24])
    hq, hf, hi, hgt, nq, kc, vc, ks, vs, kw, vw, ng = (w[:, at[n]:at[n + 1]] for n in range(12))
    fm = np.concatenate([hq, hf, hgt, nq[:, PAIRED], kc, vc, ks, kw, hi, vs, vw], axis=1)
    a = {"xT": np.ascontiguousarray(i["x"][0].T), "w_ada": i["w_ada"][0], "w_in": pair_groups(fm),
         "w_gates": np.ascontiguousarray(ng.reshape(KD, P, 24).transpose(1, 0, 2))}
    wo = i["w_out"][0]
    a["w_out"] = pair_groups(np.concatenate([wo[:512], wo[512:][PAIRED]]))
    for x in "kv":
        w1 = i[f"cmp_w1_{x}"][0].reshape(2, 16, 64, 256)
        a[f"w1_{x}"] = np.ascontiguousarray(w1.transpose(0, 2, 1, 3).reshape(P, 16, 256))
        a[f"w2_{x}"] = np.ascontiguousarray(i[f"cmp_w2_{x}"][0].reshape(2, P, 64).transpose(1, 0, 2))
        a[f"pos_{x}"] = np.ascontiguousarray(i[f"cmp_pos_{x}"][0].reshape(2, 16, 64).transpose(0, 2, 1).reshape(P, 16))
    a["router_w"] = np.ascontiguousarray(i["router_w"][0].reshape(KD, P, E).transpose(1, 0, 2))
    a["exp_gu"] = np.ascontiguousarray(i["w_exp_gu"][0].reshape(E, KD, P, 2 * EH).transpose(0, 2, 1, 3))
    a["exp_dn"] = np.ascontiguousarray(i["w_exp_dn"][0].reshape(E, 2, P, D).transpose(0, 2, 1, 3))
    a["sh_gu"] = np.ascontiguousarray(i["w_sh_gu"][0].reshape(KD, P, 2 * EH).transpose(1, 0, 2))
    a["sh_dn"] = np.ascontiguousarray(i["w_sh_dn"][0].reshape(2, P, D).transpose(1, 0, 2))
    a["w_mod"] = i["w_mod_2"]
    for n in (1, 2):
        gu = i[f"w_ffn{n}_gu_2"].reshape(2, KD, P, 2, FT, P)
        a[f"ffn{n}_gu"] = np.ascontiguousarray(gu.transpose(0, 4, 2, 1, 3, 5).reshape(2, FT, P, KD, 2 * P))
        a[f"ffn{n}_dn"] = np.ascontiguousarray(i[f"w_ffn{n}_down_2"].reshape(2, FT, P, D))
    at = np.cumsum([0, 512, 128, 128, 256, 256, 256, 256, 256])
    a["w_in_2"] = np.stack([pair_groups(np.concatenate([x[:, :512][:, PAIRED], x[:, 512:]], axis=1)) for x in i["w_in_2"]])
    a["w_out_2"] = np.stack([pair_groups(np.concatenate([x[:512][PAIRED], x[512:]])) for x in i["w_out_2"]])
    for x in "ax":
        g = i[f"lru_gate_{x}_w_2"]
        b = np.zeros((2, P, 2, P), g.dtype)
        for h in range(4):
            r = slice(64 * (h % 2), 64 * (h % 2) + 64)
            b[:, r, h // 2, r] = g[:, h]
        a[f"gate_{x}"] = b
    vecs = {
        "c": i["c"][0], "b_ada": i["b_ada"][0], "norm1_g": i["norm1_g"][0], "lb0": i["hg_lb_logits"][0],
        "lb1": i["hg_lb_logits"][1], "hg_norm_g": i["hg_norm_g"][0], "b1_k": i["cmp_b1_k"][0], "b1_v": i["cmp_b1_v"][0],
        "norm2_g": i["norm2_g"][0], "final_g": i["final_g"], "c_2": i["c_2"][0], "b_mod0": i["b_mod_2"][0],
        "b_mod1": i["b_mod_2"][1], "g_norm": i["g_norm_2"], "conv_w": i["lru_conv_w_2"], "conv_b": i["lru_conv_b_2"],
        "gate_a_b": i["lru_gate_a_b_2"], "gate_x_b": i["lru_gate_x_b_2"], "lam": i["lru_lambda_2"],
        "sc_conv_w": i["sc_conv_w_2"], "g_final": i["g_final_2"],
    }
    cols = [vec_cols(vecs[name]) for name, _ in VEC_COLS[:-2]]
    order = [4 * (n % 2) + n // 2 for n in range(8)]
    for row in (i["router_bias"][0], i["attn_sinks_2"][:, order].reshape(-1)):
        cols.append(np.broadcast_to(row[None, :], (P, row.size)))
    a["vecs"] = np.ascontiguousarray(np.concatenate(cols, axis=1))
    a["consts"] = constants()
    a["alibi"] = alibi()
    return a


def build(nc, t):
    k = Kernel(nc, t)
    k.setup()
    first = 16
    k.modulation(t["w_ada"][:, 0:first * P], k.v("c"), k.v("b_ada", 0, first), first)
    k.first_mixer()
    k.moe()
    k.norm(k.xT, k.v("final_g"))
    for layer in range(2):
        k.mod = k.mods[1 - layer]
        a, b = 5 * Modulation.CHUNK, 5 * Modulation.CHUNK // P
        beside = (t["w_mod"][1][:, 0:a], k.v("c_2"), k.v("b_mod1", 0, b), k.mods[0][:, 0:b], 5) if layer == 0 else None
        k.feed_forward(layer, 0, t["ffn1_gu"][layer], t["ffn1_dn"][layer], beside)
        k.second_mixer(layer)
        beside = (t["w_mod"][1][:, a:], k.v("c_2"), k.v("b_mod1", b), k.mods[0][:, b:], 4) if layer == 0 else None
        k.feed_forward(layer, 2, t["ffn2_gu"][layer], t["ffn2_dn"][layer], beside)
    with nc.sbuf_tensor("out_T", [P, KD, S], F32) as out_T:
        k.norm(out_T, k.v("g_final"))
        k.store(out_T)


def kernel(**inputs):
    import concourse.bacc as bacc
    from concourse.bass_utils import run_bass_kernel_spmd

    nc = bacc.Bacc("TRN2", target_bir_lowering=False, num_devices=1)
    arrays = layout(inputs)
    t = {name: nc.dram_tensor("in_" + name, a.shape, mybir.dt.from_np(a.dtype), kind="ExternalInput").ap()
         for name, a in arrays.items()}
    t["out"] = nc.dram_tensor("out", (D, S), F32, kind="ExternalOutput").ap()
    build(nc, t)
    result = run_bass_kernel_spmd(nc, [{"in_" + name: a for name, a in arrays.items()}], core_ids=[0])
    return np.ascontiguousarray(result.results[0]["out"].T)[None]
```
